# Optimizing a Trainium2 kernel written in Bass

```python
import math
import jax
import jax.numpy as jnp
from jax import lax
import numpy as np

D_MODEL = 1024
BATCH = 1
SEQ = 512
DEPTH = 1

HEAD_DIM = 64
FOX_HEADS = 4
SWA_HEADS = 4
SWA_KV_HEADS = 2
SWA_WINDOW = 128
DIFF_HEADS = 4
DIFF_QK_DIM = 32
DIL_HEADS = 4
DIL_PATTERNS = ((128, 1), (512, 4), (2048, 16))
N_BRANCHES = 4
BRANCH_WIDTH = 4 * HEAD_DIM
QUERY_BLOCK = 128
BAND_BLOCK = 128
BAND_PAD = 128
T5_BUCKETS = 32
T5_MAX_DIST = 2048
T5_HEADS = SWA_HEADS + DIFF_HEADS + DIL_HEADS
N_EXPERTS = 64
TOP_K = 8
N_GROUPS = 8
TOPK_GROUPS = 4
EXPERT_DIM = 256
SHARED_DIM = 256
ROUTED_SCALE = 2.5
MOE_BLOCK = 128
ALPHA = (2 * DEPTH) ** 0.25
BETA = (8 * DEPTH) ** -0.25
LN_EPS = 1e-5
IN_SPLITS = (
    FOX_HEADS * HEAD_DIM, FOX_HEADS * HEAD_DIM, FOX_HEADS * HEAD_DIM, FOX_HEADS,
    SWA_HEADS * HEAD_DIM, SWA_KV_HEADS * HEAD_DIM, SWA_KV_HEADS * HEAD_DIM,
    DIFF_HEADS * 2 * DIFF_QK_DIM, DIFF_HEADS * 2 * DIFF_QK_DIM, DIFF_HEADS * HEAD_DIM,
    DIL_HEADS * HEAD_DIM, DIL_HEADS * HEAD_DIM, DIL_HEADS * HEAD_DIM,
    N_BRANCHES * D_MODEL,
)
D_IN = sum(IN_SPLITS)

kernel_name = 'hybrid_fox_swa_diff_dilated_moe_deepnorm'

def layer_norm(x, g, b):
    xf = x.astype(jnp.float32)
    mu = jnp.mean(xf, axis=-1, keepdims=True)
    var = jnp.mean(jnp.square(xf - mu), axis=-1, keepdims=True)
    y = (xf - mu) * lax.rsqrt(var + LN_EPS)
    return (y * g.astype(jnp.float32) + b.astype(jnp.float32)).astype(x.dtype)

def t5_bucket(dist):
    n = jnp.maximum(dist, 0)
    exact = T5_BUCKETS // 2
    nf = jnp.maximum(n, 1).astype(jnp.float32)
    large = exact + (jnp.log(nf / exact) / math.log(T5_MAX_DIST / exact) * (T5_BUCKETS - exact)).astype(jnp.int32)
    large = jnp.minimum(large, T5_BUCKETS - 1)
    return jnp.where(n < exact, n, large)

def forgetting_attention(q, k, v, log_f):
    bsz, seq, heads, dh = q.shape
    nb = seq // QUERY_BLOCK
    c = jnp.cumsum(log_f, axis=1)
    c_keys = c.transpose(0, 2, 1)
    kpos = jnp.arange(seq)
    scale = dh ** -0.5

    def block(args):
        qi, ci, i = args
        qpos = i * QUERY_BLOCK + jnp.arange(QUERY_BLOCK)
        s = jnp.einsum('bqhd,bkhd->bhqk', qi, k) * scale
        s = s + (ci.transpose(0, 2, 1)[:, :, :, None] - c_keys[:, :, None, :])
        s = jnp.where(kpos[None, :] <= qpos[:, None], s, -jnp.inf)
        return jnp.einsum('bhqk,bkhd->bqhd', jax.nn.softmax(s, axis=-1), v)

    qb = q.reshape(bsz, nb, QUERY_BLOCK, heads, dh).swapaxes(0, 1)
    cb = c.reshape(bsz, nb, QUERY_BLOCK, heads).swapaxes(0, 1)
    o = lax.map(block, (qb, cb, jnp.arange(nb)))
    return o.swapaxes(0, 1).reshape(bsz, seq, heads, dh)

def differential_attention(q1, q2, k1, k2, v, lam, table):
    bsz, seq, heads, dq = q1.shape
    nb = seq // QUERY_BLOCK
    kpos = jnp.arange(seq)
    scale = dq ** -0.5

    def block(args):
        q1i, q2i, i = args
        qpos = i * QUERY_BLOCK + jnp.arange(QUERY_BLOCK)
        dist = qpos[:, None] - kpos[None, :]
        bias = table[t5_bucket(dist)].transpose(2, 0, 1)
        valid = dist >= 0

        def probs(qi, ki):
            s = jnp.einsum('bqhd,bkhd->bhqk', qi, ki) * scale + bias
            return jax.nn.softmax(jnp.where(valid, s, -jnp.inf), axis=-1)

        p = probs(q1i, k1) - lam * probs(q2i, k2)
        return jnp.einsum('bhqk,bkhd->bqhd', p, v)

    def to_blocks(t):
        return t.reshape(bsz, nb, QUERY_BLOCK, heads, t.shape[-1]).swapaxes(0, 1)

    o = lax.map(block, (to_blocks(q1), to_blocks(q2), jnp.arange(nb)))
    return o.swapaxes(0, 1).reshape(bsz, seq, heads, v.shape[-1])

def banded_attention(q, k, v, max_dist, dilation, table, sinks=None):
    bp, seq_len, hq, dh = q.shape
    hkv = k.shape[2]
    rep = hq // hkv
    blk = math.gcd(seq_len, BAND_BLOCK)
    nb = seq_len // blk
    kw = blk + BAND_PAD
    qb = q.reshape(bp, nb, blk, hkv, rep, dh)
    pad = ((0, 0), (BAND_PAD, 0), (0, 0), (0, 0))
    idx = jnp.arange(nb)[:, None] * blk + jnp.arange(kw)[None, :]
    ks = jnp.pad(k, pad)[:, idx]
    vs = jnp.pad(v, pad)[:, idx]
    qpos = jnp.arange(nb)[:, None] * blk + jnp.arange(blk)[None, :]
    kpos = idx - BAND_PAD
    dist = qpos[:, :, None] - kpos[:, None, :]
    valid = (dist >= 0) & (dist <= max_dist) & (kpos[:, None, :] >= 0)
    bias = table[t5_bucket(dist * dilation)]
    bias = bias.reshape(nb, blk, kw, hkv, rep).transpose(0, 3, 4, 1, 2)
    s = jnp.einsum('bnqgrd,bnkgd->bngrqk', qb, ks) * (dh ** -0.5) + bias
    s = jnp.where(valid[:, None, None], s, -jnp.inf)
    m = jnp.max(s, axis=-1)
    if sinks is not None:
        sk = sinks.reshape(hkv, rep)[:, :, None]
        m = jnp.maximum(m, sk)
    p = jnp.exp(s - m[..., None])
    den = jnp.sum(p, axis=-1)
    if sinks is not None:
        den = den + jnp.exp(sk - m)
    o = jnp.einsum('bngrqk,bnkgd->bnqgrd', p, vs) / den.transpose(0, 1, 4, 2, 3)[..., None]
    lse = (m + jnp.log(den)).transpose(0, 1, 4, 2, 3).reshape(bp, seq_len, hq)
    return o.reshape(bp, seq_len, hq, dh), lse

def to_residues(t, dil):
    b, s = t.shape[0], t.shape[1]
    return t.reshape(b, s // dil, dil, *t.shape[2:]).swapaxes(1, 2).reshape(b * dil, s // dil, *t.shape[2:])

def from_residues(t, b, dil):
    s_sub = t.shape[1]
    return t.reshape(b, dil, s_sub, *t.shape[2:]).swapaxes(1, 2).reshape(b, s_sub * dil, *t.shape[2:])

def dilated_attention(q, k, v, table):
    bsz = q.shape[0]
    outs, lses = [], []
    for window, dil in DIL_PATTERNS:
        o, lse = banded_attention(to_residues(q, dil), to_residues(k, dil), to_residues(v, dil),
                                  window // dil, dil, table)
        outs.append(from_residues(o, bsz, dil))
        lses.append(from_residues(lse, bsz, dil))
    wts = jax.nn.softmax(jnp.stack(lses), axis=0)
    return jnp.einsum('pbsh,pbshd->bshd', wts, jnp.stack(outs))

def mixer_sublayer(x, t5_table, w_in, b_forget, sinks, lam_q1, lam_k1, lam_q2, lam_k2,
                   diff_norm_g, w_branch, w_out, lam_init):
    bsz, seq, _ = x.shape
    f32 = jnp.float32
    h = x @ w_in
    offs = [int(o) for o in np.cumsum(IN_SPLITS)[:-1]]
    (qa, ka, va, fa, qb, kb, vb, qc, kc, vc, qd, kd, vd, gates) = jnp.split(h, offs, axis=-1)

    def heads(t, n):
        return t.astype(f32).reshape(bsz, seq, n, -1)

    tab = t5_table.astype(f32)
    log_f = jax.nn.log_sigmoid(fa.astype(f32) + b_forget.astype(f32))
    ya = forgetting_attention(heads(qa, FOX_HEADS), heads(ka, FOX_HEADS), heads(va, FOX_HEADS), log_f)
    yb, _ = banded_attention(heads(qb, SWA_HEADS), heads(kb, SWA_KV_HEADS), heads(vb, SWA_KV_HEADS),
                             SWA_WINDOW - 1, 1, tab[:, :SWA_HEADS], sinks.astype(f32))
    qc = heads(qc, DIFF_HEADS).reshape(bsz, seq, DIFF_HEADS, 2, DIFF_QK_DIM)
    kc = heads(kc, DIFF_HEADS).reshape(bsz, seq, DIFF_HEADS, 2, DIFF_QK_DIM)
    lam = (jnp.exp(jnp.sum(lam_q1.astype(f32) * lam_k1.astype(f32)))
           - jnp.exp(jnp.sum(lam_q2.astype(f32) * lam_k2.astype(f32))) + lam_init)
    yc = differential_attention(qc[:, :, :, 0], qc[:, :, :, 1], kc[:, :, :, 0], kc[:, :, :, 1],
                                heads(vc, DIFF_HEADS), lam, tab[:, SWA_HEADS:SWA_HEADS + DIFF_HEADS])
    yc = yc * lax.rsqrt(jnp.mean(yc * yc, axis=-1, keepdims=True) + LN_EPS) * diff_norm_g.astype(f32) * (1.0 - lam_init)
    yd = dilated_attention(heads(qd, DIL_HEADS), heads(kd, DIL_HEADS), heads(vd, DIL_HEADS),
                           tab[:, SWA_HEADS + DIFF_HEADS:])
    gates = gates.reshape(bsz, seq, N_BRANCHES, D_MODEL)
    merged = jnp.zeros_like(x)
    for i, y in enumerate((ya, yb, yc, yd)):
        y = y.reshape(bsz, seq, BRANCH_WIDTH).astype(x.dtype)
        merged = merged + jax.nn.sigmoid(gates[:, :, i]) * (y @ w_branch[i])
    return merged @ w_out

def swiglu(x, w_gate, w_up, w_down):
    return (jax.nn.silu(x @ w_gate) * (x @ w_up)) @ w_down

def routed_experts(xf, idx, wts, w_gate_e, w_up_e, w_down_e):
    n_tok, d = xf.shape
    nk = n_tok * TOP_K
    nblk = -(-nk // MOE_BLOCK) + N_EXPERTS
    rows = nblk * MOE_BLOCK
    flat_e = idx.reshape(-1)
    flat_tok = jnp.arange(nk, dtype=jnp.int32) // TOP_K
    flat_w = wts.reshape(-1)
    order = jnp.argsort(flat_e)
    se = flat_e[order]
    counts = jnp.bincount(flat_e, length=N_EXPERTS)
    starts = jnp.cumsum(counts) - counts
    padded = (counts + MOE_BLOCK - 1) // MOE_BLOCK * MOE_BLOCK
    pends = jnp.cumsum(padded)
    pstarts = pends - padded
    dest = pstarts[se] + jnp.arange(nk) - starts[se]
    row_tok = jnp.full((rows,), n_tok, jnp.int32).at[dest].set(flat_tok[order])
    row_w = jnp.zeros((rows,), jnp.float32).at[dest].set(flat_w[order])
    blk_e = jnp.minimum(jnp.searchsorted(pends, jnp.arange(nblk) * MOE_BLOCK, side='right'), N_EXPERTS - 1)
    x_pad = jnp.concatenate([xf, jnp.zeros((1, d), xf.dtype)], axis=0)

    def step(acc, blk):
        tok, w, e = blk
        yb = swiglu(x_pad[tok], w_gate_e[e], w_up_e[e], w_down_e[e]).astype(jnp.float32) * w[:, None]
        return acc.at[tok].add(yb), None

    acc, _ = lax.scan(step, jnp.zeros((n_tok + 1, d), jnp.float32),
                      (row_tok.reshape(nblk, MOE_BLOCK), row_w.reshape(nblk, MOE_BLOCK), blk_e))
    return acc[:n_tok].astype(xf.dtype)

def moe_sublayer(x, w_router, router_bias, w_gate_e, w_up_e, w_down_e, w_gate_s, w_up_s, w_down_s):
    bsz, seq, d = x.shape
    n_tok = bsz * seq
    xf = x.reshape(n_tok, d)
    scores = jax.nn.sigmoid((xf @ w_router).astype(jnp.float32))
    choice = scores + router_bias.astype(jnp.float32)
    group_score = jnp.sum(lax.top_k(choice.reshape(n_tok, N_GROUPS, -1), 2)[0], axis=-1)
    _, gidx = lax.top_k(group_score, TOPK_GROUPS)
    gmask = jnp.sum(jax.nn.one_hot(gidx, N_GROUPS, dtype=jnp.float32), axis=1) > 0
    emask = jnp.repeat(gmask, N_EXPERTS // N_GROUPS, axis=1)
    _, idx = lax.top_k(jnp.where(emask, choice, -jnp.inf), TOP_K)
    sel = jnp.take_along_axis(scores, idx, axis=1)
    wts = sel / jnp.sum(sel, axis=-1, keepdims=True) * ROUTED_SCALE
    routed = routed_experts(xf, idx, wts, w_gate_e, w_up_e, w_down_e)
    shared = swiglu(xf, w_gate_s, w_up_s, w_down_s)
    return (shared + routed).reshape(bsz, seq, d)

def setup_inputs(seed: int = 0) -> dict:
    key = jax.random.key(seed)
    ks = jax.random.split(key, 24)

    def nrm(k, shape, scale):
        return jax.random.normal(k, shape, jnp.float32) * scale

    L, D, E, F, FS = DEPTH, D_MODEL, N_EXPERTS, EXPERT_DIM, SHARED_DIM
    return {
        'x': nrm(ks[0], (BATCH, SEQ, D), 1.0),
        't5_table': nrm(ks[1], (T5_BUCKETS, T5_HEADS), 0.5),
        'w_in': nrm(ks[2], (L, D, D_IN), D ** -0.5),
        'b_forget': 2.0 + nrm(ks[3], (L, FOX_HEADS), 0.1),
        'attn_sinks': nrm(ks[4], (L, SWA_HEADS), 0.5),
        'lam_q1': nrm(ks[5], (L, DIFF_QK_DIM), 0.1),
        'lam_k1': nrm(ks[6], (L, DIFF_QK_DIM), 0.1),
        'lam_q2': nrm(ks[7], (L, DIFF_QK_DIM), 0.1),
        'lam_k2': nrm(ks[8], (L, DIFF_QK_DIM), 0.1),
        'diff_norm_g': 1.0 + nrm(ks[9], (L, HEAD_DIM), 0.05),
        'w_branch': nrm(ks[10], (L, N_BRANCHES, BRANCH_WIDTH, D), BETA * BRANCH_WIDTH ** -0.5),
        'w_out': nrm(ks[11], (L, D, D), BETA * D ** -0.5),
        'ln1_g': 1.0 + nrm(ks[12], (L, D), 0.05),
        'ln1_b': nrm(ks[13], (L, D), 0.02),
        'w_router': nrm(ks[14], (L, D, E), D ** -0.5),
        'router_bias': nrm(ks[15], (L, E), 0.01),
        'w_gate_e': nrm(ks[16], (L, E, D, F), D ** -0.5),
        'w_up_e': nrm(ks[17], (L, E, D, F), D ** -0.5),
        'w_down_e': nrm(ks[18], (L, E, F, D), BETA * F ** -0.5),
        'w_gate_s': nrm(ks[19], (L, D, FS), D ** -0.5),
        'w_up_s': nrm(ks[20], (L, D, FS), D ** -0.5),
        'w_down_s': nrm(ks[21], (L, FS, D), BETA * FS ** -0.5),
        'ln2_g': 1.0 + nrm(ks[22], (L, D), 0.05),
        'ln2_b': nrm(ks[23], (L, D), 0.02),
    }

def reference(x, t5_table, w_in, b_forget, attn_sinks, lam_q1, lam_k1, lam_q2, lam_k2,
              diff_norm_g, w_branch, w_out, ln1_g, ln1_b, w_router, router_bias,
              w_gate_e, w_up_e, w_down_e, w_gate_s, w_up_s, w_down_s, ln2_g, ln2_b):
    for layer in range(DEPTH):
        lam_init = 0.8 - 0.6 * math.exp(-0.3 * layer)
        mix = mixer_sublayer(x, t5_table, w_in[layer], b_forget[layer], attn_sinks[layer],
                             lam_q1[layer], lam_k1[layer], lam_q2[layer], lam_k2[layer],
                             diff_norm_g[layer], w_branch[layer], w_out[layer], lam_init)
        x = layer_norm(ALPHA * x + mix, ln1_g[layer], ln1_b[layer])
        ffn = moe_sublayer(x, w_router[layer], router_bias[layer], w_gate_e[layer], w_up_e[layer],
                           w_down_e[layer], w_gate_s[layer], w_up_s[layer], w_down_s[layer])
        x = layer_norm(ALPHA * x + ffn, ln2_g[layer], ln2_b[layer])
    return x


_drawn_inputs = setup_inputs


def setup_inputs(seed=0):
    import zlib

    import numpy as np

    out = dict(_drawn_inputs(seed))
    spreads = {}
    factors = {'attn_sinks': 8.0, 'lam_k1': 3.562, 'lam_q2': 4.804, 'lam_k2': 8.0, 'ln2_b': 2.913}
    for name, (base, spread) in spreads.items():
        noise = np.random.default_rng([zlib.crc32(name.encode()), seed]).standard_normal(out[name].shape)
        drawn = base * np.exp(spread * noise) if base else spread * noise
        out[name] = jnp.asarray(drawn.astype(out[name].dtype))
    for name, factor in factors.items():
        out[name] = (out[name] * factor).astype(out[name].dtype)
    return out
```

```python
from contextlib import ExitStack

import numpy as np

import concourse.bass as bass
from concourse import mybir

F32 = mybir.dt.float32
U32 = mybir.dt.uint32
I32 = mybir.dt.int32
ALU = mybir.AluOpType
ACT = mybir.ActivationFunctionType
AX = mybir.AxisListType

P = 128
SEQ = 512
D = 1024
QT = SEQ // P
KT = D // P
HD = 64
WINDOW = 128
DILATIONS = ((128, 1), (512, 4), (2048, 16))
N_EXP = 64
TOP_K = 8
N_GROUPS = 8
TOPK_GROUPS = 4
GROUP = N_EXP // N_GROUPS
F = 256
FT = F // P
ROUTED_SCALE = 2.5
ALPHA = 2 ** 0.25
EPS = 1e-5
LAM_INIT = 0.2
BUCKETS = 32
MAX_DIST = 2048
MASKED = 1e30
UNUSED = 65536.0
NO_SLOT = 16384.0
BR_A, BR_B, BR_C, BR_D = range(4)

PROJ = ([("q", BR_A, 0), ("q", BR_A, 1), ("k", BR_A, 0), ("k", BR_A, 1), ("v", BR_A, 0), ("v", BR_A, 1)]
        + [("q", BR_B, 0), ("q", BR_B, 1), ("k", BR_B, 0), ("v", BR_B, 0)]
        + [(kind, br, j) for br in (BR_C, BR_D) for kind in "qkv" for j in range(2)])
V_AT = {(BR_A, 0): 0, (BR_A, 1): 1, (BR_B, 0): 2, (BR_C, 0): 3, (BR_C, 1): 4, (BR_D, 0): 5, (BR_D, 1): 6}
N_PROJ = len(PROJ)
N_MERGE = 4 * KT
N_CHUNKS = N_PROJ + N_MERGE + KT
RING = 8
SLOT = 10 * P

COLS = {("q", BR_A): 0, ("k", BR_A): 256, ("v", BR_A): 512, "f": 768,
        ("q", BR_B): 772, ("k", BR_B): 1028, ("v", BR_B): 1156,
        ("q", BR_C): 1284, ("k", BR_C): 1540, ("v", BR_C): 1796,
        ("q", BR_D): 2052, ("k", BR_D): 2308, ("v", BR_D): 2564, "gates": 2820}


def attention_steps():
    return ([(BR_A, h, 0, q) for h in range(4) for q in range(QT)]
            + [(BR_B, h, 0, q) for h in range(4) for q in range(QT)]
            + [(BR_C, h, c, q) for h in range(4) for c in range(2) for q in range(QT)]
            + [(BR_D, h, 0, q) for h in range(4) for q in range(QT)])


STEPS = attention_steps()


def keys_of(branch, qt):
    if branch == BR_B:
        return max(qt - 1, 0), min(qt, 1) + 1
    return 0, qt + 1


def order_of_work():
    proj, merges, steps = list(range(6, N_PROJ)), list(range(N_MERGE)), list(range(len(STEPS)))
    order = [("proj", c) for c in range(6)]

    def step(s):
        out = [("scores", s)]
        if s >= 1:
            out.append(("turn", s - 1))
        if s >= 2:
            out.append(("values", s - 2))
        if s >= 4 and STEPS[s - 4][0] != STEPS[s - 3][0]:
            out += [("turn_y", 2 * STEPS[s - 4][0] + j) for j in range(2)]
        return out

    def merge(m):
        return [("gate", m)], [("branch", m)]

    for s in range(16):
        order += [("proj", proj.pop(0))] + step(s)
    for s in range(16, 20):
        order += step(s)
    at = 20
    while at < len(STEPS):
        g, z = merge(merges.pop(0))
        n = 4 if STEPS[at][0] == BR_C else 2
        order += g
        for s in range(at, min(at + n // 2, len(STEPS))):
            order += step(s)
        order += z
        for s in range(at + n // 2, min(at + n, len(STEPS))):
            order += step(s)
        at += n
    last = len(STEPS)
    g, z = merge(merges.pop(0))
    order += g + [("turn", last - 1), ("values", last - 2)] + z
    g, z = merge(merges.pop(0))
    order += g + [("values", last - 1)] + z
    order += [("turn_y", 2 * BR_D + j) for j in range(2)]
    while merges:
        g, z = merge(merges.pop(0))
        order += g + z
    return order


def distance_constants():
    dist = 511 - np.arange(640)
    n = np.maximum(dist, 0)
    exact = BUCKETS // 2
    large = exact + (np.log(np.maximum(n, 1) / exact) / np.log(MAX_DIST / exact) * (BUCKETS - exact)).astype(np.int32)
    bucket = np.where(n < exact, n, np.minimum(large, BUCKETS - 1))
    onehot = -(np.arange(BUCKETS)[:, None] == bucket[None, :]).astype(np.float32)
    times = sum(((dist <= (w // d) * d) & (dist % d == 0)).astype(np.int64) for w, d in DILATIONS)
    causal = np.where(dist >= 0, 0.0, MASKED)
    window = np.where((dist >= 0) & (dist < WINDOW), 0.0, MASKED)
    dilated = np.where((dist >= 0) & (times > 0), -np.log(np.maximum(times, 1)), MASKED)
    rows = [window] * 4 + [causal] * 4 + [dilated] * 4 + [causal]
    mask = np.zeros((16, 640), np.float32)
    mask[:13] = np.stack(rows)
    return onehot, mask


def build(nc, a, out):
    order = order_of_work()
    turns = [x for x in order if x[0] in ("turn", "turn_y")]
    turn_at = {x: n for n, x in enumerate(turns)}
    n_steps = len(STEPS)
    last_step = {br: max(s for s, x in enumerate(STEPS) if x[0] == br) for br in range(4)}
    norm_step = last_step[BR_C] + 3
    merges_before_norm = sum(kind == "branch" for kind, _ in order[:order.index(("scores", norm_step))])
    at_proj = {n: n + 1 for n in range(N_PROJ)}

    ctx = ExitStack()
    with ctx:
        def sb(name, shape, dt=F32):
            return ctx.enter_context(nc.sbuf_tensor(name, shape, dt))

        def sem(name):
            return ctx.enter_context(nc.semaphore(name))

        PS = ctx.enter_context(nc.psum_tensor("PS", [P, 8, 512], F32))
        ident = sb("ident", [P, P])
        before = sb("before", [P, P])
        ones = sb("ones", [P, P])
        half_neg = sb("half_neg", [P, 16])
        slot_no = sb("slot_no", [P, P])
        tok_row = sb("tok_row", [P, QT])
        ring = sb("ring", [P, RING, SLOT])
        xT = sb("xT", [P, KT, SEQ])
        mT = sb("mT", [P, KT, SEQ])
        region = sb("region", [P, 29400])

        def carve(start, shape):
            n = int(np.prod(shape))
            v = region[:, start:start + n]
            if len(shape) == 2:
                v = v.rearrange("p (a b) -> p a b", a=shape[0])
            elif len(shape) == 3:
                v = v.rearrange("p (a b c) -> p a b c", a=shape[0], b=shape[1])
            return v, start + n

        qA, o = carve(0, (4, SEQ))
        kA, o = carve(o, (4, SEQ))
        qB, o = carve(o, (2, SEQ))
        kB, o = carve(o, (1, SEQ))
        qC, o = carve(o, (2, SEQ))
        kC, o = carve(o, (2, SEQ))
        qD, o = carve(o, (2, SEQ))
        kD, o = carve(o, (2, SEQ))
        V, o = carve(o, (QT, 7, P))
        strips, o = carve(o, (13, SEQ))
        probs, o = carve(o, (3, SEQ + 2))
        probsT, o = carve(o, (3, SEQ))
        Y, o = carve(o, (2 * QT, F))
        yT, o = carve(o, (4, SEQ))
        gate, o = carve(o, (2, SEQ))
        gated, o = carve(o, (2, SEQ))
        assert o <= 29400, o
        w_gu, o = carve(0, (2, KT, 2 * F))
        w_dn, o = carve(o, (2, FT, D))
        x_nat, o = carve(o, (QT, D))
        x1, o = carve(o, (QT, D))
        ln2, o = carve(o, (2, D))
        onehot, o = carve(o, (2, QT, P))
        w_r, o = carve(o, (KT, N_EXP))
        info, o = carve(o, (QT, N_EXP + 2, 3))
        pos, o = carve(o, (QT, N_EXP + 2))
        top2, o = carve(o, (N_GROUPS, 8))
        rt64, o = carve(o, (4, N_EXP))
        score, o = carve(o, (N_EXP,))
        choice, o = carve(o, (N_EXP,))
        assert o <= 29400, o
        rows8, o = carve(0, (2, TOP_K, D))
        flat = ring[:, :, :].rearrange("p a b -> p (a b)")
        x_slots = flat[:, 0:2 * D].rearrange("p (a b) -> p a b", a=2)
        x_slotsT = flat[:, 2 * D:4 * D].rearrange("p (a k t) -> p a k t", a=2, k=KT)
        y_slots = flat[:, 4 * D:6 * D].rearrange("p (a b) -> p a b", a=2)
        h_slots = flat[:, 6 * D:6 * D + 512].rearrange("p (a b) -> p a b", a=2)
        hT = flat[:, 6 * D + 512:7 * D].rearrange("p (a k t) -> p a k t", a=2, k=FT)
        sig = flat[:, 7 * D:7 * D + 512].rearrange("p (a b) -> p a b", a=2)
        silu = flat[:, 7 * D + 512:8 * D].rearrange("p (a b) -> p a b", a=2)

        w_f = sb("w_f", [P, KT, 4])
        b_f = sb("b_f", [4, 1])
        fg = yT[0:4, :, :]
        neg_oh = gate.rearrange("p a b -> p (a b)")[0:BUCKETS, 0:640]
        dist_mask = gated.rearrange("p a b -> p (a b)")[0:16, 0:640]
        table = sb("table", [BUCKETS, 16])
        dist_bias = Y.rearrange("p a b -> p (a b)")[0:16, 0:640]
        neg_sink = sb("neg_sink", [P, 4])
        lam_in = sb("lam_in", [P, 4, 32])
        lam_mul = sb("lam_mul", [P, 2, 32])
        lam_s = sb("lam_s", [P, 8])
        norm_g = sb("norm_g", [P, HD])
        nmax = sb("nmax", [P, n_steps])
        den = sb("den", [P, n_steps])
        rden = sb("rden", [P, n_steps])
        yc_sq = sb("yc_sq", [P, F])
        yc_ss = sb("yc_ss", [P, 16])
        ln1 = sb("ln1", [P, 2, D])
        stats = sb("stats", [P, 2, 6])
        mv = sb("mv", [P, 8])
        r_bias = sb("r_bias", [P, N_EXP])
        gscore = sb("gscore", [P, 8])
        rt8 = sb("rt8", [P, 8, 8])
        sel = sb("sel", [P, QT, N_EXP])
        rank = sb("rank", [P, N_EXP])
        wsum = sb("wsum", [P, 8])
        rows_u = sb("rows_u", [P, 4, 2], U32)
        w_slot = sb("w_slot", [P, 4, 1])
        most = sb("most", [P, 2])
        most_i = sb("most_i", [1, 2], I32)
        ov_slot = sb("ov_slot", [P, P])

        bias_d = nc.dram_tensor("bias_d", (13, P, 640), F32).ap()
        x1_d = nc.dram_tensor("x1_d", (SEQ, D), F32).ap()
        rows_d = nc.dram_tensor("rows_d", (SEQ * TOP_K, D), F32).ap()

        S_BANK, T_BANK, O_BANK, C_BANK = 0, 2, 4, 6
        G_BANK, X_BANK, H_BANK, I_BANK, Y_BANK = 0, 2, 4, 5, 6

        ring_in = [sem(f"ring_in{j}") for j in range(RING)]
        small_in = sem("small_in")
        xT_in = sem("xT_in")
        bias_io = sem("bias_io")
        strips_in = sem("strips_in")
        aug_in = sem("aug_in")
        consts_made = sem("consts_made")
        dve_chain = sem("dve_chain")
        act_chain = sem("act_chain")
        pool_chain = sem("pool_chain")
        bias_mm = sem("bias_mm")
        bias_made = sem("bias_made")
        forget_exp = sem("forget_exp")
        forget_made = sem("forget_made")
        lam_dots = sem("lam_dots")
        lam_exp = sem("lam_exp")
        chunk_done = sem("chunk_done")
        proj_done = sem("proj_done")
        proj_out = sem("proj_out")
        scores_done = sem("scores_done")
        biased = sem("biased")
        probs_made = sem("probs_made")
        turned = sem("turned")
        turned_out = sem("turned_out")
        values_done = sem("values_done")
        y_made = sem("y_made")
        yc_stat = sem("yc_stat")
        yc_rms = sem("yc_rms")
        y_ready = sem("y_ready")
        gate_done = sem("gate_done")
        gate_exp = sem("gate_exp")
        branch_done = sem("branch_done")
        gated_made = sem("gated_made")
        merged = sem("merged")
        x_in = sem("x_in")
        late_in = sem("late_in")
        mix_done = sem("mix_done")
        var_made = sem("var_made")
        rstd_made = sem("rstd_made")
        x1_made = sem("x1_made")
        x1_stored = sem("x1_stored")
        x1_turned = sem("x1_turned")
        x1T_made = sem("x1T_made")
        router_done = sem("router_done")
        router_exp = sem("router_exp")
        sel_made = sem("sel_made")
        scores_used = sem("scores_used")
        pos_done = sem("pos_done")
        info_made = sem("info_made")
        most_made = sem("most_made")
        sh_in = sem("sh_in")
        gu_in = [sem(f"gu_in{b}") for b in range(2)]
        dn_in = [sem(f"dn_in{b}") for b in range(2)]
        slots_in = [sem(f"slots_in{b}") for b in range(2)]
        slots_clear = sem("slots_clear")
        gathers_begun = sem("gathers_begun")
        scatters_begun = sem("scatters_begun")
        gu_a = sem("gu_a")
        gu_b = sem("gu_b")
        sig_a = sem("sig_a")
        sig_b = sem("sig_b")
        silu_made = sem("silu_made")
        h_a = sem("h_a")
        h_b = sem("h_b")
        h_turned_a = sem("h_turned_a")
        h_turned_b = sem("h_turned_b")
        hT_a = sem("hT_a")
        hT_b = sem("hT_b")
        y_done = sem("y_done")
        y_out0 = sem("y_out0")
        y_out1 = sem("y_out1")
        onehot_made = sem("onehot_made")
        slots_done = sem("slots_done")
        rows_made = sem("rows_made")
        slots_turned = sem("slots_turned")
        slotsT_made = sem("slotsT_made")
        rows_out = [sem(f"rows_out{b}") for b in range(2)]
        ov = {n: sem(f"ov_{n}") for n in ("w", "oh", "idx", "rows", "in", "tr", "xT", "gu", "sig", "silu", "h",
                                          "hturn", "hT", "y", "yout", "out", "turns")}
        rows8_in = [sem(f"rows8_in{b}") for b in range(2)]
        sums = sem("sums")
        out_made = sem("out_made")
        out_stored = sem("out_stored")

        def mT_nat(t):
            return mT[:, :, :].rearrange("p a b -> p (a b)")[:, t * D:(t + 1) * D]

        block = ctx.enter_context(nc.Block())

        SMALL = 9
        N_LATE = 5

        @block.sync
        def _(sp):
            sp.dma_start(w_f[:], a["w_f"]).then_inc(small_in, 16)
            sp.dma_start(b_f[:], a["b_forget"].rearrange("o h -> h o")).then_inc(small_in, 16)
            sp.dma_start(neg_oh, a["neg_onehot"]).then_inc(small_in, 16)
            sp.dma_start(dist_mask, a["dist_mask"]).then_inc(small_in, 16)
            sp.wait_ge(consts_made, 1)
            sp.dma_start(table[:, 0:12], a["t5_table"]).then_inc(small_in, 16)
            sp.dma_start(neg_sink[:], bass.AP(a["attn_sinks"].tensor, 0, [[0, P], [1, 4]])).then_inc(small_in, 16)
            sp.dma_start(lam_in[:, :, :], bass.AP(a["lam"].tensor, 0, [[0, P], [32, 4], [1, 32]]))\
                .then_inc(small_in, 16)
            sp.dma_start(norm_g[:], bass.AP(a["diff_norm_g"].tensor, 0, [[0, P], [1, HD]])).then_inc(small_in, 16)
            sp.dma_start(xT[:, :, :], a["xT"].rearrange("(c p) n -> p c n", p=P)).then_inc(xT_in, 16)
            sp.dma_start(ln1[:, 0, :], bass.AP(a["ln1_g"].tensor, 0, [[0, P], [1, D]])).then_inc(small_in, 16)

            def chunk(j):
                if j >= RING:
                    sp.wait_ge(chunk_done, j - RING + 1)
                if j < N_PROJ:
                    src, n = a["w_proj"][j], KT * P
                elif j < N_PROJ + N_MERGE:
                    src, n = a["w_merge"][j - N_PROJ], 10 * P
                else:
                    k = j - N_PROJ - N_MERGE
                    src, n = a["w_out"][0, k * P:(k + 1) * P, :], D
                sp.dma_start(ring[:, j % RING, 0:n], src).then_inc(ring_in[j % RING], 16)

            for j in range(4):
                chunk(j)
            sp.wait_ge(bias_made, 1)
            sp.dma_start(bias_d, dist_bias[0:13, :].unsqueeze(1).broadcast_to([13, P, 640])).then_inc(bias_io, 16)
            sp.wait_ge(bias_io, 16)
            sp.dma_start(strips[:, :, :], bass.AP(bias_d.tensor, P - 1, [[639, P], [P * 640, 13], [1, SEQ]]))\
                .then_inc(strips_in, 16)
            for j in range(4, 8):
                chunk(j)
            sp.wait_ge(forget_made, 1)
            sp.dma_start(kA[64:65, :, :], fg[:, 2, :]).then_inc(aug_in, 16)
            sp.dma_start(qA[65:66, :, :], fg[:, 3, :]).then_inc(aug_in, 16)
            for j in range(8, N_CHUNKS):
                chunk(j)

            sp.wait_ge(branch_done, N_MERGE)
            sp.wait_ge(merged, N_MERGE)
            for t in range(QT):
                sp.dma_start(x_nat[:, t, :], a["x"][0, t * P:(t + 1) * P, :]).then_inc(x_in, 16)
            sp.dma_start(ln1[:, 1, :], bass.AP(a["ln1_b"].tensor, 0, [[0, P], [1, D]])).then_inc(late_in, 16)
            sp.dma_start(w_r[:], a["w_router"][0].rearrange("(p c) e -> p c e", c=KT)).then_inc(late_in, 16)
            sp.dma_start(r_bias[:], bass.AP(a["router_bias"].tensor, 0, [[0, P], [1, N_EXP]])).then_inc(late_in, 16)
            sp.dma_start(ln2[:, 0, :], bass.AP(a["ln2_g"].tensor, 0, [[0, P], [1, D]])).then_inc(late_in, 16)
            sp.dma_start(ln2[:, 1, :], bass.AP(a["ln2_b"].tensor, 0, [[0, P], [1, D]])).then_inc(late_in, 16)
            sp.dma_start(w_gu[:, 1, :, :], a["w_gu_s"].rearrange("p (c n) -> p c n", c=KT)).then_inc(sh_in, 16)
            sp.dma_start(w_dn[:, 1, :, :], a["w_down_s"][0].rearrange("(t p) n -> p t n", p=P)).then_inc(sh_in, 16)
            for t in range(QT):
                sp.wait_ge(x1_made, t + 1)
                sp.dma_start(x1_d[t * P:(t + 1) * P, :], x1[:, t, :]).then_inc(x1_stored, 16)

            with sp.Fori(0, N_EXP // 4) as i:
                for b in range(4):
                    e = i * 4 + b
                    sp.wait_ge(gu_b, i * 4 + b + QT - 1)
                    sp.dma_start(w_gu[:, b % 2, :, :],
                                 a["w_gu"][bass.ds(e, 1)].rearrange("o p (c n) -> (o p) c n", c=KT))\
                        .then_inc(gu_in[b % 2], 16)
                    sp.wait_ge(y_done, i * 4 + b + QT - 1)
                    sp.dma_start(w_dn[:, b % 2, :, :],
                                 a["w_down_e"][0, bass.ds(e, 1)].rearrange("o (t p) n -> (o p) t n", p=P))\
                        .then_inc(dn_in[b % 2], 16)

            sp.wait_ge(most_made, 1)
            n = sp.value_load(most_i[0:1, 0:1], min_val=0, max_val=SEQ)
            with sp.If(n > P):
                sp.wait_ge(y_done, QT + N_EXP)
                with sp.Fori(1, SEQ // P) as c:
                    with sp.Fori(0, N_EXP) as e:
                        j = (c - 1) * N_EXP + e
                        sp.wait_ge(ov["y"], j + 1)
                        sp.dma_start(w_gu[:, 0, :, :],
                                     a["w_gu"][bass.ds(e, 1)].rearrange("o p (c n) -> (o p) c n", c=KT))\
                            .then_inc(ov["w"], 16)
                        sp.dma_start(w_dn[:, 0, :, :],
                                     a["w_down_e"][0, bass.ds(e, 1)].rearrange("o (t p) n -> (o p) t n", p=P))\
                            .then_inc(ov["w"], 16)
                sp.wait_ge(ov["out"], 16 * (SEQ // P - 1) * N_EXP)

            sp.wait_ge(y_done, QT + N_EXP)
            for b in range(2):
                sp.wait_ge(rows_out[b], 16 * (N_EXP // 2 + 1))
            for t in range(QT):
                if t >= 2:
                    sp.wait_ge(sums, t - 1)
                sp.dma_start(rows8[:, t % 2, :, :],
                             rows_d[t * P * TOP_K:(t + 1) * P * TOP_K, :].rearrange("(p r) d -> p r d", r=TOP_K))\
                    .then_inc(rows8_in[t % 2], 16)
            for t in range(QT):
                sp.wait_ge(out_made, t + 1)
                sp.dma_start(out[0, t * P:(t + 1) * P, :], mT_nat(t)).then_inc(out_stored, 16)
            sp.wait_ge(out_stored, 16 * QT)
            sp.wait_ge(x1_stored, 16 * QT)

        @block.tensor
        def _(pe):
            def qk_of(s):
                br, h, c, qt = STEPS[s]
                k0, nk = keys_of(br, qt)
                q, k = {BR_A: (qA, kA), BR_B: (qB, kB), BR_C: (qC, kC), BR_D: (qD, kD)}[br]
                if br == BR_A:
                    base, n, jq, jk = 0, 66, h, h
                elif br == BR_B:
                    base, n, jq, jk = 64 * (h // 2), 64, h % 2, 0
                elif br == BR_C:
                    base, n, jq, jk = 64 * (h % 2) + 32 * c, 32, h // 2, h // 2
                else:
                    base, n, jq, jk = 64 * (h % 2), 64, h // 2, h // 2
                return (q[base:base + n, jq, qt * P:(qt + 1) * P], k[base:base + n, jk, k0 * P:(k0 + nk) * P])

            def v_of(s, kt):
                br, h, _, _ = STEPS[s]
                if br == BR_B:
                    return V[:, kt, V_AT[br, 0], HD * (h // 2):HD * (h // 2) + HD]
                return V[:, kt, V_AT[br, h // 2], HD * (h % 2):HD * (h % 2) + HD]

            pe.wait_ge(consts_made, 2)
            pe.wait_ge(small_in, 16 * SMALL)
            nc.tensor.matmul(PS[0:16, S_BANK, 0:512], table[:, :], neg_oh[:, 0:512], start=True, stop=True)
            nc.tensor.matmul(PS[0:16, S_BANK + 1, 0:128], table[:, :], neg_oh[:, 512:640], start=True, stop=True)\
                .then_inc(bias_mm, 1)
            pe.wait_ge(xT_in, 16)
            for c in range(KT):
                mm = nc.tensor.matmul(PS[0:4, C_BANK, :], w_f[:, c, :], xT[:, c, :], start=(c == 0), stop=(c == KT - 1))
            mm.then_inc(proj_done, 1)

            for kind, n in order:
                if kind == "proj":
                    u = at_proj[n]
                    w = ring[:, n % RING, :].rearrange("p (c n) -> p c n", c=10)
                    bank = C_BANK + u % 2
                    pe.wait_ge(ring_in[n % RING], 16 * (n // RING + 1))
                    if u >= 2:
                        pe.wait_ge(proj_out, u - 1)
                    if PROJ[n][0] == "v":
                        for t in range(QT):
                            for c in range(KT):
                                mm = nc.tensor.matmul(PS[:, bank, t * P:(t + 1) * P], xT[:, c, t * P:(t + 1) * P],
                                                      w[:, c, :], start=(c == 0), stop=(c == KT - 1))
                    else:
                        for c in range(KT):
                            mm = nc.tensor.matmul(PS[:, bank, :], w[:, c, :], xT[:, c, :], start=(c == 0),
                                                  stop=(c == KT - 1))
                    mm.then_inc(proj_done, 1)
                    pe.wait_ge(proj_done, u + 1)
                    pe.sem_inc(chunk_done, 1)
                elif kind == "scores":
                    br, h, _, qt = STEPS[n]
                    if qt == 0:
                        need = max(at_proj[m] for m, x in enumerate(PROJ) if x[1] == br and x[0] in "qk")
                        pe.wait_ge(proj_out, need + 1)
                        if br == BR_A:
                            pe.wait_ge(aug_in, 32)
                    if n < 2:
                        pe.wait_ge(bias_made, 1)
                    else:
                        pe.wait_ge(biased, n - 1)
                    q, k = qk_of(n)
                    nk = keys_of(br, qt)[1]
                    nc.tensor.matmul(PS[:, S_BANK + n % 2, 0:nk * P], q, k, start=True, stop=True)\
                        .then_inc(scores_done, 1)
                elif kind == "turn":
                    u = turn_at[kind, n]
                    br, _, _, qt = STEPS[n]
                    pe.wait_ge(probs_made, n + 1)
                    if u >= 2:
                        pe.wait_ge(turned_out, u - 1)
                    for j in range(keys_of(br, qt)[1]):
                        mm = nc.tensor.transpose(PS[:, T_BANK + u % 2, j * P:(j + 1) * P],
                                                 probs[:, n % 3, j * P:(j + 1) * P], ident[:, :])
                    mm.then_inc(turned, 1)
                elif kind == "values":
                    br, _, _, qt = STEPS[n]
                    k0, nk = keys_of(br, qt)
                    pe.wait_ge(turned_out, turn_at["turn", n] + 1)
                    need = max(at_proj[m] for m, x in enumerate(PROJ) if x[1] == br and x[0] == "v")
                    pe.wait_ge(proj_out, need + 1)
                    if n >= 2:
                        pe.wait_ge(y_made, n - 1)
                    for j in range(nk):
                        mm = nc.tensor.matmul(PS[:, O_BANK + n % 2, 0:HD], probsT[:, n % 3, j * P:(j + 1) * P],
                                              v_of(n, k0 + j), start=(j == 0), stop=(j == nk - 1))
                    mm.then_inc(values_done, 1)
                elif kind == "turn_y":
                    u = turn_at[kind, n]
                    br, j = n // 2, n % 2
                    pe.wait_ge(y_ready, br + 1)
                    pe.wait_ge(turned_out, u - 1)
                    for t in range(QT):
                        mm = nc.tensor.transpose(PS[:, T_BANK + u % 2, t * P:(t + 1) * P],
                                                 Y[:, (br % 2) * QT + t, j * P:(j + 1) * P], ident[:, :])
                    mm.then_inc(turned, 1)
                elif kind == "gate":
                    j = N_PROJ + n
                    w = ring[:, j % RING, :].rearrange("p (c n) -> p c n", c=10)
                    pe.wait_ge(ring_in[j % RING], 16 * (j // RING + 1))
                    if n == 0:
                        pe.wait_ge(proj_out, N_PROJ + 1)
                    else:
                        pe.wait_ge(gate_exp, n)
                    for c in range(KT):
                        mm = nc.tensor.matmul(PS[:, C_BANK, :], w[:, c, :], xT[:, c, :], start=(c == 0),
                                              stop=(c == KT - 1))
                    mm.then_inc(gate_done, 1)
                elif kind == "branch":
                    j, br = N_PROJ + n, n // KT
                    w = ring[:, j % RING, :].rearrange("p (c n) -> p c n", c=10)
                    pe.wait_ge(turned_out, turn_at["turn_y", 2 * br + 1] + 1)
                    if n >= 1:
                        pe.wait_ge(gated_made, n)
                    for c in range(2):
                        mm = nc.tensor.matmul(PS[:, C_BANK + 1, :], w[:, KT + c, :], yT[:, (br % 2) * 2 + c, :],
                                              start=(c == 0), stop=(c == 1))
                    mm.then_inc(branch_done, 1)
                    pe.wait_ge(branch_done, n + 1)
                    pe.sem_inc(chunk_done, 1)

            def mix(t):
                if t == 0:
                    for k in range(KT):
                        j = N_PROJ + N_MERGE + k
                        pe.wait_ge(ring_in[j % RING], 16 * (j // RING + 1))
                    pe.wait_ge(merged, N_MERGE)
                    pe.wait_ge(biased, n_steps)
                    pe.wait_ge(y_made, n_steps)
                if t >= 2:
                    pe.wait_ge(var_made, t - 1)
                bank = S_BANK if t % 2 == 0 else O_BANK
                for half in range(2):
                    for k in range(KT):
                        j = N_PROJ + N_MERGE + k
                        mm = nc.tensor.matmul(PS[:, bank + half, :], mT[:, k, t * P:(t + 1) * P],
                                              ring[:, j % RING, half * 512:half * 512 + 512],
                                              start=(k == 0), stop=(k == KT - 1))
                mm.then_inc(mix_done, 1)

            def turn_x1(t):
                pe.wait_ge(x1_made, t + 1)
                if t == 0:
                    pe.wait_ge(turned_out, len(turns))
                else:
                    pe.wait_ge(x1T_made, t)
                xs = x1[:, t, :].rearrange("p (q c) -> p c q", c=KT)
                for c in range(KT):
                    mm = nc.tensor.transpose(PS[:, X_BANK + c // 4, (c % 4) * P:(c % 4 + 1) * P], xs[:, c, :],
                                             ident[:, :])
                mm.then_inc(x1_turned, 1)

            def router(t):
                pe.wait_ge(x1T_made, t + 1)
                if t == 0:
                    pe.wait_ge(late_in, 16 * N_LATE)
                    pe.wait_ge(gate_exp, N_MERGE)
                else:
                    pe.wait_ge(router_exp, t)
                for c in range(KT):
                    mm = nc.tensor.matmul(PS[:, C_BANK, 0:N_EXP], xT[:, c, t * P:(t + 1) * P], w_r[:, c, :],
                                          start=(c == 0), stop=(c == KT - 1))
                mm.then_inc(router_done, 1)

            def positions(t):
                pe.wait_ge(sel_made, min(t + 1, QT))
                if t == 0:
                    pe.wait_ge(gated_made, N_MERGE)
                else:
                    pe.wait_ge(info_made, t)
                for u in range(min(t + 1, QT)):
                    mm = nc.tensor.matmul(PS[:, C_BANK + 1, 0:N_EXP], (before if u == t else ones)[:, :], sel[:, u, :],
                                          start=(u == 0), stop=(u == min(t, QT - 1)))
                mm.then_inc(pos_done, 1)

            def gate_up(xs, w, half, done):
                for c in range(KT):
                    mm = nc.tensor.matmul(PS[:, G_BANK + half, 0:F], xs(c), w[:, c, half * F:(half + 1) * F],
                                          start=(c == 0), stop=(c == KT - 1))
                mm.then_inc(done, 1)

            def turn_h(b, half, done):
                nc.tensor.transpose(PS[:, H_BANK, 0:P], h_slots[:, b, half * P:(half + 1) * P], ident[:, :])\
                    .then_inc(done, 1)

            def down(b, wb, half):
                for n in range(2):
                    mm = nc.tensor.matmul(PS[:, Y_BANK + n, :], hT[:, b, half, :],
                                          w_dn[:, wb, half, n * 512:(n + 1) * 512], start=(half == 0), stop=(half == 1))
                return mm

            def shared(t):
                if t == 0:
                    pe.wait_ge(sh_in, 32)
                    pe.wait_ge(var_made, QT)
                else:
                    pe.wait_ge(h_a, t)
                    pe.wait_ge(h_b, t)
                for half, done in ((0, gu_a), (1, gu_b)):
                    gate_up(lambda c: xT[:, c, t * P:(t + 1) * P], w_gu[:, 1, :, :], half, done)
                pe.wait_ge(h_a, t + 1)
                turn_h(t % 2, 0, h_turned_a)
                pe.wait_ge(hT_a, t + 1)
                if t == 0:
                    pe.wait_ge(router_exp, QT)
                    pe.wait_ge(most_made, 1)
                else:
                    pe.wait_ge(y_out1, 2 * t)
                down(t % 2, 1, 0)
                pe.wait_ge(h_b, t + 1)
                turn_h(t % 2, 1, h_turned_b)
                pe.wait_ge(hT_b, t + 1)
                down(t % 2, 1, 1).then_inc(y_done, 1)

            mix(0)
            mix(1)
            for t in range(QT):
                turn_x1(t)
                router(t)
                if t + 2 < QT:
                    mix(t + 2)
                if t >= 1:
                    positions(t - 1)
            positions(QT - 1)
            positions(QT)
            for t in range(QT):
                shared(t)

            def slots(j, b):
                pe.wait_ge(onehot_made, j + 1)
                pe.wait_ge(rows_made, j)
                for t in range(QT):
                    mm = nc.tensor.matmul(PS[:, I_BANK, 0:3], onehot[:, b % 2, t, :],
                                          info[:, t, bass.ds(j, 1), :].rearrange("p a b -> p (a b)"),
                                          start=(t == 0), stop=(t == QT - 1))
                mm.then_inc(slots_done, 1)

            def turn_slots(j, b, wait):
                wait()
                pe.wait_ge(slotsT_made, j)
                xs = x_slots[:, b % 2, :].rearrange("p (q c) -> p c q", c=KT)
                for c in range(KT):
                    mm = nc.tensor.transpose(PS[:, X_BANK + c // 4, (c % 4) * P:(c % 4 + 1) * P], xs[:, c, :],
                                             ident[:, :])
                mm.then_inc(slots_turned, 1)

            slots(0, 0)
            slots(1, 1)
            turn_slots(0, 0, lambda: pe.wait_ge(slots_in[0], 16))
            with pe.Fori(0, N_EXP // 4) as i:
                for b in range(4):
                    e = i * 4 + b
                    pe.wait_ge(slotsT_made, e + 1)
                    pe.wait_ge(gu_in[b % 2], i * 32 + 16 * (b // 2 + 1))
                    pe.wait_ge(h_a, e + QT)
                    xs = lambda c, b=b: x_slotsT[:, b % 2, c, :]
                    gate_up(xs, w_gu[:, b % 2, :, :], 0, gu_a)
                    pe.wait_ge(h_b, e + QT)
                    gate_up(xs, w_gu[:, b % 2, :, :], 1, gu_b)
                    pe.wait_ge(h_a, e + QT + 1)
                    turn_h(b % 2, 0, h_turned_a)
                    turn_slots(e + 1, b + 1,
                               lambda: pe.wait_ge(slots_in[(b + 1) % 2], i * 32 + 16 * ((b + 1) // 2 + 1)))
                    pe.wait_ge(hT_a, e + QT + 1)
                    pe.wait_ge(dn_in[b % 2], i * 32 + 16 * (b // 2 + 1))
                    pe.wait_ge(y_out0, e + 1)
                    pe.wait_ge(y_out1, e + 2 * QT)
                    down(b % 2, b % 2, 0)
                    pe.wait_ge(h_b, e + QT + 1)
                    turn_h(b % 2, 1, h_turned_b)
                    slots(e + 2, b)
                    pe.wait_ge(hT_b, e + QT + 1)
                    down(b % 2, b % 2, 1).then_inc(y_done, 1)

            n = pe.value_load(most_i[0:1, 0:1], min_val=0, max_val=SEQ)
            with pe.If(n > P):
                pe.sem_inc(ov["y"], 1)
                with pe.Fori(1, SEQ // P) as c:
                    with pe.Fori(0, N_EXP) as e:
                        j = (c - 1) * N_EXP + e
                        pe.wait_ge(ov["oh"], j + 1)
                        for t in range(QT):
                            mm = nc.tensor.matmul(PS[:, I_BANK, 0:3], onehot[:, 0, t, :],
                                                  info[:, t, bass.ds(e, 1), :].rearrange("p a b -> p (a b)"),
                                                  start=(t == 0), stop=(t == QT - 1))
                        mm.then_inc(ov["idx"], 1)
                        pe.wait_ge(ov["in"], j * 16 + 16)
                        xs = x_slots[:, 0, :].rearrange("p (q c) -> p c q", c=KT)
                        for k in range(KT):
                            mm = nc.tensor.transpose(PS[:, X_BANK + k // 4, (k % 4) * P:(k % 4 + 1) * P], xs[:, k, :],
                                                     ident[:, :])
                        mm.then_inc(ov["tr"], 1)
                        pe.wait_ge(ov["xT"], j + 1)
                        pe.wait_ge(ov["w"], j * 32 + 32)
                        for half in range(2):
                            gate_up(lambda k: x_slotsT[:, 0, k, :], w_gu[:, 0, :, :], half, ov["gu"])
                        for half in range(2):
                            pe.wait_ge(ov["h"], j * 2 + half + 1)
                            if half == 1:
                                pe.wait_ge(ov["hT"], j * 2 + 1)
                            turn_h(0, half, ov["hturn"])
                        pe.wait_ge(ov["hT"], j * 2 + 2)
                        for half in range(2):
                            mm = down(0, 0, half)
                        mm.then_inc(ov["y"], 1)

        @block.scalar
        def _(act):
            chain = [0]

            def link(ins):
                chain[0] += 1
                ins.then_inc(act_chain, 1)
                act.wait_ge(act_chain, chain[0])

            act.wait_ge(forget_exp, 1)
            link(nc.scalar.activation(fg[:, 1, :], fg[:, 1, :], ACT.Exp))
            nc.scalar.activation(fg[:, 1, :], fg[:, 1, :], ACT.Ln, bias=1.0).then_inc(forget_exp, 1)
            act.wait_ge(lam_dots, 1)
            nc.scalar.activation(lam_s[:, 2:4], lam_s[:, 0:2], ACT.Exp).then_inc(lam_exp, 1)

            for kind, n in order:
                if kind == "proj":
                    u = at_proj[n]
                    what, br, j = PROJ[n]
                    bank = PS[:, C_BANK + u % 2, :]
                    act.wait_ge(proj_done, u + 1)
                    scale = -(32 if br == BR_C else HD) ** -0.5 if what == "q" else 1.0
                    if what == "v":
                        nc.scalar.activation(V[:, :, V_AT[br, j], :], bank.rearrange("p (t n) -> p t n", t=QT),
                                             ACT.Copy).then_inc(proj_out, 1)
                    elif br == BR_A:
                        dst = qA if what == "q" else kA
                        nc.scalar.activation(dst[0:HD, 2 * j, :], bank[0:HD, :], ACT.Copy, scale=scale)
                        nc.scalar.activation(dst[0:HD, 2 * j + 1, :], bank[HD:P, :], ACT.Copy, scale=scale)\
                            .then_inc(proj_out, 1)
                    else:
                        dst = {("q", BR_B): qB, ("k", BR_B): kB, ("q", BR_C): qC, ("k", BR_C): kC,
                               ("q", BR_D): qD, ("k", BR_D): kD}[what, br]
                        nc.scalar.activation(dst[:, j, :], bank, ACT.Copy, scale=scale).then_inc(proj_out, 1)
                elif kind == "scores":
                    br, h, _, qt = STEPS[n]
                    nk = keys_of(br, qt)[1] * P + (br == BR_B)
                    act.wait_ge(biased, n + 1)
                    nc.scalar.activation(probs[:, n % 3, 0:nk], probs[:, n % 3, 0:nk], ACT.Exp,
                                         bias=nmax[:, n:n + 1], scale=-1.0, accum_out=den[:, n:n + 1])\
                        .then_inc(probs_made, 1)
                elif kind == "turn":
                    u = turn_at[kind, n]
                    nk = keys_of(STEPS[n][0], STEPS[n][3])[1] * P
                    act.wait_ge(turned, u + 1)
                    if n >= 3:
                        act.wait_ge(values_done, n - 2)
                    nc.scalar.activation(probsT[:, n % 3, 0:nk], PS[:, T_BANK + u % 2, 0:nk], ACT.Copy)\
                        .then_inc(turned_out, 1)
                elif kind == "turn_y":
                    u = turn_at[kind, n]
                    br, j = n // 2, n % 2
                    act.wait_ge(turned, u + 1)
                    if br >= 2:
                        act.wait_ge(branch_done, (br - 1) * KT)
                    nc.scalar.activation(yT[:, (br % 2) * 2 + j, :], PS[:, T_BANK + u % 2, :], ACT.Copy)\
                        .then_inc(turned_out, 1)
                elif kind == "gate":
                    act.wait_ge(gate_done, n + 1)
                    if n >= 2:
                        act.wait_ge(gated_made, n - 1)
                    nc.scalar.activation(gate[:, n % 2, :], PS[:, C_BANK, :], ACT.Exp, scale=-1.0)\
                        .then_inc(gate_exp, 1)

            def x1T_copy(t):
                act.wait_ge(x1_turned, t + 1)
                for h in range(2):
                    ins = nc.scalar.activation(xT[:, 4 * h:4 * h + 4, t * P:(t + 1) * P],
                                               PS[:, X_BANK + h, :].rearrange("p (c n) -> p c n", c=4), ACT.Copy)
                ins.then_inc(x1T_made, 1)

            def router_exponential(t):
                act.wait_ge(router_done, t + 1)
                if t >= 1:
                    act.wait_ge(scores_used, t)
                nc.scalar.activation(score[:, :], PS[:, C_BANK, 0:N_EXP], ACT.Exp, scale=-1.0).then_inc(router_exp, 1)

            for t in range(QT):
                x1T_copy(t)
                router_exponential(t)

            def sigmoid(half, done):
                nc.scalar.activation(sig[:, half, 0:P], PS[:, G_BANK + half, 0:P], ACT.Sigmoid).then_inc(done, 1)

            def hT_copy(b, half, done):
                nc.scalar.activation(hT[:, b, half, :], PS[:, H_BANK, 0:P], ACT.Copy).then_inc(done, 1)

            for t in range(QT):
                for half, ready, done, made in ((0, gu_a, sig_a, h_a), (1, gu_b, sig_b, h_b)):
                    act.wait_ge(ready, t + 1)
                    if t >= 1:
                        act.wait_ge(made, t)
                    sigmoid(half, done)
                act.wait_ge(h_turned_a, t + 1)
                if t >= 2:
                    act.wait_ge(y_done, t - 1)
                hT_copy(t % 2, 0, hT_a)
                act.wait_ge(h_turned_b, t + 1)
                hT_copy(t % 2, 1, hT_b)

            def slotsT_copy(j, b):
                act.wait_ge(slots_turned, j + 1)
                for h in range(2):
                    ins = nc.scalar.activation(x_slotsT[:, b % 2, 4 * h:4 * h + 4, :],
                                               PS[:, X_BANK + h, :].rearrange("p (c n) -> p c n", c=4), ACT.Copy)
                ins.then_inc(slotsT_made, 1)

            slotsT_copy(0, 0)
            act.sem_inc(y_out0, 1)
            with act.Fori(0, N_EXP // 4) as i:
                for b in range(4):
                    e = i * 4 + b
                    for half, ready, done, made in ((0, gu_a, sig_a, h_a), (1, gu_b, sig_b, h_b)):
                        act.wait_ge(ready, e + QT + 1)
                        act.wait_ge(made, e + QT)
                        sigmoid(half, done)
                    act.wait_ge(h_turned_a, e + QT + 1)
                    act.wait_ge(y_done, e + QT - 1)
                    hT_copy(b % 2, 0, hT_a)
                    slotsT_copy(e + 1, b + 1)
                    act.wait_ge(h_turned_b, e + QT + 1)
                    hT_copy(b % 2, 1, hT_b)
                    act.wait_ge(y_done, e + QT + 1)
                    act.wait_ge(rows_out[b % 2], i * 32 + 16 * (b // 2 + 1))
                    nc.scalar.activation(y_slots[:, b % 2, 0:512], PS[:, Y_BANK, :], ACT.Copy,
                                         scale=w_slot[:, b, :]).then_inc(y_out0, 1)

            n = act.value_load(most_i[0:1, 0:1], min_val=0, max_val=SEQ)
            with act.If(n > P):
                with act.Fori(1, SEQ // P) as c:
                    with act.Fori(0, N_EXP) as e:
                        j = (c - 1) * N_EXP + e
                        act.wait_ge(ov["tr"], j + 1)
                        for h in range(2):
                            ins = nc.scalar.activation(x_slotsT[:, 0, 4 * h:4 * h + 4, :],
                                                       PS[:, X_BANK + h, :].rearrange("p (c n) -> p c n", c=4),
                                                       ACT.Copy)
                        ins.then_inc(ov["xT"], 1)
                        for half in range(2):
                            act.wait_ge(ov["gu"], j * 2 + half + 1)
                            sigmoid(half, ov["sig"])
                        for half in range(2):
                            act.wait_ge(ov["hturn"], j * 2 + half + 1)
                            hT_copy(0, half, ov["hT"])

        @block.vector
        def _(dve):
            chain = [0]

            def link(ins):
                chain[0] += 1
                ins.then_inc(dve_chain, 1)
                dve.wait_ge(dve_chain, chain[0])

            nc.vector.memset(table[:, :], 0.0).then_inc(consts_made, 1)
            link(nc.vector.memset(qA[64:66, :, :], 1.0))
            link(nc.vector.memset(kA[64:66, :, :], 1.0))
            dve.wait_ge(small_in, 16 * SMALL)
            dve.wait_ge(bias_mm, 1)
            link(nc.vector.tensor_tensor(dist_bias[:, 0:512], PS[0:16, S_BANK, 0:512], dist_mask[:, 0:512], ALU.add))
            nc.vector.tensor_tensor(dist_bias[:, 512:640], PS[0:16, S_BANK + 1, 0:128], dist_mask[:, 512:640], ALU.add)\
                .then_inc(bias_made, 1)
            dve.wait_ge(proj_done, 1)
            link(nc.vector.tensor_scalar(fg[:, 0, :], PS[0:4, C_BANK, :], b_f[:, 0:1], None, ALU.add))
            proj_out_first = nc.vector.tensor_scalar(fg[:, 2, :], fg[:, 0, :], -1.0, None, ALU.mult)
            link(proj_out_first)
            link(nc.vector.tensor_tensor(fg[:, 1, :], fg[:, 0, :], fg[:, 2, :], ALU.min))
            link(nc.vector.tensor_scalar(fg[:, 0, :], fg[:, 0, :], 0.0, None, ALU.min))
            dve.sem_inc(proj_out, 1)
            dve.sem_inc(forget_exp, 1)
            for m in range(2):
                link(nc.vector.tensor_tensor_reduce(lam_mul[:, m, :], lam_in[:, 2 * m, :], lam_in[:, 2 * m + 1, :],
                                                    1.0, 0.0, ALU.mult, ALU.add, lam_s[:, m:m + 1]))
            dve.sem_inc(lam_dots, 1)
            link(nc.vector.tensor_scalar(neg_sink[:, :], neg_sink[:, :], -1.0, None, ALU.mult))
            dve.wait_ge(forget_exp, 2)
            link(nc.vector.tensor_tensor(fg[:, 0, :], fg[:, 0, :], fg[:, 1, :], ALU.subtract))
            link(nc.vector.tensor_tensor_scan(fg[:, 2, :], fg[:, 0, :], fg[:, 0, :], 0.0, ALU.add, ALU.bypass))
            link(nc.vector.tensor_scalar(fg[:, 3, :], fg[:, 2, :], -1.0, None, ALU.mult))
            dve.sem_inc(forget_made, 1)
            dve.wait_ge(lam_exp, 1)
            link(nc.vector.tensor_tensor(lam_s[:, 4:5], lam_s[:, 3:4], lam_s[:, 2:3], ALU.subtract))
            link(nc.vector.tensor_scalar(lam_s[:, 5:6], lam_s[:, 4:5], -LAM_INIT, None, ALU.add))

            def turn_wait(s):
                dve.wait_ge(turned, turn_at["turn", s] + 1)

            def bias_step(s):
                br, h, c, qt = STEPS[s]
                nk = keys_of(br, qt)[1] * P
                row = {BR_A: 12, BR_B: h, BR_C: 4 + h, BR_D: 8 + h}[br]
                if s == 0:
                    dve.wait_ge(strips_in, 16)
                dve.wait_ge(scores_done, s + 1)
                if s >= 3:
                    turn_wait(s - 3)
                if br == BR_B:
                    nc.vector.tensor_copy(probs[:, s % 3, nk:nk + 1], neg_sink[:, h:h + 1])
                start = neg_sink[:, h:h + 1] if br == BR_B else 3e38
                lo = SEQ - nk
                nc.vector.tensor_tensor_reduce(probs[:, s % 3, 0:nk], PS[:, S_BANK + s % 2, 0:nk], strips[:, row, lo:SEQ],
                                               1.0, start, ALU.add, ALU.min, nmax[:, s:s + 1]).then_inc(biased, 1)

            def out_step(s):
                br, h, c, qt = STEPS[s]
                dve.wait_ge(values_done, s + 1)
                link(nc.vector.reciprocal(rden[:, s:s + 1], den[:, s:s + 1]))
                dst = Y[:, (br % 2) * QT + qt, h * HD:(h + 1) * HD]
                src = PS[:, O_BANK + s % 2, 0:HD]
                if br >= 2 and s == last_step[br - 1] + 1:
                    dve.wait_ge(turned, turn_at["turn_y", 2 * (br - 2) + 1] + 1)
                if br == BR_C and c == 1:
                    link(nc.vector.tensor_scalar(rden[:, s:s + 1], rden[:, s:s + 1], lam_s[:, 5:6], None, ALU.mult))
                    dve.wait_ge(y_made, s - QT + 1)
                    nc.vector.scalar_tensor_tensor(dst, src, rden[:, s:s + 1], dst, ALU.mult, ALU.add)\
                        .then_inc(y_made, 1)
                else:
                    nc.vector.tensor_scalar(dst, src, rden[:, s:s + 1], None, ALU.mult).then_inc(y_made, 1)
                if s == last_step[br]:
                    dve.wait_ge(y_made, s + 1)
                    if br == BR_C:
                        for t in range(QT):
                            yt = Y[:, (br % 2) * QT + t, :]
                            link(nc.vector.tensor_tensor(yc_sq[:, :], yt, yt, ALU.mult))
                            link(nc.vector.tensor_reduce(yc_ss[:, 4 * t:4 * t + 4],
                                                         yc_sq[:, :].rearrange("p (h d) -> p h d", h=4), AX.X, ALU.add))
                        link(nc.vector.tensor_scalar(yc_ss[:, :], yc_ss[:, :], 1.0 / HD, EPS, ALU.mult, ALU.add))
                        dve.sem_inc(yc_stat, 1)
                    else:
                        dve.sem_inc(y_ready, 1)

            def norm_c():
                dve.wait_ge(yc_rms, 1)
                for t in range(QT):
                    for h in range(4):
                        yt = Y[:, (BR_C % 2) * QT + t, h * HD:(h + 1) * HD]
                        ins = nc.vector.scalar_tensor_tensor(yt, yt, yc_ss[:, 4 * t + h:4 * t + h + 1], norm_g[:, :],
                                                             ALU.mult, ALU.mult)
                        if t == QT - 1 and h == 3:
                            link(ins)
                for t in range(QT):
                    yt = Y[:, (BR_C % 2) * QT + t, :]
                    ins = nc.vector.tensor_scalar(yt, yt, 1.0 - LAM_INIT, None, ALU.mult)
                    link(ins)
                dve.sem_inc(y_ready, 1)

            for kind, n in order:
                if kind == "scores":
                    bias_step(n)
                    if n == norm_step:
                        norm_c()
                elif kind == "values":
                    out_step(n)
                elif kind == "gate":
                    dve.wait_ge(gate_exp, n + 1)
                    g = gate[:, n % 2, :]
                    link(nc.vector.tensor_scalar(g, g, 1.0, None, ALU.add))
                    link(nc.vector.reciprocal(g, g))
                elif kind == "branch":
                    dve.wait_ge(branch_done, n + 1)
                    if n < KT:
                        dst = mT[:, n, :]
                    else:
                        dst = gated[:, n % 2, :]
                        if n >= KT + 2:
                            dve.wait_ge(merged, n - 1)
                    nc.vector.tensor_tensor(dst, PS[:, C_BANK + 1, :], gate[:, n % 2, :], ALU.mult)\
                        .then_inc(gated_made, 1)

            def norm(v, k):
                for h in range(2):
                    ins = nc.vector.bn_stats(stats[:, h, :], v[:, h * 512:(h + 1) * 512])
                link(ins)
                link(nc.vector.bn_aggr(mv[:, 0:2], stats[:, :, :].rearrange("p a b -> p (a b)")))
                link(nc.vector.tensor_scalar(mv[:, 1:2], mv[:, 1:2], EPS, None, ALU.add))
                dve.sem_inc(var_made, 1)
                dve.wait_ge(rstd_made, k + 1)
                link(nc.vector.tensor_scalar(v, v, mv[:, 0:1], mv[:, 1:2], ALU.subtract, ALU.mult))

            def first_norm(t):
                bank = S_BANK if t % 2 == 0 else O_BANK
                dve.wait_ge(mix_done, t + 1)
                dve.wait_ge(x_in, 16 * QT)
                v = x1[:, t, :]
                link(nc.vector.scalar_tensor_tensor(v, x_nat[:, t, :], ALPHA,
                                                    PS[:, bank:bank + 2, :].rearrange("p a b -> p (a b)"),
                                                    ALU.mult, ALU.add))
                norm(v, t)
                link(nc.vector.tensor_tensor(v, v, ln1[:, 0, :], ALU.mult))
                if t == 0:
                    dve.wait_ge(late_in, 16 * N_LATE)
                nc.vector.tensor_tensor(v, v, ln1[:, 1, :], ALU.add).then_inc(x1_made, 1)

            def pick(values, eighth, n, k, dst):
                more, same, upto = (rt8[:, 0, :], rt8[:, 1, :], rt8[:, 2, :]) if n == 8 else \
                    (rt64[:, 0, :], rt64[:, 1, :], rt64[:, 2, :])
                left = wsum[:, 4:5]
                link(nc.vector.tensor_scalar(more, values, eighth, None, ALU.is_gt))
                link(nc.vector.tensor_reduce(left, more, AX.X, ALU.add))
                link(nc.vector.tensor_scalar(left, left, -1.0, float(k), ALU.mult, ALU.add))
                link(nc.vector.tensor_scalar(same, values, eighth, None, ALU.is_equal))
                link(nc.vector.tensor_tensor_scan(upto, same, same, 0.0, ALU.add, ALU.bypass))
                link(nc.vector.scalar_tensor_tensor(same, upto, left, same, ALU.is_le, ALU.mult))
                link(nc.vector.tensor_tensor(dst, more, same, ALU.add))

            def route(t):
                dve.wait_ge(router_exp, t + 1)
                link(nc.vector.tensor_scalar(score[:, :], score[:, :], 1.0, None, ALU.add))
                link(nc.vector.reciprocal(score[:, :], score[:, :]))
                link(nc.vector.tensor_tensor(choice[:, :], score[:, :], r_bias[:, :], ALU.add))
                for g in range(N_GROUPS):
                    ins = nc.vector.max(top2[:, g, :], choice[:, g * GROUP:(g + 1) * GROUP])
                link(ins)
                link(nc.vector.tensor_tensor(gscore[:, :], top2[:, :, 0], top2[:, :, 1], ALU.add))
                link(nc.vector.max(rt8[:, 4, :], gscore[:, :]))
                pick(gscore[:, :], rt8[:, 4, TOPK_GROUPS - 1:TOPK_GROUPS], 8, TOPK_GROUPS, rt8[:, 3, :])
                link(nc.vector.tensor_scalar(rt8[:, 5, :], rt8[:, 3, :], MASKED, -MASKED, ALU.mult, ALU.add))
                c8 = choice[:, :].rearrange("p (g e) -> p g e", g=N_GROUPS)
                link(nc.vector.tensor_tensor(c8, c8, rt8[:, 5, :].unsqueeze(2).broadcast_to([P, N_GROUPS, GROUP]),
                                             ALU.add))
                link(nc.vector.max(rt8[:, 6, :], choice[:, :]))
                pick(choice[:, :], rt8[:, 6, TOP_K - 1:TOP_K], N_EXP, TOP_K, sel[:, t, :])
                dve.sem_inc(sel_made, 1)
                s = sel[:, t, :]
                link(nc.vector.tensor_tensor_reduce(rt64[:, 3, :], s, score[:, :], 1.0, 0.0, ALU.mult, ALU.add,
                                                    wsum[:, 0:1]))
                dve.sem_inc(scores_used, 1)
                link(nc.vector.reciprocal(wsum[:, 1:2], wsum[:, 0:1]))
                link(nc.vector.tensor_scalar(info[:, t, 0:N_EXP, 2], rt64[:, 3, :], wsum[:, 1:2], ROUTED_SCALE,
                                             ALU.mult, ALU.mult))
                link(nc.vector.tensor_tensor_scan(rank[:, :], s, s, 0.0, ALU.add, ALU.bypass))
                dve.wait_ge(consts_made, 6)
                tok = tok_row[:, t:t + 1]
                link(nc.vector.tensor_scalar(info[:, t, 0:N_EXP, 0], s, 0.0, tok, ALU.mult, ALU.add))
                link(nc.vector.tensor_scalar(info[:, t, 0:N_EXP, 0], info[:, t, 0:N_EXP, 0], -UNUSED, None, ALU.add))
                link(nc.vector.tensor_scalar(wsum[:, 2:3], tok, float(TOP_K), -1.0 - UNUSED, ALU.mult, ALU.add))
                link(nc.vector.tensor_scalar(info[:, t, 0:N_EXP, 1], rank[:, :], wsum[:, 2:3], None, ALU.add))

            def slots_of(t):
                dve.wait_ge(pos_done, t + 1)
                p = PS[:, C_BANK + 1, 0:N_EXP]
                link(nc.vector.tensor_scalar(rt64[:, 0, :], sel[:, t, :], -NO_SLOT, NO_SLOT, ALU.mult, ALU.add))
                nc.vector.tensor_tensor(pos[:, t, 0:N_EXP], p, rt64[:, 0, :], ALU.add).then_inc(info_made, 1)

            dve.wait_ge(branch_done, N_MERGE)
            dve.wait_ge(merged, N_MERGE)
            nc.vector.memset(pos[:, :, :], NO_SLOT)
            link(nc.vector.memset(info[:, :, :, :], 0.0))
            first_norm(0)
            first_norm(1)
            for t in range(QT):
                route(t)
                if t + 2 < QT:
                    first_norm(t + 2)
                if t >= 1:
                    slots_of(t - 1)
            slots_of(QT - 1)
            dve.wait_ge(pos_done, QT + 1)
            link(nc.vector.tensor_reduce(most[:, 0:1], PS[:, C_BANK + 1, 0:N_EXP], AX.X, ALU.max))
            nc.vector.tensor_copy(most_i[:, 0:1], most[0:1, 0:1]).then_inc(most_made, 1)

            def h_half(half, b, count, done):
                nc.vector.tensor_tensor(silu[:, half, 0:P], PS[:, G_BANK + half, 0:P], sig[:, half, 0:P], ALU.mult)\
                    .then_inc(silu_made, 1)
                dve.wait_ge(silu_made, count)
                nc.vector.tensor_tensor(h_slots[:, b, half * P:(half + 1) * P], PS[:, G_BANK + half, P:F],
                                        silu[:, half, 0:P], ALU.mult).then_inc(done, 1)

            for t in range(QT):
                dve.wait_ge(sig_a, t + 1)
                if t >= 2:
                    dve.wait_ge(y_done, t - 1)
                h_half(0, t % 2, 2 * t + 1, h_a)
                dve.wait_ge(sig_b, t + 1)
                h_half(1, t % 2, 2 * t + 2, h_b)
                dve.wait_ge(y_done, t + 1)
                for n in range(2):
                    nc.vector.scalar_tensor_tensor(mT_nat(t)[:, n * 512:(n + 1) * 512], x1[:, t, n * 512:(n + 1) * 512],
                                                   ALPHA, PS[:, Y_BANK + n, :], ALU.mult, ALU.add).then_inc(y_out1, 1)

            def mark_slots(j, b):
                nc.vector.tensor_tensor(onehot[:, b % 2, :, :],
                                        slot_no[:, :].unsqueeze(1).broadcast_to([P, QT, P]),
                                        pos[:, :, bass.ds(j, 1)].broadcast_to([P, QT, P]),
                                        ALU.is_equal).then_inc(onehot_made, 1)

            def rows_of(b, done):
                nc.vector.tensor_copy(w_slot[:, b, :], PS[:, I_BANK, 2:3])
                nc.vector.tensor_scalar(rows_u[:, b, :], PS[:, I_BANK, 0:2], UNUSED, None, ALU.add).then_inc(done, 1)

            dve.wait_ge(info_made, QT)
            for j in range(2):
                mark_slots(j, j)
            for j in range(2):
                dve.wait_ge(slots_done, j + 1)
                rows_of(j, rows_made)
                dve.wait_ge(rows_out[j], 16)
            with dve.Fori(0, N_EXP // 4) as i:
                for b in range(4):
                    e = i * 4 + b
                    dve.wait_ge(slots_done, e + 1)
                    mark_slots(e + 2, b)
                    dve.wait_ge(sig_a, e + QT + 1)
                    h_half(0, b % 2, e * 2 + 2 * QT + 1, h_a)
                    dve.wait_ge(sig_b, e + QT + 1)
                    h_half(1, b % 2, e * 2 + 2 * QT + 2, h_b)
                    dve.wait_ge(slots_done, e + 3)
                    dve.wait_ge(y_out0, e + 1)
                    dve.wait_ge(rows_out[b % 2], i * 32 + 16 * (b // 2 + 1))
                    rows_of((b + 2) % 4, rows_made)
                    dve.wait_ge(y_done, e + QT + 1)
                    nc.vector.tensor_scalar(y_slots[:, b % 2, 512:D], PS[:, Y_BANK + 1, :], w_slot[:, b, :], None,
                                            ALU.mult).then_inc(y_out1, 1)

            n = dve.value_load(most_i[0:1, 0:1], min_val=0, max_val=SEQ)
            with dve.If(n > P):
                nc.vector.tensor_copy(ov_slot[:, :], slot_no[:, :]).then_inc(ov["silu"], 1)
                with dve.Fori(1, SEQ // P) as c:
                    dve.wait_ge(ov["silu"], (c - 1) * (2 * N_EXP + 1) + 1)
                    nc.vector.tensor_scalar(ov_slot[:, :], ov_slot[:, :], float(P), None, ALU.add)\
                        .then_inc(ov["silu"], 1)
                    dve.wait_ge(ov["silu"], (c - 1) * (2 * N_EXP + 1) + 2)
                    dve.sem_inc(ov["turns"], 1)
                    with dve.Fori(0, N_EXP) as e:
                        j = (c - 1) * N_EXP + e
                        nc.vector.tensor_tensor(onehot[:, 0, :, :],
                                                ov_slot[:, :].unsqueeze(1).broadcast_to([P, QT, P]),
                                                pos[:, :, bass.ds(e, 1)].broadcast_to([P, QT, P]),
                                                ALU.is_equal).then_inc(ov["oh"], 1)
                        dve.wait_ge(ov["idx"], j + 1)
                        rows_of(0, ov["rows"])
                        for half in range(2):
                            dve.wait_ge(ov["sig"], j * 2 + half + 1)
                            nc.vector.tensor_tensor(silu[:, half, 0:P], PS[:, G_BANK + half, 0:P], sig[:, half, 0:P],
                                                    ALU.mult).then_inc(ov["silu"], 1)
                            dve.wait_ge(ov["silu"], j * 2 + half + c + 2)
                            nc.vector.tensor_tensor(h_slots[:, 0, half * P:(half + 1) * P], PS[:, G_BANK + half, P:F],
                                                    silu[:, half, 0:P], ALU.mult).then_inc(ov["h"], 1)
                        dve.wait_ge(ov["y"], j + 2)
                        for m in range(2):
                            ins = nc.vector.tensor_scalar(y_slots[:, 0, m * 512:(m + 1) * 512], PS[:, Y_BANK + m, :],
                                                          w_slot[:, 0, :], None, ALU.mult)
                        ins.then_inc(ov["yout"], 1)
                        dve.wait_ge(ov["out"], j * 16 + 16)

            for t in range(QT):
                dve.wait_ge(rows8_in[t % 2], 16 * (t // 2 + 1))
                v = mT_nat(t)
                acc = rows8[:, t % 2, 0, :]
                link(nc.vector.tensor_reduce(ring[:, 0:1, 0:D].rearrange("p a b -> p (a b)"),
                                             rows8[:, t % 2, :, :].rearrange("p r d -> p d r"), AX.X, ALU.add))
                dve.sem_inc(sums, 1)
                link(nc.vector.tensor_tensor(v, v, ring[:, 0, 0:D], ALU.add))
                norm(v, QT + t)
                link(nc.vector.tensor_tensor(v, v, ln2[:, 0, :], ALU.mult))
                nc.vector.tensor_tensor(v, v, ln2[:, 1, :], ALU.add).then_inc(out_made, 1)

        @block.gpsimd
        def _(pool):
            pool.wait_ge(consts_made, 1)
            nc.gpsimd.memset(ones[:, :], 1.0).then_inc(pool_chain, 1)
            nc.gpsimd.memset(half_neg[:, :], -0.5).then_inc(pool_chain, 1)
            nc.gpsimd.memset(ident[:, :], 0.0).then_inc(pool_chain, 1)
            pool.wait_ge(pool_chain, 3)
            nc.gpsimd.affine_select(out=ident[:, :], in_=ident[:, :], compare_op=ALU.not_equal, fill=1.0, base=0,
                                    pattern=[[-1, P]], channel_multiplier=1).then_inc(consts_made, 1)
            nc.gpsimd.affine_select(out=before[:, :], in_=ones[:, :], compare_op=ALU.is_gt, fill=0.0, base=0,
                                    pattern=[[1, P]], channel_multiplier=-1).then_inc(consts_made, 1)
            nc.gpsimd.iota(slot_no[:, :], pattern=[[1, P]], base=0, channel_multiplier=0,
                           allow_small_or_imprecise_dtypes=True).then_inc(consts_made, 1)
            nc.gpsimd.iota(tok_row[:, :], pattern=[[P, QT]], base=0, channel_multiplier=1,
                           allow_small_or_imprecise_dtypes=True).then_inc(consts_made, 1)
            pool.wait_ge(consts_made, 5)
            pool.sem_inc(consts_made, 1)

            def root(v, ready, count, done):
                pool.wait_ge(ready, count)
                nc.gpsimd.tensor_tensor(v, v, half_neg[:, 0:v.shape[1]], ALU.pow).then_inc(done, 1)

            for m in range(N_MERGE):
                if m == merges_before_norm:
                    root(yc_ss[:, :], yc_stat, 1, yc_rms)
                pool.wait_ge(gated_made, m + 1)
                if m < KT:
                    pool.sem_inc(merged, 1)
                    continue
                if m >= KT + 1:
                    pool.wait_ge(merged, m)
                k = m % KT
                nc.gpsimd.tensor_tensor(mT[:, k, :], mT[:, k, :], gated[:, m % 2, :], ALU.add).then_inc(merged, 1)

            for k in range(QT):
                root(mv[:, 1:2], var_made, k + 1, rstd_made)
            pool.wait_ge(mix_done, QT)
            nc.gpsimd.memset(x_slots[:, :, :], 0.0).then_inc(slots_clear, 1)
            nc.gpsimd.memset(y_slots[:, :, :], 0.0).then_inc(slots_clear, 1)
            nc.gpsimd.memset(rows_u[:, 2:4, :], int(UNUSED)).then_inc(slots_clear, 1)
            pool.wait_ge(slots_clear, 3)
            last_tok = pool.to_reg(SEQ - 1)
            last_row = pool.to_reg(SEQ * TOP_K - 1)

            def gather(b, xb, done):
                pool.sem_inc(gathers_begun, 1)
                pool.indirect_dma_start(x_slots[:, xb, :], None, x1_d,
                                        bass.IndirectOffsetOnAxis(ap=rows_u[:, b, 0:1], axis=0),
                                        bounds_check=last_tok, oob_is_err=False).then_inc(done, 16)

            def scatter(b, yb, done):
                pool.sem_inc(scatters_begun, 1)
                pool.indirect_dma_start(rows_d, bass.IndirectOffsetOnAxis(ap=rows_u[:, b, 1:2], axis=0),
                                        y_slots[:, yb, :], None,
                                        bounds_check=last_row, oob_is_err=False).then_inc(done, 16)

            for b in range(2):
                scatter(2 + b, b, rows_out[b])
                pool.wait_ge(rows_out[b], 16)
            pool.wait_ge(x1_stored, 16 * QT)
            for j in range(2):
                pool.wait_ge(rows_made, j + 1)
                gather(j, j, slots_in[j])
            with pool.Fori(0, N_EXP // 4) as i:
                for b in range(4):
                    e = i * 4 + b
                    pool.wait_ge(rows_made, e + 3)
                    pool.wait_ge(slots_turned, e + 1)
                    gather((b + 2) % 4, b % 2, slots_in[b % 2])
                    pool.wait_ge(y_out0, e + 2)
                    pool.wait_ge(y_out1, e + 2 * QT + 1)
                    scatter(b, b % 2, rows_out[b % 2])
            for b in range(2):
                pool.wait_ge(slots_in[b], 16 * (N_EXP // 2 + 1))
                pool.wait_ge(rows_out[b], 16 * (N_EXP // 2 + 1))

            n = pool.value_load(most_i[0:1, 0:1], min_val=0, max_val=SEQ)
            with pool.If(n > P):
                with pool.Fori(1, SEQ // P) as c:
                    with pool.Fori(0, N_EXP) as e:
                        j = (c - 1) * N_EXP + e
                        pool.wait_ge(ov["rows"], j + 1)
                        gather(0, 0, ov["in"])
                        pool.wait_ge(ov["yout"], j + 1)
                        scatter(0, 0, ov["out"])
                pool.wait_ge(ov["out"], 16 * (SEQ // P - 1) * N_EXP)

            for k in range(QT, 2 * QT):
                root(mv[:, 1:2], var_made, k + 1, rstd_made)


def kernel(**inputs):
    import concourse.bacc as _bacc
    from concourse.bass_utils import run_bass_kernel_spmd as _run

    g = {k: np.asarray(v) for k, v in inputs.items()}
    w_in = g["w_in"][0]

    def columns(kind, br, j):
        first = COLS[kind, br]
        if (kind, br) == ("q", BR_B):
            return np.concatenate([first + h * HD + np.arange(HD) for h in (j, j + 2)])
        return first + j * P + np.arange(P)

    def tiles(w, n):
        return w.reshape(KT, P, n, P).transpose(2, 1, 0, 3)

    arrays = {
        "x": g["x"], "xT": g["x"][0].T, "t5_table": g["t5_table"],
        "w_proj": tiles(w_in[:, np.concatenate([columns(*c) for c in PROJ])], N_PROJ).reshape(N_PROJ, P, KT * P),
        "w_f": w_in[:, COLS["f"]:COLS["f"] + 4].reshape(KT, P, 4).transpose(1, 0, 2),
        "w_merge": np.concatenate([
            tiles(w_in[:, COLS["gates"]:], N_MERGE),
            g["w_branch"][0].reshape(4, 2, P, KT, P).transpose(0, 3, 2, 1, 4).reshape(N_MERGE, P, 2, P)],
            axis=2).reshape(N_MERGE, P, SLOT),
        "w_out": g["w_out"], "b_forget": g["b_forget"], "attn_sinks": g["attn_sinks"],
        "lam": np.stack([g["lam_q1"], g["lam_k1"], g["lam_q2"], g["lam_k2"]], axis=1),
        "diff_norm_g": g["diff_norm_g"], "ln1_g": g["ln1_g"], "ln1_b": g["ln1_b"], "ln2_g": g["ln2_g"],
        "ln2_b": g["ln2_b"], "w_router": g["w_router"], "router_bias": g["router_bias"],
        "w_gu": np.stack([g["w_gate_e"][0].reshape(N_EXP, D, FT, P), g["w_up_e"][0].reshape(N_EXP, D, FT, P)],
                         axis=3).reshape(N_EXP, P, KT * 2 * F),
        "w_down_e": g["w_down_e"],
        "w_gu_s": np.stack([g["w_gate_s"][0].reshape(D, FT, P), g["w_up_s"][0].reshape(D, FT, P)],
                           axis=2).reshape(P, KT * 2 * F),
        "w_down_s": g["w_down_s"],
    }
    arrays["neg_onehot"], arrays["dist_mask"] = distance_constants()
    arrays = {k: np.ascontiguousarray(v) for k, v in arrays.items()}
    nc = _bacc.Bacc("TRN2", target_bir_lowering=False, num_devices=1)
    aps = {k: nc.dram_tensor(f"in_{k}", v.shape, mybir.dt.from_np(v.dtype), kind="ExternalInput").ap()
           for k, v in arrays.items()}
    out = nc.dram_tensor("out_0", (1, SEQ, D), F32, kind="ExternalOutput").ap()
    build(nc, aps, out)
    r = _run(nc, [{f"in_{k}": v for k, v in arrays.items()}], core_ids=[0])
    return r.results[0]["out_0"]
```

```python
from contextlib import ExitStack

import numpy as np

import concourse.bass as bass
from concourse import mybir

F32 = mybir.dt.float32
F32R = mybir.dt.float32r
U32 = mybir.dt.uint32
I32 = mybir.dt.int32
ALU = mybir.AluOpType
ACT = mybir.ActivationFunctionType
AX = mybir.AxisListType

P = 128
SEQ = 512
D = 1024
QT = SEQ // P
KT = D // P
HD = 64
WINDOW = 128
DILATIONS = ((128, 1), (512, 4), (2048, 16))
N_EXP = 64
TOP_K = 8
N_GROUPS = 8
TOPK_GROUPS = 4
GROUP = N_EXP // N_GROUPS
F = 256
FT = F // P
ROUTED_SCALE = 2.5
ALPHA = 2 ** 0.25
EPS = 1e-5
LAM_INIT = 0.2
BUCKETS = 32
MAX_DIST = 2048
MASKED = 1e30
UNUSED = 65536.0
NO_SLOT = 16384.0
BR_A, BR_B, BR_C, BR_D = range(4)

PROJ = ([("q", BR_A, 0), ("q", BR_A, 1), ("k", BR_A, 0), ("k", BR_A, 1), ("v", BR_A, 0), ("v", BR_A, 1)]
        + [("q", BR_B, 0), ("q", BR_B, 1), ("k", BR_B, 0), ("v", BR_B, 0)]
        + [(kind, br, j) for br in (BR_C, BR_D) for kind in "qkv" for j in range(2)])
V_AT = {(BR_A, 0): 0, (BR_A, 1): 1, (BR_B, 0): 2, (BR_C, 0): 3, (BR_C, 1): 4, (BR_D, 0): 5, (BR_D, 1): 6}
N_PROJ = len(PROJ)
N_MERGE = 4 * KT
N_CHUNKS = N_PROJ + N_MERGE
RING = 3
HALVES = 2
X_PARTS = 4
W_OUT_AFTER = N_PROJ + 26
SLOT = 10 * P

COLS = {("q", BR_A): 0, ("k", BR_A): 256, ("v", BR_A): 512, "f": 768,
        ("q", BR_B): 772, ("k", BR_B): 1028, ("v", BR_B): 1156,
        ("q", BR_C): 1284, ("k", BR_C): 1540, ("v", BR_C): 1796,
        ("q", BR_D): 2052, ("k", BR_D): 2308, ("v", BR_D): 2564, "gates": 2820}


def attention_steps():
    return ([(BR_A, h, 0, q) for h in range(4) for q in range(QT)]
            + [(BR_B, h, 0, q) for h in range(4) for q in range(QT)]
            + [(BR_C, h, c, q) for h in range(4) for c in range(2) for q in range(QT)]
            + [(BR_D, h, 0, q) for h in range(4) for q in range(QT)])


STEPS = attention_steps()


def keys_of(branch, qt):
    if branch == BR_B:
        return max(qt - 1, 0), min(qt, 1) + 1
    return 0, qt + 1


def order_of_work():
    proj, merges, steps = list(range(6, N_PROJ)), list(range(N_MERGE)), list(range(len(STEPS)))
    order = [("proj", c) for c in range(6)]

    def step(s):
        out = [("scores", s)]
        if s >= 1:
            out.append(("turn", s - 1))
        if s >= 2:
            out.append(("values", s - 2))
        if s >= 4 and STEPS[s - 4][0] != STEPS[s - 3][0]:
            out += [("turn_y", 2 * STEPS[s - 4][0] + j) for j in range(2)]
        return out

    def part(m, i):
        return [("part", 3 * m + i)] + ([("gate", m)] if i == 2 else [])

    def merge(m):
        return part(m, 0) + part(m, 1) + part(m, 2), [("branch", m), ("gated", m)]

    for s in range(16):
        order += [("proj", proj.pop(0))] + step(s)
    for s in range(16, 20):
        order += step(s)
    at = 20
    while at < len(STEPS):
        m = merges.pop(0)
        if STEPS[at][0] == BR_C:
            plan = [part(m, 0), 1, part(m, 1), 1, part(m, 2), 1, [("branch", m), ("gated", m)], 1]
        else:
            plan = [part(m, 0) + part(m, 1), 1, part(m, 2) + [("branch", m)], 1, [("gated", m)]]
        for x in plan:
            if x == 1:
                if at < len(STEPS):
                    order += step(at)
                at += 1
            else:
                order += x
    last = len(STEPS)
    g, z = merge(merges.pop(0))
    order += g + [("turn", last - 1), ("values", last - 2)] + z
    g, z = merge(merges.pop(0))
    order += g + [("values", last - 1)] + z
    order += [("turn_y", 2 * BR_D + j) for j in range(2)]
    while merges:
        g, z = merge(merges.pop(0))
        order += g + z
    return order


def distance_constants():
    dist = 511 - np.arange(640)
    n = np.maximum(dist, 0)
    exact = BUCKETS // 2
    large = exact + (np.log(np.maximum(n, 1) / exact) / np.log(MAX_DIST / exact) * (BUCKETS - exact)).astype(np.int32)
    bucket = np.where(n < exact, n, np.minimum(large, BUCKETS - 1))
    onehot = -(np.arange(BUCKETS)[:, None] == bucket[None, :]).astype(np.float32)
    times = sum(((dist <= (w // d) * d) & (dist % d == 0)).astype(np.int64) for w, d in DILATIONS)
    causal = np.where(dist >= 0, 0.0, MASKED)
    window = np.where((dist >= 0) & (dist < WINDOW), 0.0, MASKED)
    dilated = np.where((dist >= 0) & (times > 0), -np.log(np.maximum(times, 1)), MASKED)
    rows = [window] * 4 + [causal] * 4 + [dilated] * 4
    mask = np.zeros((16, 640), np.float32)
    mask[:12] = np.stack(rows)
    m = np.arange(SEQ)
    strip = np.where(np.arange(P)[:, None] + (SEQ - P) - m[None, :] >= 0, 0.0, MASKED).astype(np.float32)
    return onehot, mask, strip


def build(nc, a, out):
    order = order_of_work()
    turns = [x for x in order if x[0] in ("turn", "turn_y")]
    turn_at = {x: n for n, x in enumerate(turns)}
    n_steps = len(STEPS)
    last_step = {br: max(s for s, x in enumerate(STEPS) if x[0] == br) for br in range(4)}
    norm_step = last_step[BR_C] + 3
    merges_before_norm = sum(kind == "gated" for kind, _ in order[:order.index(("scores", norm_step))])
    at_proj = {n: n + 1 for n in range(N_PROJ)}

    ctx = ExitStack()
    with ctx:
        def sb(name, shape, dt=F32):
            return ctx.enter_context(nc.sbuf_tensor(name, shape, dt))

        def sem(name):
            return ctx.enter_context(nc.semaphore(name))

        PS = ctx.enter_context(nc.psum_tensor("PS", [P, 8, 512], F32))
        ident = sb("ident", [P, P])
        before = sb("before", [P, P])
        ones = sb("ones", [P, P])
        half_neg = sb("half_neg", [P, 16])
        slot_no = sb("slot_no", [P, P])
        tok_row = sb("tok_row", [P, QT])
        mT = sb("mT", [P, KT, SEQ])
        w_f = sb("w_f", [P, KT, 4])
        b_f = sb("b_f", [4, 1])
        table = sb("table", [BUCKETS, 16])
        neg_sink = sb("neg_sink", [P, 4])
        lam_in = sb("lam_in", [P, 4, 32])
        lam_mul = sb("lam_mul", [P, 2, 32])
        lam_s = sb("lam_s", [P, 8])
        norm_g = sb("norm_g", [P, HD])
        nmax = sb("nmax", [P, n_steps])
        den = sb("den", [P, n_steps])
        rden = sb("rden", [P, n_steps])
        yc_sq = sb("yc_sq", [P, F])
        yc_ss = sb("yc_ss", [P, 16])
        stats = sb("stats", [P, 2, 6])
        mv = sb("mv", [P, 8])
        r_bias = sb("r_bias", [P, N_EXP])
        gscore = sb("gscore", [P, 8])
        rt8 = sb("rt8", [P, 8, 8])
        sel = sb("sel", [P, QT, N_EXP])
        rank = sb("rank", [P, N_EXP])
        wsum = sb("wsum", [P, 8])
        rows_u = sb("rows_u", [P, 4, 2], U32)
        w_slot = sb("w_slot", [P, 4, 1])
        most = sb("most", [P, 2])
        most_i = sb("most_i", [1, 2], I32)
        ov_slot = sb("ov_slot", [P, P])
        attention = ExitStack()

        def sb1(name, shape, dt=F32):
            return attention.enter_context(nc.sbuf_tensor(name, shape, dt))

        x_hi = sb1("x_hi", [P, KT, SEQ], F32R)
        x_lo = sb1("x_lo", [P, KT, SEQ], F32R)
        w_hi = sb1("w_hi", [P, HALVES, KT, P], F32R)
        w_lo = sb1("w_lo", [P, HALVES, KT, P], F32R)
        ring = sb1("ring", [P, RING, SLOT])
        region1 = sb1("region1", [P, 29190])

        def carve(region, start, shape):
            n = int(np.prod(shape))
            v = region[:, start:start + n]
            if len(shape) == 2:
                v = v.rearrange("p (a b) -> p a b", a=shape[0])
            elif len(shape) == 3:
                v = v.rearrange("p (a b c) -> p a b c", a=shape[0], b=shape[1])
            return v, start + n

        qA, o = carve(region1, 0, (4, SEQ))
        kA, o = carve(region1, o, (4, SEQ))
        qB, o = carve(region1, o, (2, SEQ))
        kB, o = carve(region1, o, (1, SEQ))
        qC, o = carve(region1, o, (2, SEQ))
        kC, o = carve(region1, o, (2, SEQ))
        strips, o = carve(region1, o, (13, SEQ))
        w_out, _ = carve(region1, 0, (KT, D))
        qD, o = carve(region1, o, (2, SEQ))
        kD, o = carve(region1, o, (2, SEQ))
        V, o = carve(region1, o, (QT, 7, P))
        probs, o = carve(region1, o, (3, SEQ + 2))
        probsT, o = carve(region1, o, (3, SEQ))
        Y, o = carve(region1, o, (2 * QT, F))
        yT, o = carve(region1, o, (4, SEQ))
        gate, o = carve(region1, o, (2, SEQ))
        gated, o = carve(region1, o, (2, SEQ))
        assert o == 29190, o
        fg = yT[0:4, :, :]
        neg_oh = gate.rearrange("p a b -> p (a b)")[0:BUCKETS, 0:640]
        dist_mask = gated.rearrange("p a b -> p (a b)")[0:16, 0:640]
        dist_bias = Y.rearrange("p a b -> p (a b)")[0:16, 0:640]
        attention.close()

        xT = sb("x1T", [P, KT, SEQ])
        flat = sb("slots", [P, 8 * D])
        region2 = sb("region2", [P, 32000])
        ln1, o = carve(region2, 0, (2, D))
        info, o = carve(region2, o, (QT, N_EXP + 2, 3))
        pos, o = carve(region2, o, (QT, N_EXP + 2))
        w_r, o = carve(region2, o, (KT, N_EXP))
        assert o <= RING * SLOT, o
        w_gu0, o = carve(region2, RING * SLOT, (KT, 2 * F))
        w_dn0, o = carve(region2, o, (FT, D))
        ln2, o = carve(region2, o, (2, D))
        assert o >= RING * SLOT + KT * D, o
        w_gu1, o = carve(region2, o, (KT, 2 * F))
        w_dn1, o = carve(region2, o, (FT, D))
        w_gu, w_dn = (w_gu0, w_gu1), (w_dn0, w_dn1)
        x_nat, o = carve(region2, o, (QT, D))
        x1, o = carve(region2, o, (QT, D))
        onehot, o = carve(region2, o, (2, QT, P))
        top2, o = carve(region2, o, (N_GROUPS, 8))
        rt64, o = carve(region2, o, (4, N_EXP))
        score, o = carve(region2, o, (N_EXP,))
        choice, o = carve(region2, o, (N_EXP,))
        assert o <= 32000, o
        rows8, o = carve(region2, RING * SLOT + KT * D, (2, TOP_K, D))
        assert o <= 32000, o
        x_slots = flat[:, 0:2 * D].rearrange("p (a b) -> p a b", a=2)
        x_slotsT = flat[:, 2 * D:4 * D].rearrange("p (a k t) -> p a k t", a=2, k=KT)
        y_slots = flat[:, 4 * D:6 * D].rearrange("p (a b) -> p a b", a=2)
        h_slots = flat[:, 6 * D:6 * D + 512].rearrange("p (a b) -> p a b", a=2)
        hT = flat[:, 6 * D + 512:7 * D].rearrange("p (a k t) -> p a k t", a=2, k=FT)
        sig = flat[:, 7 * D:7 * D + 512].rearrange("p (a b) -> p a b", a=2)
        silu = flat[:, 7 * D + 512:8 * D].rearrange("p (a b) -> p a b", a=2)

        bias_d = nc.dram_tensor("bias_d", (12, P, 640), F32).ap()
        x1_d = nc.dram_tensor("x1_d", (SEQ, D), F32).ap()
        rows_d = nc.dram_tensor("rows_d", (SEQ * TOP_K, D), F32).ap()

        S_BANK, T_BANK, O_BANK, C_BANK = 0, 2, 4, 6
        G_BANK, X_BANK, H_BANK, I_BANK, Y_BANK = 0, 2, 4, 5, 6

        ring_in = [sem(f"ring_in{j}") for j in range(RING)]
        small_in = sem("small_in")
        xT_in = [sem(f"xT_in{j}") for j in range(X_PARTS)]
        w_f_in = sem("w_f_in")
        x_hi_made = sem("x_hi_made")
        x_lo_made = sem("x_lo_made")
        w_hi_made = sem("w_hi_made")
        w_lo_made = sem("w_lo_made")
        w_out_in = sem("w_out_in")
        bias_io = sem("bias_io")
        causal_in = sem("causal_in")
        strips_in = [sem(f"strips_in{g}") for g in range(3)]
        aug_in = sem("aug_in")
        consts_made = sem("consts_made")
        dve_chain = sem("dve_chain")
        act_chain = sem("act_chain")
        pool_chain = sem("pool_chain")
        bias_mm = sem("bias_mm")
        bias_made = sem("bias_made")
        forget_exp = sem("forget_exp")
        forget_made = sem("forget_made")
        lam_dots = sem("lam_dots")
        lam_exp = sem("lam_exp")
        proj_done = sem("proj_done")
        proj_out = sem("proj_out")
        scores_done = sem("scores_done")
        biased = sem("biased")
        probs_made = sem("probs_made")
        turned = sem("turned")
        turned_out = sem("turned_out")
        values_done = sem("values_done")
        y_made = sem("y_made")
        yc_stat = sem("yc_stat")
        yc_rms = sem("yc_rms")
        y_ready = sem("y_ready")
        gate_done = sem("gate_done")
        gate_exp = sem("gate_exp")
        branch_done = sem("branch_done")
        gated_made = sem("gated_made")
        merged = sem("merged")
        x_in = sem("x_in")
        late_in = sem("late_in")
        ln2_in = sem("ln2_in")
        mix_done = sem("mix_done")
        var_made = sem("var_made")
        rstd_made = sem("rstd_made")
        x1_made = sem("x1_made")
        x1_stored = sem("x1_stored")
        x1_turned = sem("x1_turned")
        x1T_made = sem("x1T_made")
        router_done = sem("router_done")
        router_exp = sem("router_exp")
        sel_made = sem("sel_made")
        scores_used = sem("scores_used")
        pos_done = sem("pos_done")
        info_made = sem("info_made")
        most_made = sem("most_made")
        sh_in = sem("sh_in")
        gu_in = [sem(f"gu_in{b}") for b in range(2)]
        dn_in = [sem(f"dn_in{b}") for b in range(2)]
        slots_in = [sem(f"slots_in{b}") for b in range(2)]
        slots_clear = sem("slots_clear")
        gathers_begun = sem("gathers_begun")
        scatters_begun = sem("scatters_begun")
        gu_a = sem("gu_a")
        gu_b = sem("gu_b")
        sig_a = sem("sig_a")
        sig_b = sem("sig_b")
        silu_made = sem("silu_made")
        h_a = sem("h_a")
        h_b = sem("h_b")
        h_turned_a = sem("h_turned_a")
        h_turned_b = sem("h_turned_b")
        hT_a = sem("hT_a")
        hT_b = sem("hT_b")
        y_done = sem("y_done")
        y_out0 = sem("y_out0")
        y_out1 = sem("y_out1")
        onehot_made = sem("onehot_made")
        slots_done = sem("slots_done")
        rows_made = sem("rows_made")
        slots_turned = sem("slots_turned")
        slotsT_made = sem("slotsT_made")
        rows_out = [sem(f"rows_out{b}") for b in range(2)]
        ov = {n: sem(f"ov_{n}") for n in ("w", "oh", "idx", "rows", "in", "tr", "xT", "gu", "sig", "silu", "h",
                                          "hturn", "hT", "y", "yout", "out", "turns")}
        rows8_in = [sem(f"rows8_in{b}") for b in range(2)]
        sums = sem("sums")
        out_made = sem("out_made")
        out_stored = sem("out_stored")

        def mT_nat(t):
            return mT[:, :, :].rearrange("p a b -> p (a b)")[:, t * D:(t + 1) * D]

        block = ctx.enter_context(nc.Block())

        SMALL = 7
        N_LATE = 4

        @block.sync
        def _(sp):
            def chunk(j):
                if j >= RING:
                    if j - RING < N_PROJ:
                        sp.wait_ge(w_lo_made, j - RING + 1)
                    else:
                        sp.wait_ge(branch_done, j - RING - N_PROJ + 1)
                src, n = (a["w_proj"][j], KT * P) if j < N_PROJ else (a["w_merge"][j - N_PROJ], 10 * P)
                sp.dma_start(ring[:, j % RING, 0:n], src).then_inc(ring_in[j % RING], 16)

            sp.dma_start(w_f[:], a["w_f"]).then_inc(w_f_in, 16)
            xT_parts = a["xT"].rearrange("(c p) n -> p c n", p=P)
            k = KT // X_PARTS
            for j in range(X_PARTS):
                sp.dma_start(mT[:, j * k:(j + 1) * k, :], xT_parts[:, j * k:(j + 1) * k, :]).then_inc(xT_in[j], 16)
                if j == 0:
                    chunk(0)
            sp.dma_start(b_f[:], a["b_forget"].rearrange("o h -> h o")).then_inc(small_in, 16)
            sp.dma_start(neg_oh, a["neg_onehot"]).then_inc(small_in, 16)
            sp.dma_start(dist_mask, a["dist_mask"]).then_inc(small_in, 16)
            sp.wait_ge(consts_made, 1)
            sp.dma_start(table[:, 0:12], a["t5_table"]).then_inc(small_in, 16)
            sp.dma_start(neg_sink[:], bass.AP(a["attn_sinks"].tensor, 0, [[0, P], [1, 4]])).then_inc(small_in, 16)
            sp.dma_start(lam_in[:, :, :], bass.AP(a["lam"].tensor, 0, [[0, P], [32, 4], [1, 32]]))\
                .then_inc(small_in, 16)
            sp.dma_start(norm_g[:], bass.AP(a["diff_norm_g"].tensor, 0, [[0, P], [1, HD]])).then_inc(small_in, 16)
            sp.dma_start(strips[:, 0, :], a["causal_strip"]).then_inc(causal_in, 16)
            for j in range(1, 6):
                chunk(j)
            sp.wait_ge(bias_made, 1)
            for g in range(3):
                sp.dma_start(bias_d[4 * g:4 * g + 4], dist_bias[4 * g:4 * g + 4, :].unsqueeze(1)
                             .broadcast_to([4, P, 640])).then_inc(bias_io, 16)
            sp.wait_ge(forget_made, 1)
            sp.dma_start(kA[64:65, :, :], fg[:, 2, :]).then_inc(aug_in, 16)
            sp.dma_start(qA[65:66, :, :], fg[:, 3, :]).then_inc(aug_in, 16)
            for j in range(6, 9):
                chunk(j)
            sp.wait_ge(bias_io, 48)
            for g in range(3):
                sp.dma_start(strips[:, 1 + 4 * g:5 + 4 * g, :],
                             bass.AP(bias_d.tensor, P - 1 + 4 * g * P * 640, [[639, P], [P * 640, 4], [1, SEQ]]))\
                    .then_inc(strips_in[g], 16)
                chunk(9 + g)
            for j in range(12, N_CHUNKS):
                chunk(j)
                if j == W_OUT_AFTER:
                    sp.wait_ge(scores_done, last_step[BR_C] + 1)
                    sp.dma_start(w_out, a["w_out"][0].rearrange("(k p) n -> p k n", p=P)).then_inc(w_out_in, 16)

            sp.wait_ge(branch_done, N_MERGE)
            sp.wait_ge(merged, N_MERGE)
            for t in range(QT):
                sp.dma_start(x_nat[:, t, :], a["x"][0, t * P:(t + 1) * P, :]).then_inc(x_in, 16)
            sp.dma_start(ln1[:, 0, :], bass.AP(a["ln1_g"].tensor, 0, [[0, P], [1, D]])).then_inc(late_in, 16)
            sp.dma_start(ln1[:, 1, :], bass.AP(a["ln1_b"].tensor, 0, [[0, P], [1, D]])).then_inc(late_in, 16)
            sp.dma_start(w_r[:], a["w_router"][0].rearrange("(p c) e -> p c e", c=KT)).then_inc(late_in, 16)
            sp.dma_start(r_bias[:], bass.AP(a["router_bias"].tensor, 0, [[0, P], [1, N_EXP]])).then_inc(late_in, 16)
            sp.dma_start(w_gu[1], a["w_gu_s"].rearrange("p (c n) -> p c n", c=KT)).then_inc(sh_in, 16)
            sp.dma_start(w_dn[1], a["w_down_s"][0].rearrange("(t p) n -> p t n", p=P)).then_inc(sh_in, 16)
            for t in range(QT):
                sp.wait_ge(x1_made, t + 1)
                sp.dma_start(x1_d[t * P:(t + 1) * P, :], x1[:, t, :]).then_inc(x1_stored, 16)
            sp.wait_ge(mix_done, QT)
            sp.dma_start(ln2[:, 0, :], bass.AP(a["ln2_g"].tensor, 0, [[0, P], [1, D]])).then_inc(ln2_in, 16)
            sp.dma_start(ln2[:, 1, :], bass.AP(a["ln2_b"].tensor, 0, [[0, P], [1, D]])).then_inc(ln2_in, 16)

            with sp.Fori(0, N_EXP // 4) as i:
                for b in range(4):
                    e = i * 4 + b
                    sp.wait_ge(gu_b, i * 4 + b + QT - 1)
                    sp.dma_start(w_gu[b % 2],
                                 a["w_gu"][bass.ds(e, 1)].rearrange("o p (c n) -> (o p) c n", c=KT))\
                        .then_inc(gu_in[b % 2], 16)
                    sp.wait_ge(y_done, i * 4 + b + QT - 1)
                    sp.dma_start(w_dn[b % 2],
                                 a["w_down_e"][0, bass.ds(e, 1)].rearrange("o (t p) n -> (o p) t n", p=P))\
                        .then_inc(dn_in[b % 2], 16)

            sp.wait_ge(most_made, 1)
            n = sp.value_load(most_i[0:1, 0:1], min_val=0, max_val=SEQ)
            with sp.If(n > P):
                sp.wait_ge(y_done, QT + N_EXP)
                with sp.Fori(1, SEQ // P) as c:
                    with sp.Fori(0, N_EXP) as e:
                        j = (c - 1) * N_EXP + e
                        sp.wait_ge(ov["y"], j + 1)
                        sp.dma_start(w_gu[0],
                                     a["w_gu"][bass.ds(e, 1)].rearrange("o p (c n) -> (o p) c n", c=KT))\
                            .then_inc(ov["w"], 16)
                        sp.dma_start(w_dn[0],
                                     a["w_down_e"][0, bass.ds(e, 1)].rearrange("o (t p) n -> (o p) t n", p=P))\
                            .then_inc(ov["w"], 16)
                sp.wait_ge(ov["out"], 16 * (SEQ // P - 1) * N_EXP)

            sp.wait_ge(y_done, QT + N_EXP)
            for b in range(2):
                sp.wait_ge(rows_out[b], 16 * (N_EXP // 2 + 1))
            for t in range(QT):
                if t >= 2:
                    sp.wait_ge(sums, t - 1)
                sp.dma_start(rows8[:, t % 2, :, :],
                             rows_d[t * P * TOP_K:(t + 1) * P * TOP_K, :].rearrange("(p r) d -> p r d", r=TOP_K))\
                    .then_inc(rows8_in[t % 2], 16)
            for t in range(QT):
                sp.wait_ge(out_made, t + 1)
                sp.dma_start(out[0, t * P:(t + 1) * P, :], mT_nat(t)).then_inc(out_stored, 16)
            sp.wait_ge(out_stored, 16 * QT)
            sp.wait_ge(x1_stored, 16 * QT)

        @block.tensor
        def _(pe):
            def qk_of(s):
                br, h, c, qt = STEPS[s]
                k0, nk = keys_of(br, qt)
                q, k = {BR_A: (qA, kA), BR_B: (qB, kB), BR_C: (qC, kC), BR_D: (qD, kD)}[br]
                if br == BR_A:
                    base, n, jq, jk = 0, 66, h, h
                elif br == BR_B:
                    base, n, jq, jk = 64 * (h // 2), 64, h % 2, 0
                elif br == BR_C:
                    base, n, jq, jk = 64 * (h % 2) + 32 * c, 32, h // 2, h // 2
                else:
                    base, n, jq, jk = 64 * (h % 2), 64, h // 2, h // 2
                return (q[base:base + n, jq, qt * P:(qt + 1) * P], k[base:base + n, jk, k0 * P:(k0 + nk) * P])

            def v_of(s, kt):
                br, h, _, _ = STEPS[s]
                if br == BR_B:
                    return V[:, kt, V_AT[br, 0], HD * (h // 2):HD * (h // 2) + HD]
                return V[:, kt, V_AT[br, h // 2], HD * (h % 2):HD * (h % 2) + HD]

            pe.wait_ge(w_f_in, 16)
            for c in range(KT):
                if c % (KT // X_PARTS) == 0:
                    pe.wait_ge(xT_in[c // (KT // X_PARTS)], 16)
                mm = nc.tensor.matmul(PS[0:4, C_BANK, :], w_f[:, c, :], mT[:, c, :], start=(c == 0), stop=(c == KT - 1))
            mm.then_inc(proj_done, 1)

            def distance_bias():
                pe.wait_ge(consts_made, 2)
                pe.wait_ge(small_in, 16 * SMALL)
                nc.tensor.matmul(PS[0:16, S_BANK, 0:512], table[:, :], neg_oh[:, 0:512], start=True, stop=True)
                nc.tensor.matmul(PS[0:16, S_BANK + 1, 0:128], table[:, :], neg_oh[:, 512:640], start=True, stop=True)\
                    .then_inc(bias_mm, 1)

            def x_product_part(bank, n, i):
                if i == 0:
                    pe.wait_ge(w_hi_made, n + 1)
                if i == 2:
                    pe.wait_ge(w_lo_made, n + 1)
                for c in range(KT):
                    if n == 0:
                        (pe.wait_ge(x_hi_made, c + 1) if i == 0 else pe.wait_ge(x_lo_made, c + 1))
                    mm = nc.tensor.matmul(PS[:, bank, :], (w_hi, w_hi, w_lo)[i][:, n % HALVES, c, :],
                                          (x_hi, x_lo, x_hi)[i][:, c, :], start=(i == 0 and c == 0),
                                          stop=(i == 2 and c == KT - 1))
                return mm

            def x_product(bank, n):
                for i in range(3):
                    mm = x_product_part(bank, n, i)
                return mm

            def x_product_tokens(bank, n):
                wh, wl = w_hi[:, n % HALVES, :, :], w_lo[:, n % HALVES, :, :]
                pe.wait_ge(w_hi_made, n + 1)
                pe.wait_ge(w_lo_made, n + 1)
                for t in range(QT):
                    to, tok = PS[:, bank, t * P:(t + 1) * P], slice(t * P, (t + 1) * P)
                    for c in range(KT):
                        nc.tensor.matmul(to, x_hi[:, c, tok], wh[:, c, :], start=(c == 0), stop=False)
                        nc.tensor.matmul(to, x_hi[:, c, tok], wl[:, c, :], start=False, stop=False)
                        mm = nc.tensor.matmul(to, x_lo[:, c, tok], wh[:, c, :], start=False, stop=(c == KT - 1))
                return mm

            for kind, n in order:
                if kind == "proj":
                    u = at_proj[n]
                    bank = C_BANK + u % 2
                    if u >= 2:
                        pe.wait_ge(proj_out, u - 1)
                    (x_product_tokens if PROJ[n][0] == "v" else x_product)(bank, n).then_inc(proj_done, 1)
                    if n == 0:
                        distance_bias()
                elif kind == "scores":
                    br, h, _, qt = STEPS[n]
                    if qt == 0:
                        need = max(at_proj[m] for m, x in enumerate(PROJ) if x[1] == br and x[0] in "qk")
                        pe.wait_ge(proj_out, need + 1)
                        if br == BR_A:
                            pe.wait_ge(aug_in, 32)
                    if n < 2:
                        pe.wait_ge(bias_made, 1)
                    else:
                        pe.wait_ge(biased, n - 1)
                    q, k = qk_of(n)
                    nk = keys_of(br, qt)[1]
                    nc.tensor.matmul(PS[:, S_BANK + n % 2, 0:nk * P], q, k, start=True, stop=True)\
                        .then_inc(scores_done, 1)
                elif kind == "turn":
                    u = turn_at[kind, n]
                    br, _, _, qt = STEPS[n]
                    pe.wait_ge(probs_made, n + 1)
                    if u >= 2:
                        pe.wait_ge(turned_out, u - 1)
                    for j in range(keys_of(br, qt)[1]):
                        mm = nc.tensor.transpose(PS[:, T_BANK + u % 2, j * P:(j + 1) * P],
                                                 probs[:, n % 3, j * P:(j + 1) * P], ident[:, :])
                    mm.then_inc(turned, 1)
                elif kind == "values":
                    br, _, _, qt = STEPS[n]
                    k0, nk = keys_of(br, qt)
                    pe.wait_ge(turned_out, turn_at["turn", n] + 1)
                    need = max(at_proj[m] for m, x in enumerate(PROJ) if x[1] == br and x[0] == "v")
                    pe.wait_ge(proj_out, need + 1)
                    if n >= 2:
                        pe.wait_ge(y_made, n - 1)
                    for j in range(nk):
                        mm = nc.tensor.matmul(PS[:, O_BANK + n % 2, 0:HD], probsT[:, n % 3, j * P:(j + 1) * P],
                                              v_of(n, k0 + j), start=(j == 0), stop=(j == nk - 1))
                    mm.then_inc(values_done, 1)
                elif kind == "turn_y":
                    u = turn_at[kind, n]
                    br, j = n // 2, n % 2
                    pe.wait_ge(y_ready, br + 1)
                    pe.wait_ge(turned_out, u - 1)
                    for t in range(QT):
                        mm = nc.tensor.transpose(PS[:, T_BANK + u % 2, t * P:(t + 1) * P],
                                                 Y[:, (br % 2) * QT + t, j * P:(j + 1) * P], ident[:, :])
                    mm.then_inc(turned, 1)
                elif kind == "part":
                    m, i = divmod(n, 3)
                    if i == 0:
                        if m == 0:
                            pe.wait_ge(proj_out, N_PROJ + 1)
                        else:
                            pe.wait_ge(gate_exp, m)
                    mm = x_product_part(C_BANK, N_PROJ + m, i)
                    if i == 2:
                        mm.then_inc(gate_done, 1)
                elif kind == "branch":
                    j, br = N_PROJ + n, n // KT
                    w = ring[:, j % RING, :].rearrange("p (c n) -> p c n", c=10)
                    pe.wait_ge(turned_out, turn_at["turn_y", 2 * br + 1] + 1)
                    if n >= 1:
                        pe.wait_ge(gated_made, n)
                    for c in range(2):
                        mm = nc.tensor.matmul(PS[:, C_BANK + 1, :], w[:, KT + c, :], yT[:, (br % 2) * 2 + c, :],
                                              start=(c == 0), stop=(c == 1))
                    mm.then_inc(branch_done, 1)

            def mix(t):
                if t == 0:
                    pe.wait_ge(w_out_in, 16)
                    pe.wait_ge(merged, N_MERGE - 1)
                    pe.wait_ge(biased, n_steps)
                    pe.wait_ge(y_made, n_steps)
                if t >= 2:
                    pe.wait_ge(var_made, t - 1)
                bank = S_BANK if t % 2 == 0 else O_BANK
                for k in range(KT):
                    if t == 0 and k == KT - 1:
                        pe.wait_ge(merged, N_MERGE)
                    for half in range(2):
                        mm = nc.tensor.matmul(PS[:, bank + half, :], mT[:, k, t * P:(t + 1) * P],
                                              w_out[:, k, half * 512:half * 512 + 512],
                                              start=(k == 0), stop=(k == KT - 1))
                mm.then_inc(mix_done, 1)

            def turn_x1(t):
                pe.wait_ge(x1_made, t + 1)
                if t == 0:
                    pe.wait_ge(turned_out, len(turns))
                else:
                    pe.wait_ge(x1T_made, t)
                xs = x1[:, t, :].rearrange("p (q c) -> p c q", c=KT)
                for c in range(KT):
                    mm = nc.tensor.transpose(PS[:, X_BANK + c // 4, (c % 4) * P:(c % 4 + 1) * P], xs[:, c, :],
                                             ident[:, :])
                mm.then_inc(x1_turned, 1)

            def router(t):
                pe.wait_ge(x1T_made, t + 1)
                if t == 0:
                    pe.wait_ge(late_in, 16 * N_LATE)
                    pe.wait_ge(gate_exp, N_MERGE)
                else:
                    pe.wait_ge(router_exp, t)
                for c in range(KT):
                    mm = nc.tensor.matmul(PS[:, C_BANK, 0:N_EXP], xT[:, c, t * P:(t + 1) * P], w_r[:, c, :],
                                          start=(c == 0), stop=(c == KT - 1))
                mm.then_inc(router_done, 1)

            def positions(t):
                pe.wait_ge(sel_made, min(t + 1, QT))
                if t == 0:
                    pe.wait_ge(gated_made, N_MERGE)
                else:
                    pe.wait_ge(info_made, t)
                for u in range(min(t + 1, QT)):
                    mm = nc.tensor.matmul(PS[:, C_BANK + 1, 0:N_EXP], (before if u == t else ones)[:, :], sel[:, u, :],
                                          start=(u == 0), stop=(u == min(t, QT - 1)))
                mm.then_inc(pos_done, 1)

            def gate_up(xs, w, half, done):
                for c in range(KT):
                    mm = nc.tensor.matmul(PS[:, G_BANK + half, 0:F], xs(c), w[:, c, half * F:(half + 1) * F],
                                          start=(c == 0), stop=(c == KT - 1))
                mm.then_inc(done, 1)

            def turn_h(b, half, done):
                nc.tensor.transpose(PS[:, H_BANK, 0:P], h_slots[:, b, half * P:(half + 1) * P], ident[:, :])\
                    .then_inc(done, 1)

            def down(b, wb, half):
                for n in range(2):
                    mm = nc.tensor.matmul(PS[:, Y_BANK + n, :], hT[:, b, half, :],
                                          w_dn[wb][:, half, n * 512:(n + 1) * 512], start=(half == 0), stop=(half == 1))
                return mm

            def shared(t):
                if t == 0:
                    pe.wait_ge(sh_in, 32)
                    pe.wait_ge(var_made, QT)
                else:
                    pe.wait_ge(h_a, t)
                    pe.wait_ge(h_b, t)
                for half, done in ((0, gu_a), (1, gu_b)):
                    gate_up(lambda c: xT[:, c, t * P:(t + 1) * P], w_gu[1], half, done)
                pe.wait_ge(h_a, t + 1)
                turn_h(t % 2, 0, h_turned_a)
                pe.wait_ge(hT_a, t + 1)
                if t == 0:
                    pe.wait_ge(router_exp, QT)
                    pe.wait_ge(most_made, 1)
                else:
                    pe.wait_ge(y_out1, 2 * t)
                down(t % 2, 1, 0)
                pe.wait_ge(h_b, t + 1)
                turn_h(t % 2, 1, h_turned_b)
                pe.wait_ge(hT_b, t + 1)
                down(t % 2, 1, 1).then_inc(y_done, 1)

            mix(0)
            mix(1)
            for t in range(QT):
                turn_x1(t)
                router(t)
                if t + 2 < QT:
                    mix(t + 2)
                if t >= 1:
                    positions(t - 1)
            positions(QT - 1)
            positions(QT)
            for t in range(QT):
                shared(t)

            def slots(j, b):
                pe.wait_ge(onehot_made, j + 1)
                pe.wait_ge(rows_made, j)
                for t in range(QT):
                    mm = nc.tensor.matmul(PS[:, I_BANK, 0:3], onehot[:, b % 2, t, :],
                                          info[:, t, bass.ds(j, 1), :].rearrange("p a b -> p (a b)"),
                                          start=(t == 0), stop=(t == QT - 1))
                mm.then_inc(slots_done, 1)

            def turn_slots(j, b, wait):
                wait()
                pe.wait_ge(slotsT_made, j)
                xs = x_slots[:, b % 2, :].rearrange("p (q c) -> p c q", c=KT)
                for c in range(KT):
                    mm = nc.tensor.transpose(PS[:, X_BANK + c // 4, (c % 4) * P:(c % 4 + 1) * P], xs[:, c, :],
                                             ident[:, :])
                mm.then_inc(slots_turned, 1)

            slots(0, 0)
            slots(1, 1)
            turn_slots(0, 0, lambda: pe.wait_ge(slots_in[0], 16))
            with pe.Fori(0, N_EXP // 4) as i:
                for b in range(4):
                    e = i * 4 + b
                    pe.wait_ge(slotsT_made, e + 1)
                    pe.wait_ge(gu_in[b % 2], i * 32 + 16 * (b // 2 + 1))
                    pe.wait_ge(h_a, e + QT)
                    xs = lambda c, b=b: x_slotsT[:, b % 2, c, :]
                    gate_up(xs, w_gu[b % 2], 0, gu_a)
                    pe.wait_ge(h_b, e + QT)
                    gate_up(xs, w_gu[b % 2], 1, gu_b)
                    pe.wait_ge(h_a, e + QT + 1)
                    turn_h(b % 2, 0, h_turned_a)
                    turn_slots(e + 1, b + 1,
                               lambda: pe.wait_ge(slots_in[(b + 1) % 2], i * 32 + 16 * ((b + 1) // 2 + 1)))
                    pe.wait_ge(hT_a, e + QT + 1)
                    pe.wait_ge(dn_in[b % 2], i * 32 + 16 * (b // 2 + 1))
                    pe.wait_ge(y_out0, e + 1)
                    pe.wait_ge(y_out1, e + 2 * QT)
                    down(b % 2, b % 2, 0)
                    pe.wait_ge(h_b, e + QT + 1)
                    turn_h(b % 2, 1, h_turned_b)
                    slots(e + 2, b)
                    pe.wait_ge(hT_b, e + QT + 1)
                    down(b % 2, b % 2, 1).then_inc(y_done, 1)

            n = pe.value_load(most_i[0:1, 0:1], min_val=0, max_val=SEQ)
            with pe.If(n > P):
                pe.sem_inc(ov["y"], 1)
                with pe.Fori(1, SEQ // P) as c:
                    with pe.Fori(0, N_EXP) as e:
                        j = (c - 1) * N_EXP + e
                        pe.wait_ge(ov["oh"], j + 1)
                        for t in range(QT):
                            mm = nc.tensor.matmul(PS[:, I_BANK, 0:3], onehot[:, 0, t, :],
                                                  info[:, t, bass.ds(e, 1), :].rearrange("p a b -> p (a b)"),
                                                  start=(t == 0), stop=(t == QT - 1))
                        mm.then_inc(ov["idx"], 1)
                        pe.wait_ge(ov["in"], j * 16 + 16)
                        xs = x_slots[:, 0, :].rearrange("p (q c) -> p c q", c=KT)
                        for k in range(KT):
                            mm = nc.tensor.transpose(PS[:, X_BANK + k // 4, (k % 4) * P:(k % 4 + 1) * P], xs[:, k, :],
                                                     ident[:, :])
                        mm.then_inc(ov["tr"], 1)
                        pe.wait_ge(ov["xT"], j + 1)
                        pe.wait_ge(ov["w"], j * 32 + 32)
                        for half in range(2):
                            gate_up(lambda k: x_slotsT[:, 0, k, :], w_gu[0], half, ov["gu"])
                        for half in range(2):
                            pe.wait_ge(ov["h"], j * 2 + half + 1)
                            if half == 1:
                                pe.wait_ge(ov["hT"], j * 2 + 1)
                            turn_h(0, half, ov["hturn"])
                        pe.wait_ge(ov["hT"], j * 2 + 2)
                        for half in range(2):
                            mm = down(0, 0, half)
                        mm.then_inc(ov["y"], 1)

        @block.scalar
        def _(act):
            chain = [0]

            def link(ins):
                chain[0] += 1
                ins.then_inc(act_chain, 1)
                act.wait_ge(act_chain, chain[0])

            def split(n):
                if n < N_CHUNKS:
                    act.wait_ge(ring_in[n % RING], 16 * (n // RING + 1))
                    nc.scalar.activation(w_hi[:, n % HALVES, :, :],
                                         ring[:, n % RING, 0:KT * P].rearrange("p (c n) -> p c n", c=KT), ACT.Copy)\
                        .then_inc(w_hi_made, 1)

            for c in range(KT):
                act.wait_ge(xT_in[c // (KT // X_PARTS)], 16)
                nc.scalar.activation(x_hi[:, c, :], mT[:, c, :], ACT.Copy).then_inc(x_hi_made, 1)
                if c == 3:
                    split(0)
            split(1)
            act.wait_ge(forget_exp, 1)
            link(nc.scalar.activation(fg[:, 1, :], fg[:, 1, :], ACT.Exp))
            nc.scalar.activation(fg[:, 1, :], fg[:, 1, :], ACT.Ln, bias=1.0).then_inc(forget_exp, 1)
            act.wait_ge(lam_dots, 1)
            nc.scalar.activation(lam_s[:, 2:4], lam_s[:, 0:2], ACT.Exp).then_inc(lam_exp, 1)

            for kind, n in order:
                if kind == "proj":
                    u = at_proj[n]
                    what, br, j = PROJ[n]
                    bank = PS[:, C_BANK + u % 2, :]
                    act.wait_ge(proj_done, u + 1)
                    scale = -(32 if br == BR_C else HD) ** -0.5 if what == "q" else 1.0
                    if what == "v":
                        nc.scalar.activation(V[:, :, V_AT[br, j], :], bank.rearrange("p (t n) -> p t n", t=QT),
                                             ACT.Copy).then_inc(proj_out, 1)
                    elif br == BR_A:
                        dst = qA if what == "q" else kA
                        nc.scalar.activation(dst[0:HD, 2 * j, :], bank[0:HD, :], ACT.Copy, scale=scale)
                        nc.scalar.activation(dst[0:HD, 2 * j + 1, :], bank[HD:P, :], ACT.Copy, scale=scale)\
                            .then_inc(proj_out, 1)
                    else:
                        dst = {("q", BR_B): qB, ("k", BR_B): kB, ("q", BR_C): qC, ("k", BR_C): kC,
                               ("q", BR_D): qD, ("k", BR_D): kD}[what, br]
                        nc.scalar.activation(dst[:, j, :], bank, ACT.Copy, scale=scale).then_inc(proj_out, 1)
                    split(n + HALVES)
                elif kind == "scores":
                    br, h, _, qt = STEPS[n]
                    nk = keys_of(br, qt)[1] * P + (br == BR_B)
                    act.wait_ge(biased, n + 1)
                    nc.scalar.activation(probs[:, n % 3, 0:nk], probs[:, n % 3, 0:nk], ACT.Exp,
                                         bias=nmax[:, n:n + 1], scale=-1.0, accum_out=den[:, n:n + 1])\
                        .then_inc(probs_made, 1)
                elif kind == "turn":
                    u = turn_at[kind, n]
                    nk = keys_of(STEPS[n][0], STEPS[n][3])[1] * P
                    act.wait_ge(turned, u + 1)
                    if n >= 3:
                        act.wait_ge(values_done, n - 2)
                    nc.scalar.activation(probsT[:, n % 3, 0:nk], PS[:, T_BANK + u % 2, 0:nk], ACT.Copy)\
                        .then_inc(turned_out, 1)
                elif kind == "turn_y":
                    u = turn_at[kind, n]
                    br, j = n // 2, n % 2
                    act.wait_ge(turned, u + 1)
                    if br >= 2:
                        act.wait_ge(branch_done, (br - 1) * KT)
                    nc.scalar.activation(yT[:, (br % 2) * 2 + j, :], PS[:, T_BANK + u % 2, :], ACT.Copy)\
                        .then_inc(turned_out, 1)
                elif kind == "gate":
                    act.wait_ge(gate_done, n + 1)
                    if n >= 2:
                        act.wait_ge(gated_made, n - 1)
                    nc.scalar.activation(gate[:, n % 2, :], PS[:, C_BANK, :], ACT.Exp, scale=-1.0)\
                        .then_inc(gate_exp, 1)
                    split(N_PROJ + n + HALVES)

            def x1T_copy(t):
                act.wait_ge(x1_turned, t + 1)
                for h in range(2):
                    ins = nc.scalar.activation(xT[:, 4 * h:4 * h + 4, t * P:(t + 1) * P],
                                               PS[:, X_BANK + h, :].rearrange("p (c n) -> p c n", c=4), ACT.Copy)
                ins.then_inc(x1T_made, 1)

            def router_exponential(t):
                act.wait_ge(router_done, t + 1)
                if t >= 1:
                    act.wait_ge(scores_used, t)
                nc.scalar.activation(score[:, :], PS[:, C_BANK, 0:N_EXP], ACT.Exp, scale=-1.0).then_inc(router_exp, 1)

            for t in range(QT):
                x1T_copy(t)
                router_exponential(t)

            def sigmoid(half, done):
                nc.scalar.activation(sig[:, half, 0:P], PS[:, G_BANK + half, 0:P], ACT.Sigmoid).then_inc(done, 1)

            def hT_copy(b, half, done):
                nc.scalar.activation(hT[:, b, half, :], PS[:, H_BANK, 0:P], ACT.Copy).then_inc(done, 1)

            for t in range(QT):
                for half, ready, done, made in ((0, gu_a, sig_a, h_a), (1, gu_b, sig_b, h_b)):
                    act.wait_ge(ready, t + 1)
                    if t >= 1:
                        act.wait_ge(made, t)
                    sigmoid(half, done)
                act.wait_ge(h_turned_a, t + 1)
                if t >= 2:
                    act.wait_ge(y_done, t - 1)
                hT_copy(t % 2, 0, hT_a)
                act.wait_ge(h_turned_b, t + 1)
                hT_copy(t % 2, 1, hT_b)

            def slotsT_copy(j, b):
                act.wait_ge(slots_turned, j + 1)
                for h in range(2):
                    ins = nc.scalar.activation(x_slotsT[:, b % 2, 4 * h:4 * h + 4, :],
                                               PS[:, X_BANK + h, :].rearrange("p (c n) -> p c n", c=4), ACT.Copy)
                ins.then_inc(slotsT_made, 1)

            slotsT_copy(0, 0)
            act.sem_inc(y_out0, 1)
            with act.Fori(0, N_EXP // 4) as i:
                for b in range(4):
                    e = i * 4 + b
                    for half, ready, done, made in ((0, gu_a, sig_a, h_a), (1, gu_b, sig_b, h_b)):
                        act.wait_ge(ready, e + QT + 1)
                        act.wait_ge(made, e + QT)
                        sigmoid(half, done)
                    act.wait_ge(h_turned_a, e + QT + 1)
                    act.wait_ge(y_done, e + QT - 1)
                    hT_copy(b % 2, 0, hT_a)
                    slotsT_copy(e + 1, b + 1)
                    act.wait_ge(h_turned_b, e + QT + 1)
                    hT_copy(b % 2, 1, hT_b)
                    act.wait_ge(y_done, e + QT + 1)
                    act.wait_ge(rows_out[b % 2], i * 32 + 16 * (b // 2 + 1))
                    nc.scalar.activation(y_slots[:, b % 2, 0:512], PS[:, Y_BANK, :], ACT.Copy,
                                         scale=w_slot[:, b, :]).then_inc(y_out0, 1)

            n = act.value_load(most_i[0:1, 0:1], min_val=0, max_val=SEQ)
            with act.If(n > P):
                with act.Fori(1, SEQ // P) as c:
                    with act.Fori(0, N_EXP) as e:
                        j = (c - 1) * N_EXP + e
                        act.wait_ge(ov["tr"], j + 1)
                        for h in range(2):
                            ins = nc.scalar.activation(x_slotsT[:, 0, 4 * h:4 * h + 4, :],
                                                       PS[:, X_BANK + h, :].rearrange("p (c n) -> p c n", c=4),
                                                       ACT.Copy)
                        ins.then_inc(ov["xT"], 1)
                        for half in range(2):
                            act.wait_ge(ov["gu"], j * 2 + half + 1)
                            sigmoid(half, ov["sig"])
                        for half in range(2):
                            act.wait_ge(ov["hturn"], j * 2 + half + 1)
                            hT_copy(0, half, ov["hT"])

        @block.vector
        def _(dve):
            chain = [0]

            def link(ins):
                chain[0] += 1
                ins.then_inc(dve_chain, 1)
                dve.wait_ge(dve_chain, chain[0])

            nc.vector.memset(table[:, :], 0.0).then_inc(consts_made, 1)
            link(nc.vector.memset(qA[64:66, :, :], 1.0))
            link(nc.vector.memset(kA[64:66, :, :], 1.0))
            for c in range(KT):
                dve.wait_ge(x_hi_made, c + 1)
                nc.vector.tensor_tensor(x_lo[:, c, :], mT[:, c, :], x_hi[:, c, :].bitcast(F32), ALU.subtract)\
                    .then_inc(x_lo_made, 1)
            dve.wait_ge(small_in, 16 * SMALL)
            dve.wait_ge(bias_mm, 1)
            link(nc.vector.tensor_tensor(dist_bias[:, 0:512], PS[0:16, S_BANK, 0:512], dist_mask[:, 0:512], ALU.add))
            nc.vector.tensor_tensor(dist_bias[:, 512:640], PS[0:16, S_BANK + 1, 0:128], dist_mask[:, 512:640], ALU.add)\
                .then_inc(bias_made, 1)
            dve.wait_ge(proj_done, 1)
            link(nc.vector.tensor_scalar(fg[:, 0, :], PS[0:4, C_BANK, :], b_f[:, 0:1], None, ALU.add))
            proj_out_first = nc.vector.tensor_scalar(fg[:, 2, :], fg[:, 0, :], -1.0, None, ALU.mult)
            link(proj_out_first)
            link(nc.vector.tensor_tensor(fg[:, 1, :], fg[:, 0, :], fg[:, 2, :], ALU.min))
            link(nc.vector.tensor_scalar(fg[:, 0, :], fg[:, 0, :], 0.0, None, ALU.min))
            dve.sem_inc(proj_out, 1)
            dve.sem_inc(forget_exp, 1)
            for m in range(2):
                link(nc.vector.tensor_tensor_reduce(lam_mul[:, m, :], lam_in[:, 2 * m, :], lam_in[:, 2 * m + 1, :],
                                                    1.0, 0.0, ALU.mult, ALU.add, lam_s[:, m:m + 1]))
            dve.sem_inc(lam_dots, 1)
            link(nc.vector.tensor_scalar(neg_sink[:, :], neg_sink[:, :], -1.0, None, ALU.mult))
            dve.wait_ge(forget_exp, 2)
            link(nc.vector.tensor_tensor(fg[:, 0, :], fg[:, 0, :], fg[:, 1, :], ALU.subtract))
            link(nc.vector.tensor_tensor_scan(fg[:, 2, :], fg[:, 0, :], fg[:, 0, :], 0.0, ALU.add, ALU.bypass))
            link(nc.vector.tensor_scalar(fg[:, 3, :], fg[:, 2, :], -1.0, None, ALU.mult))
            dve.sem_inc(forget_made, 1)
            dve.wait_ge(lam_exp, 1)
            link(nc.vector.tensor_tensor(lam_s[:, 4:5], lam_s[:, 3:4], lam_s[:, 2:3], ALU.subtract))
            link(nc.vector.tensor_scalar(lam_s[:, 5:6], lam_s[:, 4:5], -LAM_INIT, None, ALU.add))

            def turn_wait(s):
                dve.wait_ge(turned, turn_at["turn", s] + 1)

            def bias_step(s):
                br, h, c, qt = STEPS[s]
                nk = keys_of(br, qt)[1] * P
                row = {BR_A: 0, BR_B: 1 + h, BR_C: 5 + h, BR_D: 9 + h}[br]
                if (h, c, qt) == (0, 0, 0):
                    if br == BR_A:
                        dve.wait_ge(causal_in, 16)
                    else:
                        dve.wait_ge(strips_in[br - 1], 16)
                dve.wait_ge(scores_done, s + 1)
                if s >= 3:
                    turn_wait(s - 3)
                if br == BR_B:
                    nc.vector.tensor_copy(probs[:, s % 3, nk:nk + 1], neg_sink[:, h:h + 1])
                start = neg_sink[:, h:h + 1] if br == BR_B else 3e38
                lo = SEQ - nk
                nc.vector.tensor_tensor_reduce(probs[:, s % 3, 0:nk], PS[:, S_BANK + s % 2, 0:nk], strips[:, row, lo:SEQ],
                                               1.0, start, ALU.add, ALU.min, nmax[:, s:s + 1]).then_inc(biased, 1)

            def out_step(s):
                br, h, c, qt = STEPS[s]
                dve.wait_ge(values_done, s + 1)
                link(nc.vector.reciprocal(rden[:, s:s + 1], den[:, s:s + 1]))
                dst = Y[:, (br % 2) * QT + qt, h * HD:(h + 1) * HD]
                src = PS[:, O_BANK + s % 2, 0:HD]
                if br >= 2 and s == last_step[br - 1] + 1:
                    dve.wait_ge(turned, turn_at["turn_y", 2 * (br - 2) + 1] + 1)
                if br == BR_C and c == 1:
                    link(nc.vector.tensor_scalar(rden[:, s:s + 1], rden[:, s:s + 1], lam_s[:, 5:6], None, ALU.mult))
                    dve.wait_ge(y_made, s - QT + 1)
                    nc.vector.scalar_tensor_tensor(dst, src, rden[:, s:s + 1], dst, ALU.mult, ALU.add)\
                        .then_inc(y_made, 1)
                else:
                    nc.vector.tensor_scalar(dst, src, rden[:, s:s + 1], None, ALU.mult).then_inc(y_made, 1)
                if s == last_step[br]:
                    dve.wait_ge(y_made, s + 1)
                    if br == BR_C:
                        for t in range(QT):
                            yt = Y[:, (br % 2) * QT + t, :]
                            link(nc.vector.tensor_tensor(yc_sq[:, :], yt, yt, ALU.mult))
                            link(nc.vector.tensor_reduce(yc_ss[:, 4 * t:4 * t + 4],
                                                         yc_sq[:, :].rearrange("p (h d) -> p h d", h=4), AX.X, ALU.add))
                        link(nc.vector.tensor_scalar(yc_ss[:, :], yc_ss[:, :], 1.0 / HD, EPS, ALU.mult, ALU.add))
                        dve.sem_inc(yc_stat, 1)
                    else:
                        dve.sem_inc(y_ready, 1)

            def norm_c():
                dve.wait_ge(yc_rms, 1)
                for t in range(QT):
                    for h in range(4):
                        yt = Y[:, (BR_C % 2) * QT + t, h * HD:(h + 1) * HD]
                        ins = nc.vector.scalar_tensor_tensor(yt, yt, yc_ss[:, 4 * t + h:4 * t + h + 1], norm_g[:, :],
                                                             ALU.mult, ALU.mult)
                        if t == QT - 1 and h == 3:
                            link(ins)
                for t in range(QT):
                    yt = Y[:, (BR_C % 2) * QT + t, :]
                    ins = nc.vector.tensor_scalar(yt, yt, 1.0 - LAM_INIT, None, ALU.mult)
                    link(ins)
                dve.sem_inc(y_ready, 1)

            for kind, n in order:
                if kind == "scores":
                    bias_step(n)
                    if n == norm_step:
                        norm_c()
                elif kind == "values":
                    out_step(n)
                elif kind == "gate":
                    dve.wait_ge(gate_exp, n + 1)
                    g = gate[:, n % 2, :]
                    link(nc.vector.tensor_scalar(g, g, 1.0, None, ALU.add))
                elif kind == "gated":
                    g = gate[:, n % 2, :]
                    link(nc.vector.reciprocal(g, g))
                    dve.wait_ge(branch_done, n + 1)
                    if n < KT:
                        dst = mT[:, n, :]
                    else:
                        dst = gated[:, n % 2, :]
                        if n >= KT + 2:
                            dve.wait_ge(merged, n - 1)
                    nc.vector.tensor_tensor(dst, PS[:, C_BANK + 1, :], gate[:, n % 2, :], ALU.mult)\
                        .then_inc(gated_made, 1)

            def norm(v, k):
                for h in range(2):
                    ins = nc.vector.bn_stats(stats[:, h, :], v[:, h * 512:(h + 1) * 512])
                link(ins)
                link(nc.vector.bn_aggr(mv[:, 0:2], stats[:, :, :].rearrange("p a b -> p (a b)")))
                link(nc.vector.tensor_scalar(mv[:, 1:2], mv[:, 1:2], EPS, None, ALU.add))
                dve.sem_inc(var_made, 1)
                dve.wait_ge(rstd_made, k + 1)
                link(nc.vector.tensor_scalar(v, v, mv[:, 0:1], mv[:, 1:2], ALU.subtract, ALU.mult))

            def first_norm(t):
                bank = S_BANK if t % 2 == 0 else O_BANK
                dve.wait_ge(mix_done, t + 1)
                dve.wait_ge(x_in, 16 * QT)
                v = x1[:, t, :]
                link(nc.vector.scalar_tensor_tensor(v, x_nat[:, t, :], ALPHA,
                                                    PS[:, bank:bank + 2, :].rearrange("p a b -> p (a b)"),
                                                    ALU.mult, ALU.add))
                norm(v, t)
                if t == 0:
                    dve.wait_ge(late_in, 16 * N_LATE)
                link(nc.vector.tensor_tensor(v, v, ln1[:, 0, :], ALU.mult))
                nc.vector.tensor_tensor(v, v, ln1[:, 1, :], ALU.add).then_inc(x1_made, 1)

            def pick(values, eighth, n, k, dst):
                more, same, upto = (rt8[:, 0, :], rt8[:, 1, :], rt8[:, 2, :]) if n == 8 else \
                    (rt64[:, 0, :], rt64[:, 1, :], rt64[:, 2, :])
                left = wsum[:, 4:5]
                link(nc.vector.tensor_scalar(more, values, eighth, None, ALU.is_gt))
                link(nc.vector.tensor_reduce(left, more, AX.X, ALU.add))
                link(nc.vector.tensor_scalar(left, left, -1.0, float(k), ALU.mult, ALU.add))
                link(nc.vector.tensor_scalar(same, values, eighth, None, ALU.is_equal))
                link(nc.vector.tensor_tensor_scan(upto, same, same, 0.0, ALU.add, ALU.bypass))
                link(nc.vector.scalar_tensor_tensor(same, upto, left, same, ALU.is_le, ALU.mult))
                link(nc.vector.tensor_tensor(dst, more, same, ALU.add))

            def route(t):
                dve.wait_ge(router_exp, t + 1)
                link(nc.vector.tensor_scalar(score[:, :], score[:, :], 1.0, None, ALU.add))
                link(nc.vector.reciprocal(score[:, :], score[:, :]))
                link(nc.vector.tensor_tensor(choice[:, :], score[:, :], r_bias[:, :], ALU.add))
                for g in range(N_GROUPS):
                    ins = nc.vector.max(top2[:, g, :], choice[:, g * GROUP:(g + 1) * GROUP])
                link(ins)
                link(nc.vector.tensor_tensor(gscore[:, :], top2[:, :, 0], top2[:, :, 1], ALU.add))
                link(nc.vector.max(rt8[:, 4, :], gscore[:, :]))
                pick(gscore[:, :], rt8[:, 4, TOPK_GROUPS - 1:TOPK_GROUPS], 8, TOPK_GROUPS, rt8[:, 3, :])
                link(nc.vector.tensor_scalar(rt8[:, 5, :], rt8[:, 3, :], MASKED, -MASKED, ALU.mult, ALU.add))
                c8 = choice[:, :].rearrange("p (g e) -> p g e", g=N_GROUPS)
                link(nc.vector.tensor_tensor(c8, c8, rt8[:, 5, :].unsqueeze(2).broadcast_to([P, N_GROUPS, GROUP]),
                                             ALU.add))
                link(nc.vector.max(rt8[:, 6, :], choice[:, :]))
                pick(choice[:, :], rt8[:, 6, TOP_K - 1:TOP_K], N_EXP, TOP_K, sel[:, t, :])
                dve.sem_inc(sel_made, 1)
                s = sel[:, t, :]
                link(nc.vector.tensor_tensor_reduce(rt64[:, 3, :], s, score[:, :], 1.0, 0.0, ALU.mult, ALU.add,
                                                    wsum[:, 0:1]))
                dve.sem_inc(scores_used, 1)
                link(nc.vector.reciprocal(wsum[:, 1:2], wsum[:, 0:1]))
                link(nc.vector.tensor_scalar(info[:, t, 0:N_EXP, 2], rt64[:, 3, :], wsum[:, 1:2], ROUTED_SCALE,
                                             ALU.mult, ALU.mult))
                link(nc.vector.tensor_tensor_scan(rank[:, :], s, s, 0.0, ALU.add, ALU.bypass))
                dve.wait_ge(consts_made, 6)
                tok = tok_row[:, t:t + 1]
                link(nc.vector.tensor_scalar(info[:, t, 0:N_EXP, 0], s, 0.0, tok, ALU.mult, ALU.add))
                link(nc.vector.tensor_scalar(info[:, t, 0:N_EXP, 0], info[:, t, 0:N_EXP, 0], -UNUSED, None, ALU.add))
                link(nc.vector.tensor_scalar(wsum[:, 2:3], tok, float(TOP_K), -1.0 - UNUSED, ALU.mult, ALU.add))
                link(nc.vector.tensor_scalar(info[:, t, 0:N_EXP, 1], rank[:, :], wsum[:, 2:3], None, ALU.add))

            def slots_of(t):
                dve.wait_ge(pos_done, t + 1)
                p = PS[:, C_BANK + 1, 0:N_EXP]
                link(nc.vector.tensor_scalar(rt64[:, 0, :], sel[:, t, :], -NO_SLOT, NO_SLOT, ALU.mult, ALU.add))
                nc.vector.tensor_tensor(pos[:, t, 0:N_EXP], p, rt64[:, 0, :], ALU.add).then_inc(info_made, 1)

            dve.wait_ge(branch_done, N_MERGE)
            dve.wait_ge(merged, N_MERGE)
            nc.vector.memset(pos[:, :, :], NO_SLOT)
            link(nc.vector.memset(info[:, :, :, :], 0.0))
            first_norm(0)
            first_norm(1)
            for t in range(QT):
                route(t)
                if t + 2 < QT:
                    first_norm(t + 2)
                if t >= 1:
                    slots_of(t - 1)
            slots_of(QT - 1)
            dve.wait_ge(pos_done, QT + 1)
            link(nc.vector.tensor_reduce(most[:, 0:1], PS[:, C_BANK + 1, 0:N_EXP], AX.X, ALU.max))
            nc.vector.tensor_copy(most_i[:, 0:1], most[0:1, 0:1]).then_inc(most_made, 1)

            def h_half(half, b, count, done):
                nc.vector.tensor_tensor(silu[:, half, 0:P], PS[:, G_BANK + half, 0:P], sig[:, half, 0:P], ALU.mult)\
                    .then_inc(silu_made, 1)
                dve.wait_ge(silu_made, count)
                nc.vector.tensor_tensor(h_slots[:, b, half * P:(half + 1) * P], PS[:, G_BANK + half, P:F],
                                        silu[:, half, 0:P], ALU.mult).then_inc(done, 1)

            for t in range(QT):
                dve.wait_ge(sig_a, t + 1)
                if t >= 2:
                    dve.wait_ge(y_done, t - 1)
                h_half(0, t % 2, 2 * t + 1, h_a)
                dve.wait_ge(sig_b, t + 1)
                h_half(1, t % 2, 2 * t + 2, h_b)
                dve.wait_ge(y_done, t + 1)
                for n in range(2):
                    nc.vector.scalar_tensor_tensor(mT_nat(t)[:, n * 512:(n + 1) * 512], x1[:, t, n * 512:(n + 1) * 512],
                                                   ALPHA, PS[:, Y_BANK + n, :], ALU.mult, ALU.add).then_inc(y_out1, 1)

            def mark_slots(j, b):
                nc.vector.tensor_tensor(onehot[:, b % 2, :, :],
                                        slot_no[:, :].unsqueeze(1).broadcast_to([P, QT, P]),
                                        pos[:, :, bass.ds(j, 1)].broadcast_to([P, QT, P]),
                                        ALU.is_equal).then_inc(onehot_made, 1)

            def rows_of(b, done):
                nc.vector.tensor_copy(w_slot[:, b, :], PS[:, I_BANK, 2:3])
                nc.vector.tensor_scalar(rows_u[:, b, :], PS[:, I_BANK, 0:2], UNUSED, None, ALU.add).then_inc(done, 1)

            dve.wait_ge(info_made, QT)
            for j in range(2):
                mark_slots(j, j)
            for j in range(2):
                dve.wait_ge(slots_done, j + 1)
                rows_of(j, rows_made)
                dve.wait_ge(rows_out[j], 16)
            with dve.Fori(0, N_EXP // 4) as i:
                for b in range(4):
                    e = i * 4 + b
                    dve.wait_ge(slots_done, e + 1)
                    mark_slots(e + 2, b)
                    dve.wait_ge(sig_a, e + QT + 1)
                    h_half(0, b % 2, e * 2 + 2 * QT + 1, h_a)
                    dve.wait_ge(sig_b, e + QT + 1)
                    h_half(1, b % 2, e * 2 + 2 * QT + 2, h_b)
                    dve.wait_ge(slots_done, e + 3)
                    dve.wait_ge(y_out0, e + 1)
                    dve.wait_ge(rows_out[b % 2], i * 32 + 16 * (b // 2 + 1))
                    rows_of((b + 2) % 4, rows_made)
                    dve.wait_ge(y_done, e + QT + 1)
                    nc.vector.tensor_scalar(y_slots[:, b % 2, 512:D], PS[:, Y_BANK + 1, :], w_slot[:, b, :], None,
                                            ALU.mult).then_inc(y_out1, 1)

            n = dve.value_load(most_i[0:1, 0:1], min_val=0, max_val=SEQ)
            with dve.If(n > P):
                nc.vector.tensor_copy(ov_slot[:, :], slot_no[:, :]).then_inc(ov["silu"], 1)
                with dve.Fori(1, SEQ // P) as c:
                    dve.wait_ge(ov["silu"], (c - 1) * (2 * N_EXP + 1) + 1)
                    nc.vector.tensor_scalar(ov_slot[:, :], ov_slot[:, :], float(P), None, ALU.add)\
                        .then_inc(ov["silu"], 1)
                    dve.wait_ge(ov["silu"], (c - 1) * (2 * N_EXP + 1) + 2)
                    dve.sem_inc(ov["turns"], 1)
                    with dve.Fori(0, N_EXP) as e:
                        j = (c - 1) * N_EXP + e
                        nc.vector.tensor_tensor(onehot[:, 0, :, :],
                                                ov_slot[:, :].unsqueeze(1).broadcast_to([P, QT, P]),
                                                pos[:, :, bass.ds(e, 1)].broadcast_to([P, QT, P]),
                                                ALU.is_equal).then_inc(ov["oh"], 1)
                        dve.wait_ge(ov["idx"], j + 1)
                        rows_of(0, ov["rows"])
                        for half in range(2):
                            dve.wait_ge(ov["sig"], j * 2 + half + 1)
                            nc.vector.tensor_tensor(silu[:, half, 0:P], PS[:, G_BANK + half, 0:P], sig[:, half, 0:P],
                                                    ALU.mult).then_inc(ov["silu"], 1)
                            dve.wait_ge(ov["silu"], j * 2 + half + c + 2)
                            nc.vector.tensor_tensor(h_slots[:, 0, half * P:(half + 1) * P], PS[:, G_BANK + half, P:F],
                                                    silu[:, half, 0:P], ALU.mult).then_inc(ov["h"], 1)
                        dve.wait_ge(ov["y"], j + 2)
                        for m in range(2):
                            ins = nc.vector.tensor_scalar(y_slots[:, 0, m * 512:(m + 1) * 512], PS[:, Y_BANK + m, :],
                                                          w_slot[:, 0, :], None, ALU.mult)
                        ins.then_inc(ov["yout"], 1)
                        dve.wait_ge(ov["out"], j * 16 + 16)

            for t in range(QT):
                dve.wait_ge(rows8_in[t % 2], 16 * (t // 2 + 1))
                v = mT_nat(t)
                acc = rows8[:, t % 2, 0, :]
                link(nc.vector.tensor_reduce(flat[:, 0:D],
                                             rows8[:, t % 2, :, :].rearrange("p r d -> p d r"), AX.X, ALU.add))
                dve.sem_inc(sums, 1)
                link(nc.vector.tensor_tensor(v, v, flat[:, 0:D], ALU.add))
                norm(v, QT + t)
                if t == 0:
                    dve.wait_ge(ln2_in, 32)
                link(nc.vector.tensor_tensor(v, v, ln2[:, 0, :], ALU.mult))
                nc.vector.tensor_tensor(v, v, ln2[:, 1, :], ALU.add).then_inc(out_made, 1)

        @block.gpsimd
        def _(pool):
            pool.wait_ge(consts_made, 1)
            nc.gpsimd.memset(ones[:, :], 1.0).then_inc(pool_chain, 1)
            nc.gpsimd.memset(half_neg[:, :], -0.5).then_inc(pool_chain, 1)
            nc.gpsimd.memset(ident[:, :], 0.0).then_inc(pool_chain, 1)
            pool.wait_ge(pool_chain, 3)
            nc.gpsimd.affine_select(out=ident[:, :], in_=ident[:, :], compare_op=ALU.not_equal, fill=1.0, base=0,
                                    pattern=[[-1, P]], channel_multiplier=1).then_inc(consts_made, 1)
            nc.gpsimd.affine_select(out=before[:, :], in_=ones[:, :], compare_op=ALU.is_gt, fill=0.0, base=0,
                                    pattern=[[1, P]], channel_multiplier=-1).then_inc(consts_made, 1)
            nc.gpsimd.iota(slot_no[:, :], pattern=[[1, P]], base=0, channel_multiplier=0,
                           allow_small_or_imprecise_dtypes=True).then_inc(consts_made, 1)
            nc.gpsimd.iota(tok_row[:, :], pattern=[[P, QT]], base=0, channel_multiplier=1,
                           allow_small_or_imprecise_dtypes=True).then_inc(consts_made, 1)
            pool.wait_ge(consts_made, 5)
            pool.sem_inc(consts_made, 1)

            def root(v, ready, count, done):
                pool.wait_ge(ready, count)
                nc.gpsimd.tensor_tensor(v, v, half_neg[:, 0:v.shape[1]], ALU.pow).then_inc(done, 1)

            def split(n):
                w = ring[:, n % RING, 0:KT * P].rearrange("p (c n) -> p c n", c=KT)
                wh, wl = w_hi[:, n % HALVES, :, :], w_lo[:, n % HALVES, :, :]
                pool.wait_ge(w_hi_made, n + 1)
                nc.gpsimd.tensor_tensor(wl, w, wh.bitcast(F32), ALU.subtract).then_inc(w_lo_made, 1)

            for n in range(N_PROJ + HALVES):
                split(n)
            for m in range(N_MERGE):
                if N_PROJ + m + HALVES < N_CHUNKS:
                    split(N_PROJ + m + HALVES)
                if m == merges_before_norm:
                    root(yc_ss[:, :], yc_stat, 1, yc_rms)
                pool.wait_ge(gated_made, m + 1)
                if m < KT:
                    pool.sem_inc(merged, 1)
                    continue
                if m >= KT + 1:
                    pool.wait_ge(merged, m)
                k = m % KT
                nc.gpsimd.tensor_tensor(mT[:, k, :], mT[:, k, :], gated[:, m % 2, :], ALU.add).then_inc(merged, 1)

            for k in range(QT):
                root(mv[:, 1:2], var_made, k + 1, rstd_made)
            pool.wait_ge(mix_done, QT)
            nc.gpsimd.memset(x_slots[:, :, :], 0.0).then_inc(slots_clear, 1)
            nc.gpsimd.memset(y_slots[:, :, :], 0.0).then_inc(slots_clear, 1)
            nc.gpsimd.memset(rows_u[:, 2:4, :], int(UNUSED)).then_inc(slots_clear, 1)
            pool.wait_ge(slots_clear, 3)
            last_tok = pool.to_reg(SEQ - 1)
            last_row = pool.to_reg(SEQ * TOP_K - 1)

            def gather(b, xb, done):
                pool.sem_inc(gathers_begun, 1)
                pool.indirect_dma_start(x_slots[:, xb, :], None, x1_d,
                                        bass.IndirectOffsetOnAxis(ap=rows_u[:, b, 0:1], axis=0),
                                        bounds_check=last_tok, oob_is_err=False).then_inc(done, 16)

            def scatter(b, yb, done):
                pool.sem_inc(scatters_begun, 1)
                pool.indirect_dma_start(rows_d, bass.IndirectOffsetOnAxis(ap=rows_u[:, b, 1:2], axis=0),
                                        y_slots[:, yb, :], None,
                                        bounds_check=last_row, oob_is_err=False).then_inc(done, 16)

            for b in range(2):
                scatter(2 + b, b, rows_out[b])
                pool.wait_ge(rows_out[b], 16)
            pool.wait_ge(x1_stored, 16 * QT)
            for j in range(2):
                pool.wait_ge(rows_made, j + 1)
                gather(j, j, slots_in[j])
            with pool.Fori(0, N_EXP // 4) as i:
                for b in range(4):
                    e = i * 4 + b
                    pool.wait_ge(rows_made, e + 3)
                    pool.wait_ge(slots_turned, e + 1)
                    gather((b + 2) % 4, b % 2, slots_in[b % 2])
                    pool.wait_ge(y_out0, e + 2)
                    pool.wait_ge(y_out1, e + 2 * QT + 1)
                    scatter(b, b % 2, rows_out[b % 2])
            for b in range(2):
                pool.wait_ge(slots_in[b], 16 * (N_EXP // 2 + 1))
                pool.wait_ge(rows_out[b], 16 * (N_EXP // 2 + 1))

            n = pool.value_load(most_i[0:1, 0:1], min_val=0, max_val=SEQ)
            with pool.If(n > P):
                with pool.Fori(1, SEQ // P) as c:
                    with pool.Fori(0, N_EXP) as e:
                        j = (c - 1) * N_EXP + e
                        pool.wait_ge(ov["rows"], j + 1)
                        gather(0, 0, ov["in"])
                        pool.wait_ge(ov["yout"], j + 1)
                        scatter(0, 0, ov["out"])
                pool.wait_ge(ov["out"], 16 * (SEQ // P - 1) * N_EXP)

            for k in range(QT, 2 * QT):
                root(mv[:, 1:2], var_made, k + 1, rstd_made)


def kernel(**inputs):
    import concourse.bacc as _bacc
    from concourse.bass_utils import run_bass_kernel_spmd as _run

    g = {k: np.asarray(v) for k, v in inputs.items()}
    w_in = g["w_in"][0]

    def columns(kind, br, j):
        first = COLS[kind, br]
        if (kind, br) == ("q", BR_B):
            return np.concatenate([first + h * HD + np.arange(HD) for h in (j, j + 2)])
        return first + j * P + np.arange(P)

    def tiles(w, n):
        return w.reshape(KT, P, n, P).transpose(2, 1, 0, 3)

    arrays = {
        "x": g["x"], "xT": g["x"][0].T, "t5_table": g["t5_table"],
        "w_proj": tiles(w_in[:, np.concatenate([columns(*c) for c in PROJ])], N_PROJ).reshape(N_PROJ, P, KT * P),
        "w_f": w_in[:, COLS["f"]:COLS["f"] + 4].reshape(KT, P, 4).transpose(1, 0, 2),
        "w_merge": np.concatenate([
            tiles(w_in[:, COLS["gates"]:], N_MERGE),
            g["w_branch"][0].reshape(4, 2, P, KT, P).transpose(0, 3, 2, 1, 4).reshape(N_MERGE, P, 2, P)],
            axis=2).reshape(N_MERGE, P, SLOT),
        "w_out": g["w_out"], "b_forget": g["b_forget"], "attn_sinks": g["attn_sinks"],
        "lam": np.stack([g["lam_q1"], g["lam_k1"], g["lam_q2"], g["lam_k2"]], axis=1),
        "diff_norm_g": g["diff_norm_g"], "ln1_g": g["ln1_g"], "ln1_b": g["ln1_b"], "ln2_g": g["ln2_g"],
        "ln2_b": g["ln2_b"], "w_router": g["w_router"], "router_bias": g["router_bias"],
        "w_gu": np.stack([g["w_gate_e"][0].reshape(N_EXP, D, FT, P), g["w_up_e"][0].reshape(N_EXP, D, FT, P)],
                         axis=3).reshape(N_EXP, P, KT * 2 * F),
        "w_down_e": g["w_down_e"],
        "w_gu_s": np.stack([g["w_gate_s"][0].reshape(D, FT, P), g["w_up_s"][0].reshape(D, FT, P)],
                           axis=2).reshape(P, KT * 2 * F),
        "w_down_s": g["w_down_s"],
    }
    arrays["neg_onehot"], arrays["dist_mask"], arrays["causal_strip"] = distance_constants()
    arrays = {k: np.ascontiguousarray(v) for k, v in arrays.items()}
    nc = _bacc.Bacc("TRN2", target_bir_lowering=False, num_devices=1)
    aps = {k: nc.dram_tensor(f"in_{k}", v.shape, mybir.dt.from_np(v.dtype), kind="ExternalInput").ap()
           for k, v in arrays.items()}
    out = nc.dram_tensor("out_0", (1, SEQ, D), F32, kind="ExternalOutput").ap()
    build(nc, aps, out)
    r = _run(nc, [{f"in_{k}": v for k, v in arrays.items()}], core_ids=[0])
    return r.results[0]["out_0"]
```

```python
from contextlib import ExitStack

import numpy as np

import concourse.bass as bass
from concourse import mybir

F32 = mybir.dt.float32
F32R = mybir.dt.float32r
U32 = mybir.dt.uint32
I32 = mybir.dt.int32
ALU = mybir.AluOpType
ACT = mybir.ActivationFunctionType
AX = mybir.AxisListType

P = 128
SEQ = 512
D = 1024
QT = SEQ // P
KT = D // P
HD = 64
WINDOW = 128
DILATIONS = ((128, 1), (512, 4), (2048, 16))
N_EXP = 64
TOP_K = 8
N_GROUPS = 8
TOPK_GROUPS = 4
GROUP = N_EXP // N_GROUPS
F = 256
FT = F // P
ROUTED_SCALE = 2.5
ALPHA = 2 ** 0.25
EPS = 1e-5
LAM_INIT = 0.2
BUCKETS = 32
MAX_DIST = 2048
MASKED = 1e30
UNUSED = 65536.0
NO_SLOT = 16384.0
BR_A, BR_B, BR_C, BR_D = range(4)

PROJ = ([("q", BR_A, 0), ("q", BR_A, 1), ("k", BR_A, 0), ("k", BR_A, 1), ("v", BR_A, 0), ("v", BR_A, 1)]
        + [("q", BR_B, 0), ("q", BR_B, 1), ("k", BR_B, 0), ("v", BR_B, 0)]
        + [(kind, br, j) for br in (BR_C, BR_D) for kind in "qkv" for j in range(2)])
V_AT = {(BR_A, 0): 0, (BR_A, 1): 1, (BR_B, 0): 2, (BR_C, 0): 3, (BR_C, 1): 4, (BR_D, 0): 5, (BR_D, 1): 6}
N_PROJ = len(PROJ)
N_MERGE = 4 * KT
N_CHUNKS = N_PROJ + N_MERGE
RING = 3
HALVES = 2
X_PARTS = 4
W_OUT_AFTER = N_PROJ + 26
SLOT = 10 * P

COLS = {("q", BR_A): 0, ("k", BR_A): 256, ("v", BR_A): 512, "f": 768,
        ("q", BR_B): 772, ("k", BR_B): 1028, ("v", BR_B): 1156,
        ("q", BR_C): 1284, ("k", BR_C): 1540, ("v", BR_C): 1796,
        ("q", BR_D): 2052, ("k", BR_D): 2308, ("v", BR_D): 2564, "gates": 2820}


def attention_steps():
    return ([(BR_A, h, 0, q) for h in range(4) for q in range(QT)]
            + [(BR_B, h, 0, q) for h in range(4) for q in range(QT)]
            + [(BR_C, h, c, q) for h in range(4) for c in range(2) for q in range(QT)]
            + [(BR_D, h, 0, q) for h in range(4) for q in range(QT)])


STEPS = attention_steps()


def keys_of(branch, qt):
    if branch == BR_B:
        return max(qt - 1, 0), min(qt, 1) + 1
    return 0, qt + 1


def order_of_work():
    proj, merges, steps = list(range(6, N_PROJ)), list(range(N_MERGE)), list(range(len(STEPS)))
    order = [("proj", c) for c in range(6)]

    def step(s):
        out = [("scores", s)]
        if s >= 1:
            out.append(("turn", s - 1))
        if s >= 2:
            out.append(("values", s - 2))
        if s >= 4 and STEPS[s - 4][0] != STEPS[s - 3][0]:
            out += [("turn_y", 2 * STEPS[s - 4][0] + j) for j in range(2)]
        return out

    def part(m, i):
        return [("part", 3 * m + i)] + ([("gate", m)] if i == 2 else [])

    def merge(m):
        return part(m, 0) + part(m, 1) + part(m, 2), [("branch", m), ("invert", m), ("gated", m)]

    for s in range(16):
        order += [("proj", proj.pop(0))] + step(s)
    for s in range(16, 20):
        order += step(s)
    at = 20
    while at < len(STEPS):
        m = merges.pop(0)
        if STEPS[at][0] == BR_C:
            plan = [part(m, 0), 1, part(m, 1), 1, part(m, 2), 1, [("branch", m), ("invert", m)], 1,
                    [("gated", m)]]
        else:
            plan = [part(m, 0) + part(m, 1), 1, part(m, 2) + [("branch", m)], 1, [("invert", m), ("gated", m)]]
        for x in plan:
            if x == 1:
                if at < len(STEPS):
                    order += step(at)
                at += 1
            else:
                order += x
    last = len(STEPS)
    g, z = merge(merges.pop(0))
    order += g + [("turn", last - 1), ("values", last - 2)] + z
    g, z = merge(merges.pop(0))
    order += g + [("values", last - 1)] + z
    order += [("turn_y", 2 * BR_D + j) for j in range(2)]
    while merges:
        g, z = merge(merges.pop(0))
        order += g + z
    return order


def distance_constants():
    dist = 511 - np.arange(640)
    n = np.maximum(dist, 0)
    exact = BUCKETS // 2
    large = exact + (np.log(np.maximum(n, 1) / exact) / np.log(MAX_DIST / exact) * (BUCKETS - exact)).astype(np.int32)
    bucket = np.where(n < exact, n, np.minimum(large, BUCKETS - 1))
    onehot = -(np.arange(BUCKETS)[:, None] == bucket[None, :]).astype(np.float32)
    times = sum(((dist <= (w // d) * d) & (dist % d == 0)).astype(np.int64) for w, d in DILATIONS)
    causal = np.where(dist >= 0, 0.0, MASKED)
    window = np.where((dist >= 0) & (dist < WINDOW), 0.0, MASKED)
    dilated = np.where((dist >= 0) & (times > 0), -np.log(np.maximum(times, 1)), MASKED)
    rows = [window] * 4 + [causal] * 4 + [dilated] * 4
    mask = np.zeros((16, 640), np.float32)
    mask[:12] = np.stack(rows)
    m = np.arange(SEQ)
    strip = np.where(np.arange(P)[:, None] + (SEQ - P) - m[None, :] >= 0, 0.0, MASKED).astype(np.float32)
    return onehot, mask, strip


def build(nc, a, out):
    order = order_of_work()
    turns = [x for x in order if x[0] in ("turn", "turn_y")]
    turn_at = {x: n for n, x in enumerate(turns)}
    n_steps = len(STEPS)
    last_step = {br: max(s for s, x in enumerate(STEPS) if x[0] == br) for br in range(4)}
    norm_step = last_step[BR_C] + 3
    merges_before_norm = sum(kind == "gated" for kind, _ in order[:order.index(("values", last_step[BR_C]))])

    ctx = ExitStack()
    with ctx:
        def sb(name, shape, dt=F32):
            return ctx.enter_context(nc.sbuf_tensor(name, shape, dt))

        def sem(name):
            return ctx.enter_context(nc.semaphore(name))

        PS = ctx.enter_context(nc.psum_tensor("PS", [P, 8, 512], F32))
        ident = sb("ident", [P, P])
        before = sb("before", [P, P])
        ones = sb("ones", [P, P])
        half_neg = sb("half_neg", [P, 16])
        slot_no = sb("slot_no", [P, P])
        tok_row = sb("tok_row", [P, QT + 1])
        mT = sb("mT", [P, KT, SEQ])
        w_f = sb("w_f", [P, KT, 4])
        b_f = sb("b_f", [4, 1])
        table = sb("table", [BUCKETS, 16])
        neg_sink = sb("neg_sink", [P, 4])
        lam_in = sb("lam_in", [P, 4, 32])
        lam_mul = sb("lam_mul", [P, 2, 32])
        lam_s = sb("lam_s", [P, 8])
        norm_g = sb("norm_g", [P, HD])
        nmax = sb("nmax", [P, n_steps])
        den = sb("den", [P, n_steps])
        rden = sb("rden", [P, n_steps])
        yc_sq = sb("yc_sq", [P, F])
        yc_ss = sb("yc_ss", [P, 16])
        stats = sb("stats", [P, 2, 6])
        mv = sb("mv", [P, 8])
        r_bias = sb("r_bias", [P, N_EXP])
        gscore = sb("gscore", [P, 8])
        rt8 = sb("rt8", [P, 8, 8])
        sel = sb("sel", [P, QT, N_EXP])
        wsum = sb("wsum", [P, 8])
        rows_u = sb("rows_u", [P, 4, 2], U32)
        w_slot = sb("w_slot", [P, 4, 1])
        most = sb("most", [P, 2])
        most_i = sb("most_i", [1, 2], I32)
        ov_slot = sb("ov_slot", [P, P])
        attention = ExitStack()

        def sb1(name, shape, dt=F32):
            return attention.enter_context(nc.sbuf_tensor(name, shape, dt))

        x_hi = sb1("x_hi", [P, KT, SEQ], F32R)
        x_lo = sb1("x_lo", [P, KT, SEQ], F32R)
        w_hi = sb1("w_hi", [P, HALVES, KT, P], F32R)
        w_lo = sb1("w_lo", [P, HALVES, KT, P], F32R)
        ring = sb1("ring", [P, RING, SLOT])
        region1 = sb1("region1", [P, 29190])

        def carve(region, start, shape):
            n = int(np.prod(shape))
            v = region[:, start:start + n]
            if len(shape) == 2:
                v = v.rearrange("p (a b) -> p a b", a=shape[0])
            elif len(shape) == 3:
                v = v.rearrange("p (a b c) -> p a b c", a=shape[0], b=shape[1])
            return v, start + n

        qA, o = carve(region1, 0, (4, SEQ))
        kA, o = carve(region1, o, (4, SEQ))
        qB, o = carve(region1, o, (2, SEQ))
        kB, o = carve(region1, o, (1, SEQ))
        qC, o = carve(region1, o, (2, SEQ))
        kC, o = carve(region1, o, (2, SEQ))
        strips, o = carve(region1, o, (13, SEQ))
        w_out, _ = carve(region1, 0, (KT, D))
        qD, o = carve(region1, o, (2, SEQ))
        kD, o = carve(region1, o, (2, SEQ))
        V, o = carve(region1, o, (QT, 7, P))
        probs, o = carve(region1, o, (3, SEQ + 2))
        probsT, o = carve(region1, o, (3, SEQ))
        Y, o = carve(region1, o, (2 * QT, F))
        yT, o = carve(region1, o, (4, SEQ))
        gate, o = carve(region1, o, (2, SEQ))
        gated, o = carve(region1, o, (2, SEQ))
        assert o == 29190, o
        fg = yT[0:4, :, :]
        neg_oh = gate.rearrange("p a b -> p (a b)")[0:BUCKETS, 0:640]
        dist_mask = gated.rearrange("p a b -> p (a b)")[0:16, 0:640]
        dist_bias = Y.rearrange("p a b -> p (a b)")[0:16, 0:640]
        attention.close()

        xT = sb("x1T", [P, KT, SEQ])
        flat = sb("slots", [P, 8 * D])
        region2 = sb("region2", [P, 27904])
        ln1, o = carve(region2, 0, (2, D))
        info, o = carve(region2, o, (QT, N_EXP + 2, 2))
        pos, o = carve(region2, o, (QT, N_EXP + 2))
        w_r, o = carve(region2, o, (KT, N_EXP))
        assert o <= RING * SLOT, o
        w_gu0, o = carve(region2, RING * SLOT, (KT, 2 * F))
        w_dn0, o = carve(region2, o, (FT, D))
        ln2, o = carve(region2, o, (2, D))
        assert o >= RING * SLOT + KT * D, o
        w_gu1, o = carve(region2, o, (KT, 2 * F))
        w_dn1, o = carve(region2, o, (FT, D))
        w_gu, w_dn = (w_gu0, w_gu1), (w_dn0, w_dn1)
        x1, o = carve(region2, o, (QT, D))
        acc = [w.rearrange("p a b -> p (a b)").rearrange("p (a b) -> p a b", a=QT) for w in w_gu]
        onehot, o = carve(region2, o, (2, QT, P))
        top2, o = carve(region2, o, (N_GROUPS, 8))
        rt64, o = carve(region2, o, (4, N_EXP))
        score, o = carve(region2, o, (N_EXP,))
        choice, o = carve(region2, o, (N_EXP,))
        assert o <= 27904, o
        first = ExitStack()
        x_nat = first.enter_context(nc.sbuf_tensor("x_nat", [P, QT, D], F32))
        first.close()
        wd_hi = sb("wd_hi", [P, FT, D], F32R)
        wd_lo = sb("wd_lo", [P, FT, D], F32R)
        hT_hi = sb("hT_hi", [P, 2, FT, P], F32R)
        hT_lo = sb("hT_lo", [P, 2, FT, P], F32R)
        x_slots = flat[:, 0:2 * D].rearrange("p (a b) -> p a b", a=2)
        x_slotsT = flat[:, 2 * D:4 * D].rearrange("p (a k t) -> p a k t", a=2, k=KT)
        y_slots = flat[:, 4 * D:6 * D].rearrange("p (a b) -> p a b", a=2)
        h_slots = flat[:, 6 * D:6 * D + 512].rearrange("p (a b) -> p a b", a=2)
        hT = flat[:, 6 * D + 512:6 * D + 512 + F].rearrange("p (k t) -> p k t", k=FT)
        sig = flat[:, 7 * D:7 * D + 512].rearrange("p (a b) -> p a b", a=2)
        silu = flat[:, 7 * D + 512:8 * D].rearrange("p (a b) -> p a b", a=2)

        bias_d = nc.dram_tensor("bias_d", (12, P, 640), F32).ap()
        x1_d = nc.dram_tensor("x1_d", (SEQ, D), F32).ap()
        acc_d = [nc.dram_tensor(f"acc_d{b}", (SEQ + P, D), F32).ap() for b in range(2)]

        S_BANK, T_BANK, O_BANK, C_BANK = 0, 2, 4, 6
        G_BANK, X_BANK, H_BANK, I_BANK, Y_BANK = 0, 2, 4, 5, 6

        ring_in = [sem(f"ring_in{j}") for j in range(RING)]
        small_in = sem("small_in")
        xT_in = [sem(f"xT_in{j}") for j in range(X_PARTS)]
        w_f_in = sem("w_f_in")
        x_hi_made = sem("x_hi_made")
        x_lo_made = sem("x_lo_made")
        w_hi_made = sem("w_hi_made")
        w_lo_made = sem("w_lo_made")
        w_out_in = sem("w_out_in")
        bias_io = sem("bias_io")
        causal_in = sem("causal_in")
        strips_in = [sem(f"strips_in{g}") for g in range(3)]
        aug_in = sem("aug_in")
        consts_made = sem("consts_made")
        dve_chain = sem("dve_chain")
        act_chain = sem("act_chain")
        pool_chain = sem("pool_chain")
        bias_mm = sem("bias_mm")
        bias_made = sem("bias_made")
        forget_mm = sem("forget_mm")
        forget_exp = sem("forget_exp")
        forget_made = sem("forget_made")
        lam_dots = sem("lam_dots")
        lam_exp = sem("lam_exp")
        proj_done = sem("proj_done")
        proj_out = sem("proj_out")
        scores_done = sem("scores_done")
        biased = sem("biased")
        probs_made = sem("probs_made")
        turned = sem("turned")
        turned_out = sem("turned_out")
        values_done = sem("values_done")
        y_made = sem("y_made")
        yc_stat = sem("yc_stat")
        yc_rms = sem("yc_rms")
        y_ready = sem("y_ready")
        gate_done = sem("gate_done")
        gate_exp = sem("gate_exp")
        branch_done = sem("branch_done")
        gated_made = sem("gated_made")
        merged = sem("merged")
        x_in = sem("x_in")
        late_in = sem("late_in")
        ln2_in = sem("ln2_in")
        mix_done = sem("mix_done")
        var_made = sem("var_made")
        rstd_made = sem("rstd_made")
        x1_made = sem("x1_made")
        x1_stored = sem("x1_stored")
        x1_turned = sem("x1_turned")
        x1T_made = sem("x1T_made")
        router_done = sem("router_done")
        router_exp = sem("router_exp")
        sel_made = sem("sel_made")
        scores_used = sem("scores_used")
        pos_done = sem("pos_done")
        info_made = sem("info_made")
        most_made = sem("most_made")
        sh_in = sem("sh_in")
        gu_in = [sem(f"gu_in{b}") for b in range(2)]
        dn_in = [sem(f"dn_in{b}") for b in range(2)]
        slots_in = [sem(f"slots_in{b}") for b in range(2)]
        slots_clear = sem("slots_clear")
        gathers_begun = sem("gathers_begun")
        scatters_begun = sem("scatters_begun")
        gu_a = sem("gu_a")
        gu_b = sem("gu_b")
        sig_a = sem("sig_a")
        sig_b = sem("sig_b")
        silu_made = sem("silu_made")
        h_a = sem("h_a")
        h_b = sem("h_b")
        h_turned_a = sem("h_turned_a")
        h_turned_b = sem("h_turned_b")
        hT_a = sem("hT_a")
        hT_b = sem("hT_b")
        hT_lo_a = sem("hT_lo_a")
        hT_lo_b = sem("hT_lo_b")
        wd_hi_made = sem("wd_hi_made")
        wd_lo_made = sem("wd_lo_made")
        y_done = sem("y_done")
        y_out0 = sem("y_out0")
        y_out1 = sem("y_out1")
        onehot_made = sem("onehot_made")
        slots_done = sem("slots_done")
        rows_made = sem("rows_made")
        slots_turned = sem("slots_turned")
        slotsT_made = sem("slotsT_made")
        rows_out = [sem(f"rows_out{b}") for b in range(2)]
        ov = {n: sem(f"ov_{n}") for n in ("w", "oh", "idx", "rows", "in", "tr", "xT", "gu", "sig", "silu", "h",
                                          "hturn", "hT", "y", "yout", "out", "turns")}
        acc_in = [[sem(f"acc_in{b}_{t}") for t in range(QT)] for b in range(2)]
        scaled = sem("scaled")
        out_made = sem("out_made")
        out_stored = sem("out_stored")

        def mT_nat(t):
            return mT[:, :, :].rearrange("p a b -> p (a b)")[:, t * D:(t + 1) * D]

        block = ctx.enter_context(nc.Block())

        SMALL = 7
        N_LATE = 4

        @block.sync
        def _(sp):
            def chunk(j):
                if j >= RING:
                    if j - RING < N_PROJ:
                        sp.wait_ge(w_lo_made, j - RING + 1)
                    else:
                        sp.wait_ge(branch_done, j - RING - N_PROJ + 1)
                src, n = (a["w_proj"][j], KT * P) if j < N_PROJ else (a["w_merge"][j - N_PROJ], 10 * P)
                sp.dma_start(ring[:, j % RING, 0:n], src).then_inc(ring_in[j % RING], 16)

            chunk(0)
            xT_parts = a["xT"].rearrange("(c p) n -> p c n", p=P)
            k = KT // X_PARTS
            for j in range(X_PARTS):
                sp.dma_start(mT[:, j * k:(j + 1) * k, :], xT_parts[:, j * k:(j + 1) * k, :]).then_inc(xT_in[j], 16)
            sp.dma_start(w_f[:], a["w_f"]).then_inc(w_f_in, 16)
            sp.dma_start(b_f[:], a["b_forget"].rearrange("o h -> h o")).then_inc(small_in, 16)
            sp.dma_start(neg_oh, a["neg_onehot"]).then_inc(small_in, 16)
            sp.dma_start(dist_mask, a["dist_mask"]).then_inc(small_in, 16)
            sp.wait_ge(consts_made, 1)
            sp.dma_start(table[:, 0:12], a["t5_table"]).then_inc(small_in, 16)
            sp.dma_start(neg_sink[:], bass.AP(a["attn_sinks"].tensor, 0, [[0, P], [1, 4]])).then_inc(small_in, 16)
            sp.dma_start(lam_in[:, :, :], bass.AP(a["lam"].tensor, 0, [[0, P], [32, 4], [1, 32]]))\
                .then_inc(small_in, 16)
            sp.dma_start(norm_g[:], bass.AP(a["diff_norm_g"].tensor, 0, [[0, P], [1, HD]])).then_inc(small_in, 16)
            sp.dma_start(strips[:, 0, :], a["causal_strip"]).then_inc(causal_in, 16)
            for j in range(1, 6):
                chunk(j)
            sp.wait_ge(bias_made, 1)
            for g in range(3):
                sp.dma_start(bias_d[4 * g:4 * g + 4], dist_bias[4 * g:4 * g + 4, :].unsqueeze(1)
                             .broadcast_to([4, P, 640])).then_inc(bias_io, 16)
            sp.wait_ge(forget_made, 1)
            sp.dma_start(kA[64:65, :, :], fg[:, 2, :]).then_inc(aug_in, 16)
            sp.dma_start(qA[65:66, :, :], fg[:, 3, :]).then_inc(aug_in, 16)
            for j in range(6, 9):
                chunk(j)
            sp.wait_ge(bias_io, 48)
            for g in range(3):
                sp.dma_start(strips[:, 1 + 4 * g:5 + 4 * g, :],
                             bass.AP(bias_d.tensor, P - 1 + 4 * g * P * 640, [[639, P], [P * 640, 4], [1, SEQ]]))\
                    .then_inc(strips_in[g], 16)
                chunk(9 + g)
            for j in range(12, N_CHUNKS):
                chunk(j)
                if j == W_OUT_AFTER:
                    sp.wait_ge(scores_done, last_step[BR_C] + 1)
                    sp.dma_start(w_out, a["w_out"][0].rearrange("(k p) n -> p k n", p=P)).then_inc(w_out_in, 16)

            sp.wait_ge(branch_done, N_MERGE)
            sp.wait_ge(merged, N_MERGE)
            for t in range(QT):
                sp.dma_start(x_nat[:, t, :], a["x"][0, t * P:(t + 1) * P, :]).then_inc(x_in, 16)
            sp.dma_start(ln1[:, 0, :], bass.AP(a["ln1_g"].tensor, 0, [[0, P], [1, D]])).then_inc(late_in, 16)
            sp.dma_start(ln1[:, 1, :], bass.AP(a["ln1_b"].tensor, 0, [[0, P], [1, D]])).then_inc(late_in, 16)
            sp.dma_start(w_r[:], a["w_router"][0].rearrange("(p c) e -> p c e", c=KT)).then_inc(late_in, 16)
            sp.dma_start(r_bias[:], bass.AP(a["router_bias"].tensor, 0, [[0, P], [1, N_EXP]])).then_inc(late_in, 16)
            sp.dma_start(w_gu[1], a["w_gu_s"].rearrange("p (c n) -> p c n", c=KT)).then_inc(sh_in, 16)
            sp.dma_start(w_dn[1], a["w_down_s"][0].rearrange("(t p) n -> p t n", p=P)).then_inc(sh_in, 16)
            for t in range(QT):
                sp.wait_ge(x1_made, t + 1)
                sp.dma_start(x1_d[t * P:(t + 1) * P, :], x1[:, t, :]).then_inc(x1_stored, 16)
            sp.wait_ge(mix_done, QT)
            sp.dma_start(ln2[:, 0, :], bass.AP(a["ln2_g"].tensor, 0, [[0, P], [1, D]])).then_inc(ln2_in, 16)
            sp.dma_start(ln2[:, 1, :], bass.AP(a["ln2_b"].tensor, 0, [[0, P], [1, D]])).then_inc(ln2_in, 16)

            def load_down(b, e):
                sp.dma_start(w_dn[b], a["w_down_e"][0, bass.ds(e, 1)].rearrange("o (t p) n -> (o p) t n", p=P))\
                    .then_inc(dn_in[b], 16)

            def load_gate_up(b, e):
                sp.dma_start(w_gu[b], a["w_gu"][bass.ds(e, 1)].rearrange("o p (c n) -> (o p) c n", c=KT))\
                    .then_inc(gu_in[b], 16)

            def load(b, e, halves_split, products_made):
                sp.wait_ge(wd_lo_made, halves_split)
                load_down(b, e)
                sp.wait_ge(gu_b, products_made)
                load_gate_up(b, e)

            load_gate_up(0, 0)
            load_down(0, 0)
            with sp.Fori(0, N_EXP // 4 - 1) as i:
                for b in range(4):
                    load((b + 1) % 2, i * 4 + b + 1, i * 8 + 2 * b + 2, i * 4 + b + QT)
            for e in range(N_EXP - 3, N_EXP):
                load(e % 2, e, 2 * e, e + QT - 1)

            sp.wait_ge(most_made, 1)
            n = sp.value_load(most_i[0:1, 0:1], min_val=0, max_val=SEQ)
            with sp.If(n > P):
                sp.wait_ge(y_done, QT + N_EXP)
                with sp.Fori(1, SEQ // P) as c:
                    with sp.Fori(0, N_EXP) as e:
                        j = (c - 1) * N_EXP + e
                        sp.wait_ge(ov["y"], j + 1)
                        sp.dma_start(w_gu[0],
                                     a["w_gu"][bass.ds(e, 1)].rearrange("o p (c n) -> (o p) c n", c=KT))\
                            .then_inc(ov["w"], 16)
                        sp.dma_start(w_dn[0],
                                     a["w_down_e"][0, bass.ds(e, 1)].rearrange("o (t p) n -> (o p) t n", p=P))\
                            .then_inc(ov["w"], 16)
                sp.wait_ge(ov["out"], 16 * (SEQ // P - 1) * N_EXP)

            sp.wait_ge(y_out1, 3 * QT)
            for b in range(2):
                sp.wait_ge(rows_out[b], 16 * (N_EXP // 2 + 1))
                for t in range(QT):
                    sp.dma_start(acc[b][:, t, :], acc_d[b][t * P:(t + 1) * P, :]).then_inc(acc_in[b][t], 16)
            for t in range(QT):
                sp.wait_ge(out_made, t + 1)
                sp.dma_start(out[0, t * P:(t + 1) * P, :], mT_nat(t)).then_inc(out_stored, 16)
            sp.wait_ge(out_stored, 16 * QT)
            sp.wait_ge(x1_stored, 16 * QT)

        @block.tensor
        def _(pe):
            def qk_of(s):
                br, h, c, qt = STEPS[s]
                k0, nk = keys_of(br, qt)
                q, k = {BR_A: (qA, kA), BR_B: (qB, kB), BR_C: (qC, kC), BR_D: (qD, kD)}[br]
                if br == BR_A:
                    base, n, jq, jk = 0, 66, h, h
                elif br == BR_B:
                    base, n, jq, jk = 64 * (h // 2), 64, h % 2, 0
                elif br == BR_C:
                    base, n, jq, jk = 64 * (h % 2) + 32 * c, 32, h // 2, h // 2
                else:
                    base, n, jq, jk = 64 * (h % 2), 64, h // 2, h // 2
                return (q[base:base + n, jq, qt * P:(qt + 1) * P], k[base:base + n, jk, k0 * P:(k0 + nk) * P])

            def v_of(s, kt):
                br, h, _, _ = STEPS[s]
                if br == BR_B:
                    return V[:, kt, V_AT[br, 0], HD * (h // 2):HD * (h // 2) + HD]
                return V[:, kt, V_AT[br, h // 2], HD * (h % 2):HD * (h % 2) + HD]

            def forget_gates():
                pe.wait_ge(w_f_in, 16)
                for c in range(KT):
                    mm = nc.tensor.matmul(PS[0:4, T_BANK, :], w_f[:, c, :], mT[:, c, :], start=(c == 0),
                                          stop=(c == KT - 1))
                mm.then_inc(forget_mm, 1)

            def distance_bias():
                pe.wait_ge(consts_made, 2)
                pe.wait_ge(small_in, 16 * SMALL)
                nc.tensor.matmul(PS[0:16, S_BANK, 0:512], table[:, :], neg_oh[:, 0:512], start=True, stop=True)
                nc.tensor.matmul(PS[0:16, S_BANK + 1, 0:128], table[:, :], neg_oh[:, 512:640], start=True, stop=True)\
                    .then_inc(bias_mm, 1)

            def x_product_part(bank, n, i):
                if i == 0:
                    pe.wait_ge(w_hi_made, n + 1)
                if i == 2:
                    pe.wait_ge(w_lo_made, n + 1)
                for c in range(KT):
                    mm = nc.tensor.matmul(PS[:, bank, :], (w_hi, w_hi, w_lo)[i][:, n % HALVES, c, :],
                                          (x_hi, x_lo, x_hi)[i][:, c, :], start=(i == 0 and c == 0),
                                          stop=(i == 2 and c == KT - 1))
                return mm

            def x_product(bank, n):
                if n == 0:
                    pe.wait_ge(w_hi_made, 1)
                    for c in range(KT):
                        pe.wait_ge(x_hi_made, c + 1)
                        nc.tensor.matmul(PS[:, bank, :], w_hi[:, 0, c, :], x_hi[:, c, :], start=(c == 0), stop=False)
                        pe.wait_ge(x_lo_made, c + 1)
                        nc.tensor.matmul(PS[:, bank, :], w_hi[:, 0, c, :], x_lo[:, c, :], start=False, stop=False)
                    return x_product_part(bank, n, 2)
                for i in range(3):
                    mm = x_product_part(bank, n, i)
                return mm

            def x_product_tokens(bank, n):
                wh, wl = w_hi[:, n % HALVES, :, :], w_lo[:, n % HALVES, :, :]
                pe.wait_ge(w_hi_made, n + 1)
                pe.wait_ge(w_lo_made, n + 1)
                for t in range(QT):
                    to, tok = PS[:, bank, t * P:(t + 1) * P], slice(t * P, (t + 1) * P)
                    for c in range(KT):
                        nc.tensor.matmul(to, x_hi[:, c, tok], wh[:, c, :], start=(c == 0), stop=False)
                        nc.tensor.matmul(to, x_hi[:, c, tok], wl[:, c, :], start=False, stop=False)
                        mm = nc.tensor.matmul(to, x_lo[:, c, tok], wh[:, c, :], start=False, stop=(c == KT - 1))
                return mm

            for kind, n in order:
                if kind == "proj":
                    u = n
                    bank = C_BANK + u % 2
                    if u >= 2:
                        pe.wait_ge(proj_out, u - 1)
                    (x_product_tokens if PROJ[n][0] == "v" else x_product)(bank, n).then_inc(proj_done, 1)
                    if n == 0:
                        forget_gates()
                        distance_bias()
                elif kind == "scores":
                    br, h, _, qt = STEPS[n]
                    if qt == 0:
                        need = max(m for m, x in enumerate(PROJ) if x[1] == br and x[0] in "qk")
                        pe.wait_ge(proj_out, need + 1)
                        if br == BR_A:
                            pe.wait_ge(aug_in, 32)
                    if n < 2:
                        pe.wait_ge(bias_made, 1)
                    else:
                        pe.wait_ge(biased, n - 1)
                    q, k = qk_of(n)
                    nk = keys_of(br, qt)[1]
                    nc.tensor.matmul(PS[:, S_BANK + n % 2, 0:nk * P], q, k, start=True, stop=True)\
                        .then_inc(scores_done, 1)
                elif kind == "turn":
                    u = turn_at[kind, n]
                    br, _, _, qt = STEPS[n]
                    pe.wait_ge(probs_made, n + 1)
                    if u >= 2:
                        pe.wait_ge(turned_out, u - 1)
                    else:
                        pe.wait_ge(forget_exp, 1)
                    for j in range(keys_of(br, qt)[1]):
                        mm = nc.tensor.transpose(PS[:, T_BANK + u % 2, j * P:(j + 1) * P],
                                                 probs[:, n % 3, j * P:(j + 1) * P], ident[:, :])
                    mm.then_inc(turned, 1)
                elif kind == "values":
                    br, _, _, qt = STEPS[n]
                    k0, nk = keys_of(br, qt)
                    pe.wait_ge(turned_out, turn_at["turn", n] + 1)
                    need = max(m for m, x in enumerate(PROJ) if x[1] == br and x[0] == "v")
                    pe.wait_ge(proj_out, need + 1)
                    if n >= 2:
                        pe.wait_ge(y_made, n - 1)
                    for j in range(nk):
                        mm = nc.tensor.matmul(PS[:, O_BANK + n % 2, 0:HD], probsT[:, n % 3, j * P:(j + 1) * P],
                                              v_of(n, k0 + j), start=(j == 0), stop=(j == nk - 1))
                    mm.then_inc(values_done, 1)
                elif kind == "turn_y":
                    u = turn_at[kind, n]
                    br, j = n // 2, n % 2
                    pe.wait_ge(y_ready, br + 1)
                    pe.wait_ge(turned_out, u - 1)
                    for t in range(QT):
                        mm = nc.tensor.transpose(PS[:, T_BANK + u % 2, t * P:(t + 1) * P],
                                                 Y[:, (br % 2) * QT + t, j * P:(j + 1) * P], ident[:, :])
                    mm.then_inc(turned, 1)
                elif kind == "part":
                    m, i = divmod(n, 3)
                    if i == 0:
                        if m == 0:
                            pe.wait_ge(proj_out, N_PROJ)
                        else:
                            pe.wait_ge(gate_exp, m)
                    mm = x_product_part(C_BANK, N_PROJ + m, i)
                    if i == 2:
                        mm.then_inc(gate_done, 1)
                elif kind == "branch":
                    j, br = N_PROJ + n, n // KT
                    w = ring[:, j % RING, :].rearrange("p (c n) -> p c n", c=10)
                    pe.wait_ge(turned_out, turn_at["turn_y", 2 * br + 1] + 1)
                    if n >= 1:
                        pe.wait_ge(gated_made, n)
                    for c in range(2):
                        mm = nc.tensor.matmul(PS[:, C_BANK + 1, :], w[:, KT + c, :], yT[:, (br % 2) * 2 + c, :],
                                              start=(c == 0), stop=(c == 1))
                    mm.then_inc(branch_done, 1)

            def mix(t):
                if t == 0:
                    pe.wait_ge(w_out_in, 16)
                    pe.wait_ge(merged, N_MERGE - 1)
                    pe.wait_ge(biased, n_steps)
                    pe.wait_ge(y_made, n_steps)
                if t >= 2:
                    pe.wait_ge(var_made, t - 1)
                bank = S_BANK if t % 2 == 0 else O_BANK
                for k in range(KT):
                    if t == 0 and k == KT - 1:
                        pe.wait_ge(merged, N_MERGE)
                    for half in range(2):
                        mm = nc.tensor.matmul(PS[:, bank + half, :], mT[:, k, t * P:(t + 1) * P],
                                              w_out[:, k, half * 512:half * 512 + 512],
                                              start=(k == 0), stop=(k == KT - 1))
                mm.then_inc(mix_done, 1)

            def turn_x1(t):
                pe.wait_ge(x1_made, t + 1)
                if t == 0:
                    pe.wait_ge(turned_out, len(turns))
                else:
                    pe.wait_ge(x1T_made, t)
                xs = x1[:, t, :].rearrange("p (q c) -> p c q", c=KT)
                for c in range(KT):
                    mm = nc.tensor.transpose(PS[:, X_BANK + c // 4, (c % 4) * P:(c % 4 + 1) * P], xs[:, c, :],
                                             ident[:, :])
                mm.then_inc(x1_turned, 1)

            def router(t):
                pe.wait_ge(x1T_made, t + 1)
                if t == 0:
                    pe.wait_ge(late_in, 16 * N_LATE)
                    pe.wait_ge(gate_exp, N_MERGE)
                else:
                    pe.wait_ge(router_exp, t)
                for c in range(KT):
                    mm = nc.tensor.matmul(PS[:, C_BANK, 0:N_EXP], xT[:, c, t * P:(t + 1) * P], w_r[:, c, :],
                                          start=(c == 0), stop=(c == KT - 1))
                mm.then_inc(router_done, 1)

            def positions(t):
                pe.wait_ge(sel_made, min(t + 1, QT))
                if t == 0:
                    pe.wait_ge(gated_made, N_MERGE)
                else:
                    pe.wait_ge(info_made, t)
                for u in range(min(t + 1, QT)):
                    mm = nc.tensor.matmul(PS[:, C_BANK + 1, 0:N_EXP], (before if u == t else ones)[:, :], sel[:, u, :],
                                          start=(u == 0), stop=(u == min(t, QT - 1)))
                mm.then_inc(pos_done, 1)

            def gate_up(xs, w, half, done):
                for c in range(KT):
                    mm = nc.tensor.matmul(PS[:, G_BANK + half, 0:F], xs(c), w[:, c, half * F:(half + 1) * F],
                                          start=(c == 0), stop=(c == KT - 1))
                mm.then_inc(done, 1)

            def turn_h(b, half, done):
                nc.tensor.transpose(PS[:, H_BANK, 0:P], h_slots[:, b, half * P:(half + 1) * P], ident[:, :])\
                    .then_inc(done, 1)

            def down(bank, b, half, low_made, count):
                hh, hl = hT_hi[:, b, half, :], hT_lo[:, b, half, :]
                for n in range(2):
                    cols = slice(n * 512, (n + 1) * 512)
                    nc.tensor.matmul(PS[:, bank + n, :], hh, wd_hi[:, half, cols], start=(half == 0), stop=False)
                    nc.tensor.matmul(PS[:, bank + n, :], hh, wd_lo[:, half, cols], start=False, stop=False)
                pe.wait_ge(low_made, count)
                for n in range(2):
                    mm = nc.tensor.matmul(PS[:, bank + n, :], hl, wd_hi[:, half, n * 512:(n + 1) * 512],
                                          start=False, stop=(half == 1))
                return mm

            def slots(j, b):
                pe.wait_ge(onehot_made, j + 1)
                pe.wait_ge(rows_made, j)
                for t in range(QT):
                    mm = nc.tensor.matmul(PS[:, I_BANK, 0:2], onehot[:, b % 2, t, :],
                                          info[:, t, bass.ds(j, 1), :].rearrange("p a b -> p (a b)"),
                                          start=(t == 0), stop=(t == QT - 1))
                mm.then_inc(slots_done, 1)

            def shared(t):
                if t == 0:
                    pe.wait_ge(sh_in, 32)
                    pe.wait_ge(var_made, QT)
                else:
                    pe.wait_ge(h_a, t)
                    pe.wait_ge(h_b, t)
                for half, done in ((0, gu_a), (1, gu_b)):
                    gate_up(lambda c: xT[:, c, t * P:(t + 1) * P], w_gu[1], half, done)
                pe.wait_ge(h_a, t + 1)
                turn_h(t % 2, 0, h_turned_a)
                pe.wait_ge(hT_a, t + 1)
                if t == 0:
                    pe.wait_ge(x1T_made, QT)
                else:
                    pe.wait_ge(y_out1, 2 * t)
                pe.wait_ge(wd_lo_made, 2)
                down(X_BANK, t % 2, 0, hT_lo_a, t + 1)
                pe.wait_ge(h_b, t + 1)
                turn_h(t % 2, 1, h_turned_b)
                pe.wait_ge(hT_b, t + 1)
                down(X_BANK, t % 2, 1, hT_lo_b, t + 1).then_inc(y_done, 1)

            mix(0)
            mix(1)
            for t in range(QT):
                turn_x1(t)
                router(t)
                if t + 2 < QT:
                    mix(t + 2)
                if 1 <= t < QT - 1:
                    positions(t - 1)
                if t == QT - 1:
                    shared(0)
            positions(QT - 2)
            shared(1)
            positions(QT - 1)
            positions(QT)
            slots(0, 0)
            slots(1, 1)
            for t in range(2, QT):
                shared(t)

            def turn_slots(j, b, wait):
                wait()
                pe.wait_ge(slotsT_made, j)
                xs = x_slots[:, b % 2, :].rearrange("p (q c) -> p c q", c=KT)
                for c in range(KT):
                    mm = nc.tensor.transpose(PS[:, X_BANK + c // 4, (c % 4) * P:(c % 4 + 1) * P], xs[:, c, :],
                                             ident[:, :])
                mm.then_inc(slots_turned, 1)

            pe.wait_ge(y_out1, 2 * QT)
            pe.wait_ge(router_exp, QT)
            pe.wait_ge(most_made, 1)
            turn_slots(0, 0, lambda: pe.wait_ge(slots_in[0], 16))
            with pe.Fori(0, N_EXP // 4) as i:
                for b in range(4):
                    e = i * 4 + b
                    pe.wait_ge(slotsT_made, e + 1)
                    pe.wait_ge(gu_in[b % 2], i * 32 + 16 * (b // 2 + 1))
                    pe.wait_ge(h_a, e + QT)
                    xs = lambda c, b=b: x_slotsT[:, b % 2, c, :]
                    gate_up(xs, w_gu[b % 2], 0, gu_a)
                    pe.wait_ge(h_b, e + QT)
                    gate_up(xs, w_gu[b % 2], 1, gu_b)
                    pe.wait_ge(h_a, e + QT + 1)
                    turn_h(b % 2, 0, h_turned_a)
                    turn_slots(e + 1, b + 1,
                               lambda: pe.wait_ge(slots_in[(b + 1) % 2], i * 32 + 16 * ((b + 1) // 2 + 1)))
                    pe.wait_ge(hT_a, e + QT + 1)
                    pe.wait_ge(wd_lo_made, e * 2 + 3)
                    pe.wait_ge(y_out0, e + 1)
                    pe.wait_ge(y_out1, e + 2 * QT)
                    down(Y_BANK, b % 2, 0, hT_lo_a, e + QT + 1)
                    pe.wait_ge(h_b, e + QT + 1)
                    turn_h(b % 2, 1, h_turned_b)
                    slots(e + 2, b)
                    pe.wait_ge(hT_b, e + QT + 1)
                    pe.wait_ge(wd_lo_made, e * 2 + 4)
                    down(Y_BANK, b % 2, 1, hT_lo_b, e + QT + 1).then_inc(y_done, 1)

            n = pe.value_load(most_i[0:1, 0:1], min_val=0, max_val=SEQ)
            with pe.If(n > P):
                pe.sem_inc(ov["y"], 1)
                with pe.Fori(1, SEQ // P) as c:
                    with pe.Fori(0, N_EXP) as e:
                        j = (c - 1) * N_EXP + e
                        pe.wait_ge(ov["oh"], j + 1)
                        for t in range(QT):
                            mm = nc.tensor.matmul(PS[:, I_BANK, 0:2], onehot[:, 0, t, :],
                                                  info[:, t, bass.ds(e, 1), :].rearrange("p a b -> p (a b)"),
                                                  start=(t == 0), stop=(t == QT - 1))
                        mm.then_inc(ov["idx"], 1)
                        pe.wait_ge(ov["in"], j * 16 + 16)
                        xs = x_slots[:, 0, :].rearrange("p (q c) -> p c q", c=KT)
                        for k in range(KT):
                            mm = nc.tensor.transpose(PS[:, X_BANK + k // 4, (k % 4) * P:(k % 4 + 1) * P], xs[:, k, :],
                                                     ident[:, :])
                        mm.then_inc(ov["tr"], 1)
                        pe.wait_ge(ov["xT"], j + 1)
                        pe.wait_ge(ov["w"], j * 32 + 32)
                        for half in range(2):
                            gate_up(lambda k: x_slotsT[:, 0, k, :], w_gu[0], half, ov["gu"])
                        for half in range(2):
                            pe.wait_ge(ov["h"], j * 2 + half + 1)
                            if half == 1:
                                pe.wait_ge(ov["hT"], j * 2 + 1)
                            turn_h(0, half, ov["hturn"])
                        pe.wait_ge(ov["hT"], j * 2 + 2)
                        for half in range(2):
                            for m in range(2):
                                mm = nc.tensor.matmul(PS[:, Y_BANK + m, :], hT[:, half, :],
                                                      w_dn[0][:, half, m * 512:(m + 1) * 512], start=(half == 0),
                                                      stop=(half == 1))
                        mm.then_inc(ov["y"], 1)

        @block.scalar
        def _(act):
            chain = [0]

            def link(ins):
                chain[0] += 1
                ins.then_inc(act_chain, 1)
                act.wait_ge(act_chain, chain[0])

            def split(n):
                if n < N_CHUNKS:
                    act.wait_ge(ring_in[n % RING], 16 * (n // RING + 1))
                    nc.scalar.activation(w_hi[:, n % HALVES, :, :],
                                         ring[:, n % RING, 0:KT * P].rearrange("p (c n) -> p c n", c=KT), ACT.Copy)\
                        .then_inc(w_hi_made, 1)

            split(0)
            for c in range(KT):
                act.wait_ge(xT_in[c // (KT // X_PARTS)], 16)
                nc.scalar.activation(x_hi[:, c, :], mT[:, c, :], ACT.Copy).then_inc(x_hi_made, 1)
            split(1)
            def forget_and_lambda():
                act.wait_ge(forget_exp, 1)
                link(nc.scalar.activation(fg[:, 1, :], fg[:, 1, :], ACT.Exp))
                nc.scalar.activation(fg[:, 1, :], fg[:, 1, :], ACT.Ln, bias=1.0).then_inc(forget_exp, 1)
                act.wait_ge(lam_dots, 1)
                nc.scalar.activation(lam_s[:, 2:4], lam_s[:, 0:2], ACT.Exp).then_inc(lam_exp, 1)

            for kind, n in order:
                if kind == "proj":
                    u = n
                    what, br, j = PROJ[n]
                    bank = PS[:, C_BANK + u % 2, :]
                    act.wait_ge(proj_done, u + 1)
                    scale = -(32 if br == BR_C else HD) ** -0.5 if what == "q" else 1.0
                    if what == "v":
                        nc.scalar.activation(V[:, :, V_AT[br, j], :], bank.rearrange("p (t n) -> p t n", t=QT),
                                             ACT.Copy).then_inc(proj_out, 1)
                    elif br == BR_A:
                        dst = qA if what == "q" else kA
                        nc.scalar.activation(dst[0:HD, 2 * j, :], bank[0:HD, :], ACT.Copy, scale=scale)
                        nc.scalar.activation(dst[0:HD, 2 * j + 1, :], bank[HD:P, :], ACT.Copy, scale=scale)\
                            .then_inc(proj_out, 1)
                    else:
                        dst = {("q", BR_B): qB, ("k", BR_B): kB, ("q", BR_C): qC, ("k", BR_C): kC,
                               ("q", BR_D): qD, ("k", BR_D): kD}[what, br]
                        nc.scalar.activation(dst[:, j, :], bank, ACT.Copy, scale=scale).then_inc(proj_out, 1)
                    split(n + HALVES)
                    if n == 0:
                        forget_and_lambda()
                elif kind == "scores":
                    br, h, _, qt = STEPS[n]
                    nk = keys_of(br, qt)[1] * P + (br == BR_B)
                    act.wait_ge(biased, n + 1)
                    nc.scalar.activation(probs[:, n % 3, 0:nk], probs[:, n % 3, 0:nk], ACT.Exp,
                                         bias=nmax[:, n:n + 1], scale=-1.0, accum_out=den[:, n:n + 1])\
                        .then_inc(probs_made, 1)
                elif kind == "turn":
                    u = turn_at[kind, n]
                    nk = keys_of(STEPS[n][0], STEPS[n][3])[1] * P
                    act.wait_ge(turned, u + 1)
                    if n >= 3:
                        act.wait_ge(values_done, n - 2)
                    nc.scalar.activation(probsT[:, n % 3, 0:nk], PS[:, T_BANK + u % 2, 0:nk], ACT.Copy)\
                        .then_inc(turned_out, 1)
                elif kind == "turn_y":
                    u = turn_at[kind, n]
                    br, j = n // 2, n % 2
                    act.wait_ge(turned, u + 1)
                    if br >= 2:
                        act.wait_ge(branch_done, (br - 1) * KT)
                    nc.scalar.activation(yT[:, (br % 2) * 2 + j, :], PS[:, T_BANK + u % 2, :], ACT.Copy)\
                        .then_inc(turned_out, 1)
                elif kind == "gate":
                    act.wait_ge(gate_done, n + 1)
                    if n >= 2:
                        act.wait_ge(gated_made, n - 1)
                    nc.scalar.activation(gate[:, n % 2, :], PS[:, C_BANK, :], ACT.Exp, scale=-1.0)\
                        .then_inc(gate_exp, 1)
                    split(N_PROJ + n + HALVES)

            def x1T_copy(t):
                act.wait_ge(x1_turned, t + 1)
                for h in range(2):
                    ins = nc.scalar.activation(xT[:, 4 * h:4 * h + 4, t * P:(t + 1) * P],
                                               PS[:, X_BANK + h, :].rearrange("p (c n) -> p c n", c=4), ACT.Copy)
                ins.then_inc(x1T_made, 1)

            def router_exponential(t):
                act.wait_ge(router_done, t + 1)
                if t >= 1:
                    act.wait_ge(scores_used, t)
                nc.scalar.activation(score[:, :], PS[:, C_BANK, 0:N_EXP], ACT.Exp, scale=-1.0).then_inc(router_exp, 1)

            for t in range(QT):
                x1T_copy(t)
                router_exponential(t)

            def sigmoid(half, done):
                nc.scalar.activation(sig[:, half, 0:P], PS[:, G_BANK + half, 0:P], ACT.Sigmoid).then_inc(done, 1)

            def hT_copy(b, half, done):
                nc.scalar.activation(hT_hi[:, b, half, :], PS[:, H_BANK, 0:P], ACT.Copy).then_inc(done, 1)

            def split_down(b):
                for half in range(2):
                    nc.scalar.activation(wd_hi[:, half, :], w_dn[b][:, half, :], ACT.Copy).then_inc(wd_hi_made, 1)

            act.wait_ge(sh_in, 32)
            split_down(1)
            for t in range(QT):
                for half, ready, done, made in ((0, gu_a, sig_a, h_a), (1, gu_b, sig_b, h_b)):
                    act.wait_ge(ready, t + 1)
                    if t >= 1:
                        act.wait_ge(made, t)
                    sigmoid(half, done)
                act.wait_ge(h_turned_a, t + 1)
                if t >= 2:
                    act.wait_ge(y_done, t - 1)
                hT_copy(t % 2, 0, hT_a)
                act.wait_ge(h_turned_b, t + 1)
                hT_copy(t % 2, 1, hT_b)

            def slotsT_copy(j, b):
                act.wait_ge(slots_turned, j + 1)
                for h in range(2):
                    ins = nc.scalar.activation(x_slotsT[:, b % 2, 4 * h:4 * h + 4, :],
                                               PS[:, X_BANK + h, :].rearrange("p (c n) -> p c n", c=4), ACT.Copy)
                ins.then_inc(slotsT_made, 1)

            slotsT_copy(0, 0)
            act.wait_ge(y_done, QT)
            act.sem_inc(y_out0, 1)
            with act.Fori(0, N_EXP // 4) as i:
                for b in range(4):
                    e = i * 4 + b
                    act.wait_ge(dn_in[b % 2], i * 32 + 16 * (b // 2 + 1))
                    split_down(b % 2)
                    for half, ready, done, made in ((0, gu_a, sig_a, h_a), (1, gu_b, sig_b, h_b)):
                        act.wait_ge(ready, e + QT + 1)
                        act.wait_ge(made, e + QT)
                        sigmoid(half, done)
                    act.wait_ge(h_turned_a, e + QT + 1)
                    act.wait_ge(y_done, e + QT - 1)
                    hT_copy(b % 2, 0, hT_a)
                    slotsT_copy(e + 1, b + 1)
                    act.wait_ge(h_turned_b, e + QT + 1)
                    hT_copy(b % 2, 1, hT_b)
                    act.wait_ge(y_done, e + QT + 1)
                    act.wait_ge(rows_out[b % 2], i * 32 + 16 * (b // 2 + 1))
                    nc.scalar.activation(y_slots[:, b % 2, 0:512], PS[:, Y_BANK, :], ACT.Copy,
                                         scale=w_slot[:, b, :]).then_inc(y_out0, 1)

            n = act.value_load(most_i[0:1, 0:1], min_val=0, max_val=SEQ)
            with act.If(n > P):
                with act.Fori(1, SEQ // P) as c:
                    with act.Fori(0, N_EXP) as e:
                        j = (c - 1) * N_EXP + e
                        act.wait_ge(ov["tr"], j + 1)
                        for h in range(2):
                            ins = nc.scalar.activation(x_slotsT[:, 0, 4 * h:4 * h + 4, :],
                                                       PS[:, X_BANK + h, :].rearrange("p (c n) -> p c n", c=4),
                                                       ACT.Copy)
                        ins.then_inc(ov["xT"], 1)
                        for half in range(2):
                            act.wait_ge(ov["gu"], j * 2 + half + 1)
                            sigmoid(half, ov["sig"])
                        for half in range(2):
                            act.wait_ge(ov["hturn"], j * 2 + half + 1)
                            nc.scalar.activation(hT[:, half, :], PS[:, H_BANK, 0:P], ACT.Copy).then_inc(ov["hT"], 1)

        @block.vector
        def _(dve):
            chain = [0]

            def link(ins):
                chain[0] += 1
                ins.then_inc(dve_chain, 1)
                dve.wait_ge(dve_chain, chain[0])

            nc.vector.memset(table[:, :], 0.0).then_inc(consts_made, 1)
            link(nc.vector.memset(qA[64:66, :, :], 1.0))
            link(nc.vector.memset(kA[64:66, :, :], 1.0))
            for c in range(KT):
                dve.wait_ge(x_hi_made, c + 1)
                nc.vector.tensor_tensor(x_lo[:, c, :], mT[:, c, :], x_hi[:, c, :].bitcast(F32), ALU.subtract)\
                    .then_inc(x_lo_made, 1)
            dve.wait_ge(small_in, 16 * SMALL)
            dve.wait_ge(forget_mm, 1)
            link(nc.vector.tensor_scalar(fg[:, 0, :], PS[0:4, T_BANK, :], b_f[:, 0:1], None, ALU.add))
            link(nc.vector.tensor_scalar(fg[:, 2, :], fg[:, 0, :], -1.0, None, ALU.mult))
            link(nc.vector.tensor_tensor(fg[:, 1, :], fg[:, 0, :], fg[:, 2, :], ALU.min))
            link(nc.vector.tensor_scalar(fg[:, 0, :], fg[:, 0, :], 0.0, None, ALU.min))
            dve.sem_inc(forget_exp, 1)
            dve.wait_ge(small_in, 16 * SMALL)
            dve.wait_ge(bias_mm, 1)
            link(nc.vector.tensor_tensor(dist_bias[:, 0:512], PS[0:16, S_BANK, 0:512], dist_mask[:, 0:512], ALU.add))
            nc.vector.tensor_tensor(dist_bias[:, 512:640], PS[0:16, S_BANK + 1, 0:128], dist_mask[:, 512:640], ALU.add)\
                .then_inc(bias_made, 1)
            for m in range(2):
                link(nc.vector.tensor_tensor_reduce(lam_mul[:, m, :], lam_in[:, 2 * m, :], lam_in[:, 2 * m + 1, :],
                                                    1.0, 0.0, ALU.mult, ALU.add, lam_s[:, m:m + 1]))
            dve.sem_inc(lam_dots, 1)
            link(nc.vector.tensor_scalar(neg_sink[:, :], neg_sink[:, :], -1.0, None, ALU.mult))
            link(nc.vector.tensor_scalar(norm_g[:, :], norm_g[:, :], 1.0 - LAM_INIT, None, ALU.mult))
            dve.wait_ge(forget_exp, 2)
            link(nc.vector.tensor_tensor(fg[:, 0, :], fg[:, 0, :], fg[:, 1, :], ALU.subtract))
            link(nc.vector.tensor_tensor_scan(fg[:, 2, :], fg[:, 0, :], fg[:, 0, :], 0.0, ALU.add, ALU.bypass))
            link(nc.vector.tensor_scalar(fg[:, 3, :], fg[:, 2, :], -1.0, None, ALU.mult))
            dve.sem_inc(forget_made, 1)
            dve.wait_ge(lam_exp, 1)
            link(nc.vector.tensor_tensor(lam_s[:, 4:5], lam_s[:, 3:4], lam_s[:, 2:3], ALU.subtract))
            link(nc.vector.tensor_scalar(lam_s[:, 5:6], lam_s[:, 4:5], -LAM_INIT, None, ALU.add))

            def turn_wait(s):
                dve.wait_ge(turned, turn_at["turn", s] + 1)

            def bias_step(s):
                br, h, c, qt = STEPS[s]
                nk = keys_of(br, qt)[1] * P
                row = {BR_A: 0, BR_B: 1 + h, BR_C: 5 + h, BR_D: 9 + h}[br]
                if (h, c, qt) == (0, 0, 0):
                    if br == BR_A:
                        dve.wait_ge(causal_in, 16)
                    else:
                        dve.wait_ge(strips_in[br - 1], 16)
                dve.wait_ge(scores_done, s + 1)
                if s >= 3:
                    turn_wait(s - 3)
                if br == BR_B:
                    nc.vector.tensor_copy(probs[:, s % 3, nk:nk + 1], neg_sink[:, h:h + 1])
                start = neg_sink[:, h:h + 1] if br == BR_B else 3e38
                lo = SEQ - nk
                nc.vector.tensor_tensor_reduce(probs[:, s % 3, 0:nk], PS[:, S_BANK + s % 2, 0:nk], strips[:, row, lo:SEQ],
                                               1.0, start, ALU.add, ALU.min, nmax[:, s:s + 1]).then_inc(biased, 1)

            def out_step(s):
                br, h, c, qt = STEPS[s]
                dve.wait_ge(values_done, s + 1)
                link(nc.vector.reciprocal(rden[:, s:s + 1], den[:, s:s + 1]))
                dst = Y[:, (br % 2) * QT + qt, h * HD:(h + 1) * HD]
                src = PS[:, O_BANK + s % 2, 0:HD]
                if br >= 2 and s == last_step[br - 1] + 1:
                    dve.wait_ge(turned, turn_at["turn_y", 2 * (br - 2) + 1] + 1)
                if br == BR_C and c == 1:
                    link(nc.vector.tensor_scalar(rden[:, s:s + 1], rden[:, s:s + 1], lam_s[:, 5:6], None, ALU.mult))
                    dve.wait_ge(y_made, s - QT + 1)
                    nc.vector.scalar_tensor_tensor(dst, src, rden[:, s:s + 1], dst, ALU.mult, ALU.add)\
                        .then_inc(y_made, 1)
                else:
                    nc.vector.tensor_scalar(dst, src, rden[:, s:s + 1], None, ALU.mult).then_inc(y_made, 1)
                if s == last_step[br]:
                    dve.wait_ge(y_made, s + 1)
                    if br == BR_C:
                        for t in range(QT):
                            yt = Y[:, (br % 2) * QT + t, :]
                            link(nc.vector.tensor_tensor(yc_sq[:, :], yt, yt, ALU.mult))
                            link(nc.vector.tensor_reduce(yc_ss[:, 4 * t:4 * t + 4],
                                                         yc_sq[:, :].rearrange("p (h d) -> p h d", h=4), AX.X, ALU.add))
                        link(nc.vector.tensor_scalar(yc_ss[:, :], yc_ss[:, :], 1.0 / HD, EPS, ALU.mult, ALU.add))
                        dve.sem_inc(yc_stat, 1)
                    else:
                        dve.sem_inc(y_ready, 1)

            def norm_c():
                dve.wait_ge(yc_rms, 1)
                for t in range(QT):
                    for h in range(4):
                        yt = Y[:, (BR_C % 2) * QT + t, h * HD:(h + 1) * HD]
                        ins = nc.vector.scalar_tensor_tensor(yt, yt, yc_ss[:, 4 * t + h:4 * t + h + 1], norm_g[:, :],
                                                             ALU.mult, ALU.mult)
                        if t == QT - 1 and h == 3:
                            link(ins)
                dve.sem_inc(y_ready, 1)

            for kind, n in order:
                if kind == "scores":
                    bias_step(n)
                    if n == norm_step:
                        norm_c()
                elif kind == "values":
                    out_step(n)
                elif kind == "gate":
                    dve.wait_ge(gate_exp, n + 1)
                    g = gate[:, n % 2, :]
                    link(nc.vector.tensor_scalar(g, g, 1.0, None, ALU.add))
                    nc.vector.reciprocal(g[:, 0:SEQ // 2], g[:, 0:SEQ // 2])
                elif kind == "invert":
                    g = gate[:, n % 2, SEQ // 2:SEQ]
                    link(nc.vector.reciprocal(g, g))
                elif kind == "gated":
                    dve.wait_ge(branch_done, n + 1)
                    if n < KT:
                        dst = mT[:, n, :]
                    else:
                        dst = gated[:, n % 2, :]
                        if n >= KT + 2:
                            dve.wait_ge(merged, n - 1)
                    nc.vector.tensor_tensor(dst, PS[:, C_BANK + 1, :], gate[:, n % 2, :], ALU.mult)\
                        .then_inc(gated_made, 1)

            def norm(v, k):
                for h in range(2):
                    ins = nc.vector.bn_stats(stats[:, h, :], v[:, h * 512:(h + 1) * 512])
                link(ins)
                link(nc.vector.bn_aggr(mv[:, 0:2], stats[:, :, :].rearrange("p a b -> p (a b)")))
                link(nc.vector.tensor_scalar(mv[:, 1:2], mv[:, 1:2], EPS, None, ALU.add))
                dve.sem_inc(var_made, 1)
                dve.wait_ge(rstd_made, k + 1)
                link(nc.vector.tensor_scalar(v, v, mv[:, 0:1], mv[:, 1:2], ALU.subtract, ALU.mult))

            def first_norm(t):
                bank = S_BANK if t % 2 == 0 else O_BANK
                dve.wait_ge(mix_done, t + 1)
                dve.wait_ge(x_in, 16 * QT)
                v = x1[:, t, :]
                link(nc.vector.scalar_tensor_tensor(v, x_nat[:, t, :], ALPHA,
                                                    PS[:, bank:bank + 2, :].rearrange("p a b -> p (a b)"),
                                                    ALU.mult, ALU.add))
                norm(v, t)
                if t == 0:
                    dve.wait_ge(late_in, 16 * N_LATE)
                link(nc.vector.tensor_tensor(v, v, ln1[:, 0, :], ALU.mult))
                nc.vector.tensor_tensor(v, v, ln1[:, 1, :], ALU.add).then_inc(x1_made, 1)

            def pick(values, eighth, n, k, dst):
                more, same, upto = (rt8[:, 0, :], rt8[:, 1, :], rt8[:, 2, :]) if n == 8 else \
                    (rt64[:, 0, :], rt64[:, 1, :], rt64[:, 2, :])
                left = wsum[:, 4:5]
                link(nc.vector.tensor_scalar(more, values, eighth, None, ALU.is_gt))
                link(nc.vector.tensor_reduce(left, more, AX.X, ALU.add))
                link(nc.vector.tensor_scalar(left, left, -1.0, float(k), ALU.mult, ALU.add))
                link(nc.vector.tensor_scalar(same, values, eighth, None, ALU.is_equal))
                link(nc.vector.tensor_tensor_scan(upto, same, same, 0.0, ALU.add, ALU.bypass))
                link(nc.vector.scalar_tensor_tensor(same, upto, left, same, ALU.is_le, ALU.mult))
                link(nc.vector.tensor_tensor(dst, more, same, ALU.add))

            def route(t):
                dve.wait_ge(router_exp, t + 1)
                link(nc.vector.tensor_scalar(score[:, :], score[:, :], 1.0, None, ALU.add))
                link(nc.vector.reciprocal(score[:, :], score[:, :]))
                link(nc.vector.tensor_tensor(choice[:, :], score[:, :], r_bias[:, :], ALU.add))
                for g in range(N_GROUPS):
                    ins = nc.vector.max(top2[:, g, :], choice[:, g * GROUP:(g + 1) * GROUP])
                link(ins)
                link(nc.vector.tensor_tensor(gscore[:, :], top2[:, :, 0], top2[:, :, 1], ALU.add))
                link(nc.vector.max(rt8[:, 4, :], gscore[:, :]))
                pick(gscore[:, :], rt8[:, 4, TOPK_GROUPS - 1:TOPK_GROUPS], 8, TOPK_GROUPS, rt8[:, 3, :])
                link(nc.vector.tensor_scalar(rt8[:, 5, :], rt8[:, 3, :], MASKED, -MASKED, ALU.mult, ALU.add))
                c8 = choice[:, :].rearrange("p (g e) -> p g e", g=N_GROUPS)
                link(nc.vector.tensor_tensor(c8, c8, rt8[:, 5, :].unsqueeze(2).broadcast_to([P, N_GROUPS, GROUP]),
                                             ALU.add))
                link(nc.vector.max(rt8[:, 6, :], choice[:, :]))
                pick(choice[:, :], rt8[:, 6, TOP_K - 1:TOP_K], N_EXP, TOP_K, sel[:, t, :])
                dve.sem_inc(sel_made, 1)
                s = sel[:, t, :]
                link(nc.vector.tensor_tensor_reduce(rt64[:, 3, :], s, score[:, :], 1.0, 0.0, ALU.mult, ALU.add,
                                                    wsum[:, 0:1]))
                dve.sem_inc(scores_used, 1)
                link(nc.vector.reciprocal(wsum[:, 1:2], wsum[:, 0:1]))
                link(nc.vector.tensor_scalar(info[:, t, 0:N_EXP, 1], rt64[:, 3, :], wsum[:, 1:2], ROUTED_SCALE,
                                             ALU.mult, ALU.mult))

            def slots_of(t):
                dve.wait_ge(pos_done, t + 1)
                p = PS[:, C_BANK + 1, 0:N_EXP]
                link(nc.vector.tensor_scalar(rt64[:, 0, :], sel[:, t, :], -NO_SLOT, NO_SLOT, ALU.mult, ALU.add))
                nc.vector.tensor_tensor(pos[:, t, 0:N_EXP], p, rt64[:, 0, :], ALU.add).then_inc(info_made, 1)

            dve.wait_ge(branch_done, N_MERGE)
            dve.wait_ge(merged, N_MERGE)
            nc.vector.memset(pos[:, :, :], NO_SLOT)
            link(nc.vector.memset(info[:, :, :, :], 0.0))
            dve.wait_ge(consts_made, 6)
            link(nc.vector.tensor_scalar(info[:, :, 0:N_EXP, 0],
                                         tok_row[:, 0:QT].unsqueeze(2).broadcast_to([P, QT, N_EXP]), -UNUSED, None,
                                         ALU.add))
            first_norm(0)
            first_norm(1)
            def h_half(half, b, count, done):
                nc.vector.tensor_tensor(silu[:, half, 0:P], PS[:, G_BANK + half, 0:P], sig[:, half, 0:P], ALU.mult)\
                    .then_inc(silu_made, 1)
                dve.wait_ge(silu_made, count)
                nc.vector.tensor_tensor(h_slots[:, b, half * P:(half + 1) * P], PS[:, G_BANK + half, P:F],
                                        silu[:, half, 0:P], ALU.mult).then_inc(done, 1)

            def hT_low(b, half, ready, count, done):
                dve.wait_ge(ready, count)
                nc.vector.tensor_tensor(hT_lo[:, b, half, :], PS[:, H_BANK, 0:P], hT_hi[:, b, half, :].bitcast(F32),
                                        ALU.subtract).then_inc(done, 1)

            def split_down(b, first):
                for half in range(2):
                    dve.wait_ge(wd_hi_made, first + half)
                    nc.vector.tensor_tensor(wd_lo[:, half, :], w_dn[b][:, half, :], wd_hi[:, half, :].bitcast(F32),
                                            ALU.subtract).then_inc(wd_lo_made, 1)

            def shared_h(t):
                dve.wait_ge(sig_a, t + 1)
                if t >= 2:
                    dve.wait_ge(y_done, t - 1)
                h_half(0, t % 2, 2 * t + 1, h_a)
                dve.wait_ge(sig_b, t + 1)
                h_half(1, t % 2, 2 * t + 2, h_b)
                hT_low(t % 2, 0, hT_a, t + 1, hT_lo_a)
                hT_low(t % 2, 1, hT_b, t + 1, hT_lo_b)

            def base(t):
                dve.wait_ge(y_done, t + 1)
                for n in range(2):
                    nc.vector.scalar_tensor_tensor(mT_nat(t)[:, n * 512:(n + 1) * 512], x1[:, t, n * 512:(n + 1) * 512],
                                                   ALPHA, PS[:, X_BANK + n, :], ALU.mult, ALU.add).then_inc(y_out1, 1)

            def mark_slots(j, b):
                nc.vector.tensor_tensor(onehot[:, b % 2, :, :],
                                        slot_no[:, :].unsqueeze(1).broadcast_to([P, QT, P]),
                                        pos[:, :, bass.ds(j, 1)].broadcast_to([P, QT, P]),
                                        ALU.is_equal).then_inc(onehot_made, 1)

            def rows_of(b, done):
                nc.vector.tensor_copy(w_slot[:, b, :], PS[:, I_BANK, 1:2])
                row = PS[:, I_BANK, 0:1]
                nc.vector.tensor_scalar(rows_u[:, b, 0:1], row, UNUSED, None, ALU.add)
                nc.vector.tensor_scalar(rows_u[:, b, 1:2], row, UNUSED, tok_row[:, QT:QT + 1], ALU.add, ALU.min)\
                    .then_inc(done, 1)

            for t in range(QT - 1):
                route(t)
                if t + 2 < QT:
                    first_norm(t + 2)
                if t >= 1:
                    slots_of(t - 1)
            split_down(1, 1)
            shared_h(0)
            route(QT - 1)
            slots_of(QT - 2)
            base(0)
            shared_h(1)
            slots_of(QT - 1)
            dve.wait_ge(pos_done, QT + 1)
            link(nc.vector.tensor_reduce(most[:, 0:1], PS[:, C_BANK + 1, 0:N_EXP], AX.X, ALU.max))
            nc.vector.tensor_copy(most_i[:, 0:1], most[0:1, 0:1]).then_inc(most_made, 1)
            dve.wait_ge(info_made, QT)
            for j in range(2):
                mark_slots(j, j)
            for j in range(2):
                dve.wait_ge(slots_done, j + 1)
                rows_of(j, rows_made)
            base(1)
            for t in range(2, QT):
                shared_h(t)
                base(t)

            with dve.Fori(0, N_EXP // 4) as i:
                for b in range(4):
                    e = i * 4 + b
                    dve.wait_ge(slots_done, e + 1)
                    mark_slots(e + 2, b)
                    split_down(b % 2, e * 2 + 3)
                    dve.wait_ge(sig_a, e + QT + 1)
                    h_half(0, b % 2, e * 2 + 2 * QT + 1, h_a)
                    dve.wait_ge(sig_b, e + QT + 1)
                    h_half(1, b % 2, e * 2 + 2 * QT + 2, h_b)
                    hT_low(b % 2, 0, hT_a, e + QT + 1, hT_lo_a)
                    hT_low(b % 2, 1, hT_b, e + QT + 1, hT_lo_b)
                    dve.wait_ge(slots_done, e + 3)
                    dve.wait_ge(y_out0, e + 1)
                    dve.wait_ge(rows_out[b % 2], i * 32 + 16 * (b // 2 + 1))
                    rows_of((b + 2) % 4, rows_made)
                    dve.wait_ge(y_done, e + QT + 1)
                    nc.vector.tensor_scalar(y_slots[:, b % 2, 512:D], PS[:, Y_BANK + 1, :], w_slot[:, b, :], None,
                                            ALU.mult).then_inc(y_out1, 1)

            n = dve.value_load(most_i[0:1, 0:1], min_val=0, max_val=SEQ)
            with dve.If(n > P):
                nc.vector.tensor_copy(ov_slot[:, :], slot_no[:, :]).then_inc(ov["silu"], 1)
                with dve.Fori(1, SEQ // P) as c:
                    dve.wait_ge(ov["silu"], (c - 1) * (2 * N_EXP + 1) + 1)
                    nc.vector.tensor_scalar(ov_slot[:, :], ov_slot[:, :], float(P), None, ALU.add)\
                        .then_inc(ov["silu"], 1)
                    dve.wait_ge(ov["silu"], (c - 1) * (2 * N_EXP + 1) + 2)
                    dve.sem_inc(ov["turns"], 1)
                    with dve.Fori(0, N_EXP) as e:
                        j = (c - 1) * N_EXP + e
                        nc.vector.tensor_tensor(onehot[:, 0, :, :],
                                                ov_slot[:, :].unsqueeze(1).broadcast_to([P, QT, P]),
                                                pos[:, :, bass.ds(e, 1)].broadcast_to([P, QT, P]),
                                                ALU.is_equal).then_inc(ov["oh"], 1)
                        dve.wait_ge(ov["idx"], j + 1)
                        rows_of(0, ov["rows"])
                        for half in range(2):
                            dve.wait_ge(ov["sig"], j * 2 + half + 1)
                            nc.vector.tensor_tensor(silu[:, half, 0:P], PS[:, G_BANK + half, 0:P], sig[:, half, 0:P],
                                                    ALU.mult).then_inc(ov["silu"], 1)
                            dve.wait_ge(ov["silu"], j * 2 + half + c + 2)
                            nc.vector.tensor_tensor(h_slots[:, 0, half * P:(half + 1) * P], PS[:, G_BANK + half, P:F],
                                                    silu[:, half, 0:P], ALU.mult).then_inc(ov["h"], 1)
                        dve.wait_ge(ov["y"], j + 2)
                        for m in range(2):
                            ins = nc.vector.tensor_scalar(y_slots[:, 0, m * 512:(m + 1) * 512], PS[:, Y_BANK + m, :],
                                                          w_slot[:, 0, :], None, ALU.mult)
                        ins.then_inc(ov["yout"], 1)
                        dve.wait_ge(ov["out"], j * 16 + 16)

            def total(t):
                v, m = mT_nat(t), mv[:, 4 * (t % 2):4 * (t % 2) + 2]
                dve.wait_ge(acc_in[1][t], 16)
                link(nc.vector.tensor_tensor(v, v, acc[1][:, t, :], ALU.add))
                for h in range(2):
                    ins = nc.vector.bn_stats(stats[:, h, :], v[:, h * 512:(h + 1) * 512])
                link(ins)
                link(nc.vector.bn_aggr(m, stats[:, :, :].rearrange("p a b -> p (a b)")))
                nc.vector.tensor_scalar(m[:, 1:2], m[:, 1:2], EPS, None, ALU.add).then_inc(var_made, 1)

            def scale(t):
                v, m = mT_nat(t), mv[:, 4 * (t % 2):4 * (t % 2) + 2]
                dve.wait_ge(rstd_made, QT + t + 1)
                link(nc.vector.tensor_scalar(v, v, m[:, 0:1], m[:, 1:2], ALU.subtract, ALU.mult))
                nc.vector.tensor_tensor(v, v, ln2[:, 0, :], ALU.mult).then_inc(scaled, 1)

            for t in range(QT):
                dve.wait_ge(acc_in[0][t], 16)
                link(nc.vector.tensor_tensor(mT_nat(t), mT_nat(t), acc[0][:, t, :], ALU.add))
            dve.wait_ge(ln2_in, 32)
            total(0)
            for t in range(1, QT):
                total(t)
                scale(t - 1)
            scale(QT - 1)

        @block.gpsimd
        def _(pool):
            pool.wait_ge(consts_made, 1)
            nc.gpsimd.memset(ones[:, :], 1.0).then_inc(pool_chain, 1)
            nc.gpsimd.memset(half_neg[:, :], -0.5).then_inc(pool_chain, 1)
            nc.gpsimd.memset(ident[:, :], 0.0).then_inc(pool_chain, 1)
            pool.wait_ge(pool_chain, 3)
            nc.gpsimd.affine_select(out=ident[:, :], in_=ident[:, :], compare_op=ALU.not_equal, fill=1.0, base=0,
                                    pattern=[[-1, P]], channel_multiplier=1).then_inc(consts_made, 1)
            nc.gpsimd.affine_select(out=before[:, :], in_=ones[:, :], compare_op=ALU.is_gt, fill=0.0, base=0,
                                    pattern=[[1, P]], channel_multiplier=-1).then_inc(consts_made, 1)
            nc.gpsimd.iota(slot_no[:, :], pattern=[[1, P]], base=0, channel_multiplier=0,
                           allow_small_or_imprecise_dtypes=True).then_inc(consts_made, 1)
            nc.gpsimd.iota(tok_row[:, :], pattern=[[P, QT + 1]], base=0, channel_multiplier=1,
                           allow_small_or_imprecise_dtypes=True).then_inc(consts_made, 1)
            pool.wait_ge(consts_made, 5)
            pool.sem_inc(consts_made, 1)

            def root(v, ready, count, done):
                pool.wait_ge(ready, count)
                nc.gpsimd.tensor_tensor(v, v, half_neg[:, 0:v.shape[1]], ALU.pow).then_inc(done, 1)

            def split(n):
                w = ring[:, n % RING, 0:KT * P].rearrange("p (c n) -> p c n", c=KT)
                wh, wl = w_hi[:, n % HALVES, :, :], w_lo[:, n % HALVES, :, :]
                pool.wait_ge(w_hi_made, n + 1)
                nc.gpsimd.tensor_tensor(wl, w, wh.bitcast(F32), ALU.subtract).then_inc(w_lo_made, 1)

            for n in range(N_PROJ + HALVES):
                split(n)
            for m in range(N_MERGE):
                if N_PROJ + m + HALVES < N_CHUNKS:
                    split(N_PROJ + m + HALVES)
                if m == merges_before_norm:
                    root(yc_ss[:, :], yc_stat, 1, yc_rms)
                pool.wait_ge(gated_made, m + 1)
                if m < KT:
                    pool.sem_inc(merged, 1)
                    continue
                if m >= KT + 1:
                    pool.wait_ge(merged, m)
                k = m % KT
                nc.gpsimd.tensor_tensor(mT[:, k, :], mT[:, k, :], gated[:, m % 2, :], ALU.add).then_inc(merged, 1)

            for k in range(QT):
                root(mv[:, 1:2], var_made, k + 1, rstd_made)
            pool.wait_ge(mix_done, QT)
            nc.gpsimd.memset(x_slots[:, :, :], 0.0).then_inc(slots_clear, 1)
            nc.gpsimd.memset(y_slots[:, :, :], 0.0).then_inc(slots_clear, 1)
            pool.wait_ge(slots_clear, 2)
            for b in range(2):
                pool.dma_start(acc_d[b].rearrange("(t p) d -> p t d", p=P),
                               y_slots[:, b, :].unsqueeze(1).broadcast_to([P, QT + 1, D])).then_inc(rows_out[b], 16)
            last_tok = pool.to_reg(SEQ - 1)
            last_row = pool.to_reg(SEQ + P - 1)

            def gather(b, xb, done):
                pool.sem_inc(gathers_begun, 1)
                pool.indirect_dma_start(x_slots[:, xb, :], None, x1_d,
                                        bass.IndirectOffsetOnAxis(ap=rows_u[:, b, 0:1], axis=0),
                                        bounds_check=last_tok, oob_is_err=False).then_inc(done, 16)

            def scatter(b, yb, done):
                pool.sem_inc(scatters_begun, 1)
                pool.indirect_dma_start(acc_d[yb], bass.IndirectOffsetOnAxis(ap=rows_u[:, b, 1:2], axis=0),
                                        y_slots[:, yb, :], None,
                                        bounds_check=last_row, oob_is_err=True, compute_op=ALU.add).then_inc(done, 16)

            pool.wait_ge(x1_stored, 16 * QT)
            for j in range(2):
                pool.wait_ge(rows_made, j + 1)
                gather(j, j, slots_in[j])
            with pool.Fori(0, N_EXP // 4) as i:
                for b in range(4):
                    e = i * 4 + b
                    pool.wait_ge(rows_made, e + 3)
                    pool.wait_ge(slots_turned, e + 1)
                    gather((b + 2) % 4, b % 2, slots_in[b % 2])
                    pool.wait_ge(y_out0, e + 2)
                    pool.wait_ge(y_out1, e + 2 * QT + 1)
                    scatter(b, b % 2, rows_out[b % 2])
            for b in range(2):
                pool.wait_ge(slots_in[b], 16 * (N_EXP // 2 + 1))
                pool.wait_ge(rows_out[b], 16 * (N_EXP // 2 + 1))

            n = pool.value_load(most_i[0:1, 0:1], min_val=0, max_val=SEQ)
            with pool.If(n > P):
                with pool.Fori(1, SEQ // P) as c:
                    with pool.Fori(0, N_EXP) as e:
                        j = (c - 1) * N_EXP + e
                        pool.wait_ge(ov["rows"], j + 1)
                        gather(0, 0, ov["in"])
                        pool.wait_ge(ov["yout"], j + 1)
                        scatter(0, 0, ov["out"])
                pool.wait_ge(ov["out"], 16 * (SEQ // P - 1) * N_EXP)

            for t in range(QT + 1):
                if t < QT:
                    root(mv[:, 4 * (t % 2) + 1:4 * (t % 2) + 2], var_made, QT + t + 1, rstd_made)
                if t >= 1:
                    pool.wait_ge(scaled, t)
                    nc.gpsimd.tensor_tensor(mT_nat(t - 1), mT_nat(t - 1), ln2[:, 1, :], ALU.add).then_inc(out_made, 1)


def kernel(**inputs):
    import concourse.bacc as _bacc
    from concourse.bass_utils import run_bass_kernel_spmd as _run

    g = {k: np.asarray(v) for k, v in inputs.items()}
    w_in = g["w_in"][0]

    def columns(kind, br, j):
        first = COLS[kind, br]
        if (kind, br) == ("q", BR_B):
            return np.concatenate([first + h * HD + np.arange(HD) for h in (j, j + 2)])
        return first + j * P + np.arange(P)

    def tiles(w, n):
        return w.reshape(KT, P, n, P).transpose(2, 1, 0, 3)

    arrays = {
        "x": g["x"], "xT": g["x"][0].T, "t5_table": g["t5_table"],
        "w_proj": tiles(w_in[:, np.concatenate([columns(*c) for c in PROJ])], N_PROJ).reshape(N_PROJ, P, KT * P),
        "w_f": w_in[:, COLS["f"]:COLS["f"] + 4].reshape(KT, P, 4).transpose(1, 0, 2),
        "w_merge": np.concatenate([
            tiles(w_in[:, COLS["gates"]:], N_MERGE),
            g["w_branch"][0].reshape(4, 2, P, KT, P).transpose(0, 3, 2, 1, 4).reshape(N_MERGE, P, 2, P)],
            axis=2).reshape(N_MERGE, P, SLOT),
        "w_out": g["w_out"], "b_forget": g["b_forget"], "attn_sinks": g["attn_sinks"],
        "lam": np.stack([g["lam_q1"], g["lam_k1"], g["lam_q2"], g["lam_k2"]], axis=1),
        "diff_norm_g": g["diff_norm_g"], "ln1_g": g["ln1_g"], "ln1_b": g["ln1_b"], "ln2_g": g["ln2_g"],
        "ln2_b": g["ln2_b"], "w_router": g["w_router"], "router_bias": g["router_bias"],
        "w_gu": np.stack([g["w_gate_e"][0].reshape(N_EXP, D, FT, P), g["w_up_e"][0].reshape(N_EXP, D, FT, P)],
                         axis=3).reshape(N_EXP, P, KT * 2 * F),
        "w_down_e": g["w_down_e"],
        "w_gu_s": np.stack([g["w_gate_s"][0].reshape(D, FT, P), g["w_up_s"][0].reshape(D, FT, P)],
                           axis=2).reshape(P, KT * 2 * F),
        "w_down_s": g["w_down_s"],
    }
    arrays["neg_onehot"], arrays["dist_mask"], arrays["causal_strip"] = distance_constants()
    arrays = {k: np.ascontiguousarray(v) for k, v in arrays.items()}
    nc = _bacc.Bacc("TRN2", target_bir_lowering=False, num_devices=1)
    aps = {k: nc.dram_tensor(f"in_{k}", v.shape, mybir.dt.from_np(v.dtype), kind="ExternalInput").ap()
           for k, v in arrays.items()}
    out = nc.dram_tensor("out_0", (1, SEQ, D), F32, kind="ExternalOutput").ap()
    build(nc, aps, out)
    r = _run(nc, [{f"in_{k}": v for k, v in arrays.items()}], core_ids=[0])
    return r.results[0]["out_0"]
```
